# Optimizing a Trainium2 kernel written in Bass

```python
import jax, jax.numpy as jnp
from jax import lax
import numpy as np
import math

D_MODEL = 1024
BATCH = 1
SEQ = 256
DEPTH = 2

GRID_W = 64
CTX_LEN = 256
A_HEADS = 8
A_KV_HEADS = 2
A_HEAD_DIM = 64
ROPE_THETA = 10000.0
Q_BLOCK = 128
B_HEADS = 4
B_HEAD_DIM = 128
B_CHUNK = 128
B_CONV = 3
POOL_WINDOWS = (2, 4, 8, 16)
POOL_GROUP = D_MODEL // 4
N_EXPERTS = 16
EC_FACTOR = 2
D_EXPERT = 1024
NORM_EPS = 1e-6

A_Q = A_HEADS * A_HEAD_DIM
A_KV = A_KV_HEADS * A_HEAD_DIM
B_W = B_HEADS * B_HEAD_DIM
N_GATES = 2 * 2 * B_HEADS
EVEN_IN = A_Q + 2 * A_KV + 4 * B_W + N_GATES
MIX_W = A_Q + B_W
EVEN_SPLITS = (A_Q, A_Q + A_KV, A_Q + 2 * A_KV, A_Q + 2 * A_KV + B_W, A_Q + 2 * A_KV + 2 * B_W,
               A_Q + 2 * A_KV + 3 * B_W, A_Q + 2 * A_KV + 4 * B_W)
N_EVEN = (DEPTH + 1) // 2
N_ODD = DEPTH // 2


def rmsnorm(x, g):
    xf = x.astype(jnp.float32)
    y = xf * lax.rsqrt(jnp.mean(xf * xf, axis=-1, keepdims=True) + NORM_EPS)
    return (y * g.astype(jnp.float32)).astype(x.dtype)

def adaln(cond, w, b):
    m = jax.nn.silu(cond) @ w + b
    return m.reshape(cond.shape[:-1] + (1, 6, D_MODEL))

def modulate(x, g, shift, scale):
    return rmsnorm(x, g) * (1 + scale) + shift

def axial_rope(n_tokens):
    rows = n_tokens // GRID_W
    row_ids = jnp.repeat(jnp.arange(rows, dtype=jnp.float32), GRID_W)
    col_ids = jnp.tile(jnp.arange(GRID_W, dtype=jnp.float32), rows)
    half = A_HEAD_DIM // 2
    inv = ROPE_THETA ** (-jnp.arange(0, half, 2, dtype=jnp.float32) / half)
    ang = jnp.stack([row_ids[:, None] * inv, col_ids[:, None] * inv], axis=1)
    return jnp.cos(ang), jnp.sin(ang)

def apply_rope(x, cos, sin):
    Bn, n, H, d = x.shape
    xr = x.reshape(Bn, n, H, 2, 2, d // 4)
    x1, x2 = xr[..., 0, :], xr[..., 1, :]
    c = cos[None, :, None].astype(x.dtype)
    s = sin[None, :, None].astype(x.dtype)
    return jnp.stack([x1 * c - x2 * s, x2 * c + x1 * s], axis=-2).reshape(x.shape)

def attend_blocks(q, k, v):
    Bn, Lq, _, d = q.shape
    G = A_HEADS // A_KV_HEADS
    nb = Lq // Q_BLOCK
    qb = q.reshape(Bn, nb, Q_BLOCK, A_KV_HEADS, G, d).transpose(1, 0, 3, 4, 2, 5)
    kt = jnp.swapaxes(k, 1, 2)
    vt = jnp.swapaxes(v, 1, 2)
    scale = d ** -0.5

    def one_block(qblk):
        s = jnp.einsum('bhgtd,bhsd->bhgts', qblk, kt).astype(jnp.float32) * scale
        p = jax.nn.softmax(s, axis=-1).astype(vt.dtype)
        return jnp.einsum('bhgts,bhsd->bhgtd', p, vt)

    o = lax.map(one_block, qb)
    return o.transpose(1, 0, 4, 2, 3, 5).reshape(Bn, Lq, A_HEADS * d)

def short_conv(x, w):
    n = x.shape[1]
    pad = B_CONV // 2
    xp = jnp.pad(x, ((0, 0), (pad, B_CONV - 1 - pad), (0, 0)))
    return sum(xp[:, j:j + n] * w[j] for j in range(B_CONV))

def mlstm_zero_state(Bn):
    return (jnp.zeros((Bn, B_HEADS, B_HEAD_DIM, B_HEAD_DIM), jnp.float32),
            jnp.zeros((Bn, B_HEADS, B_HEAD_DIM), jnp.float32),
            jnp.full((Bn, B_HEADS), -1e30, jnp.float32))

def mlstm_scan(q, k, v, ig, lf, state):
    Bn, H, L, d = q.shape
    nc = L // B_CHUNK
    k = k * (d ** -0.5)

    def to_chunks(a):
        a = a.reshape(a.shape[:2] + (nc, B_CHUNK) + a.shape[3:])
        return jnp.moveaxis(a, 2, 0)

    tril = jnp.tril(jnp.ones((B_CHUNK, B_CHUNK), dtype=bool))

    def step(carry, inp):
        C, n, m = carry
        qc, kc, vc, ic, fc = inp
        b = jnp.cumsum(fc, axis=-1)
        log_d = jnp.where(tril, b[..., :, None] - b[..., None, :] + ic[..., None, :], -jnp.inf)
        log_inter = m[..., None] + b
        m_t = jnp.maximum(log_inter, jnp.max(log_d, axis=-1))
        w_intra = jnp.exp(log_d - m_t[..., None]) * jnp.einsum('bhtd,bhsd->bhts', qc, kc)
        w_inter = jnp.exp(log_inter - m_t)
        num = (w_inter[..., None] * jnp.einsum('bhed,bhtd->bhte', C, qc)
               + jnp.einsum('bhts,bhse->bhte', w_intra, vc))
        den = w_inter * jnp.einsum('bhd,bhtd->bht', n, qc) + jnp.sum(w_intra, axis=-1)
        h = num / jnp.maximum(jnp.abs(den), jnp.exp(-m_t))[..., None]
        b_end = b[..., -1]
        log_w = b_end[..., None] - b + ic
        m_new = jnp.maximum(m + b_end, jnp.max(log_w, axis=-1))
        w_s = jnp.exp(log_w - m_new[..., None])
        decay = jnp.exp(m + b_end - m_new)
        C = decay[..., None, None] * C + jnp.einsum('bhs,bhse,bhsd->bhed', w_s, vc, kc)
        n = decay[..., None] * n + jnp.einsum('bhs,bhsd->bhd', w_s, kc)
        return (C, n, m_new), h

    state, h = lax.scan(step, state, tuple(to_chunks(a) for a in (q, k, v, ig, lf)))
    h = jnp.moveaxis(h, 0, 2).reshape(Bn, H, L, d)
    return h, state

def mlstm_bidir(q, k, v, ig, lf, states):
    h_f, s_f = mlstm_scan(q, k, v, ig[0], lf[0], states[0])
    flip = lambda a: jnp.flip(a, axis=2)
    h_b, s_b = mlstm_scan(flip(q), flip(k), flip(v), flip(ig[1]), flip(lf[1]), states[1])
    return h_f + flip(h_b), (s_f, s_b)

def even_mixer(h_lat, h_ctx, ctx_out, w_in, w_out, g_qn, g_kn, w_conv, b_gate, g_hn):
    Bn, L, _ = h_lat.shape

    def project(h):
        n = h.shape[1]
        qa, ka, va, qb, kb, vb, ob, gt = jnp.split(h @ w_in, EVEN_SPLITS, axis=-1)
        qa = rmsnorm(qa.reshape(Bn, n, A_HEADS, A_HEAD_DIM), g_qn)
        ka = rmsnorm(ka.reshape(Bn, n, A_KV_HEADS, A_HEAD_DIM), g_kn)
        va = va.reshape(Bn, n, A_KV_HEADS, A_HEAD_DIM)
        qk = jax.nn.silu(short_conv(jnp.concatenate([qb, kb], axis=-1), w_conv))
        to_heads = lambda a: a.reshape(Bn, n, B_HEADS, B_HEAD_DIM).transpose(0, 2, 1, 3).astype(jnp.float32)
        qm, km, vm = to_heads(qk[..., :B_W]), to_heads(qk[..., B_W:]), to_heads(vb)
        g = (gt + b_gate).astype(jnp.float32).reshape(Bn, n, 2, 2, B_HEADS).transpose(2, 3, 0, 4, 1)
        ig = g[:, 0]
        lf = jax.nn.log_sigmoid(g[:, 1])
        return (qa, ka, va), (qm, km, vm, ig, lf), ob

    def mlstm_out(hm, ob):
        n = hm.shape[2]
        hm = rmsnorm(jnp.swapaxes(hm, 1, 2), g_hn.reshape(B_HEADS, B_HEAD_DIM))
        return hm.reshape(Bn, n, B_W).astype(ob.dtype) * jax.nn.sigmoid(ob)

    (qa_c, ka_c, va_c), mc, ob_c = project(h_ctx)
    (qa_l, ka_l, va_l), ml, ob_l = project(h_lat)
    cos, sin = axial_rope(L)
    qa_l = apply_rope(qa_l, cos, sin)
    ka_l = apply_rope(ka_l, cos, sin)
    o_a = attend_blocks(qa_l, jnp.concatenate([ka_c, ka_l], axis=1), jnp.concatenate([va_c, va_l], axis=1))
    st0 = mlstm_zero_state(Bn)
    h_c, ctx_states = mlstm_bidir(*mc, (st0, st0))
    h_l, _ = mlstm_bidir(*ml, ctx_states)
    y = jnp.concatenate([o_a, mlstm_out(h_l, ob_l)], axis=-1) @ w_out
    yc = None
    if ctx_out:
        yc = jnp.concatenate([attend_blocks(qa_c, ka_c, va_c), mlstm_out(h_c, ob_c)], axis=-1) @ w_out
    return y, yc

def pool_mixer(h, w_in, w_grp, s_pool):
    Bn, n, _ = h.shape
    u = h @ w_in
    uf = u.astype(jnp.float32)
    S = jnp.pad(jnp.cumsum(uf, axis=1), ((0, 0), (1, 0), (0, 0)))
    t = jnp.arange(n)
    outs = []
    for gi, w in enumerate(POOL_WINDOWS):
        lo = w // 2
        hi = w - 1 - lo
        a = jnp.clip(t - lo, 0, n - 1)
        e = jnp.clip(t + hi, 0, n - 1)
        Sg = S[:, :, gi * POOL_GROUP:(gi + 1) * POOL_GROUP]
        cnt = (e - a + 1).astype(jnp.float32)[None, :, None]
        outs.append((Sg[:, e + 1] - Sg[:, a]) / cnt - uf[:, :, gi * POOL_GROUP:(gi + 1) * POOL_GROUP])
    p = jnp.stack(outs, axis=2).astype(u.dtype)
    y = jnp.einsum('bngc,gce->bnge', p, w_grp).reshape(Bn, n, D_MODEL)
    return y * s_pool

def ec_moe(h, w_router, w_gate, w_up, w_down):
    Bn, n, Dm = h.shape
    cap = max(1, EC_FACTOR * n // N_EXPERTS)
    aff = jax.nn.softmax(jnp.einsum('bnd,de->bne', h, w_router).astype(jnp.float32), axis=-1)
    gate, idx = lax.top_k(jnp.swapaxes(aff, 1, 2), cap)
    xs = jax.vmap(lambda hb, ib: hb[ib])(h, idx)
    a = jax.nn.silu(jnp.einsum('becd,edf->becf', xs, w_gate)) * jnp.einsum('becd,edf->becf', xs, w_up)
    out = jnp.einsum('becf,efd->becd', a, w_down) * gate[..., None].astype(h.dtype)
    return jax.vmap(lambda ob, ib: jnp.zeros((n, Dm), ob.dtype).at[ib.reshape(-1)].add(ob.reshape(-1, Dm)))(out, idx)

def first_inputs(seed: int = 0) -> dict:
    key = jax.random.key(seed)
    ks = jax.random.split(key, 23)
    nrm = lambda k, shape, s: s * jax.random.normal(k, shape, jnp.float32)
    fb = jnp.linspace(3.0, 6.0, B_HEADS)
    gate_base = jnp.concatenate([jnp.zeros((B_HEADS,)), fb, jnp.zeros((B_HEADS,)), fb])
    return {
        "x": nrm(ks[0], (BATCH, SEQ, D_MODEL), 1.0),
        "c": nrm(ks[1], (BATCH, D_MODEL), 1.0),
        "ctx": nrm(ks[2], (BATCH, CTX_LEN, D_MODEL), 1.0),
        "c_ctx": nrm(ks[3], (D_MODEL,), 1.0),
        "w_mod": nrm(ks[4], (DEPTH, D_MODEL, 6 * D_MODEL), 0.5 * D_MODEL ** -0.5),
        "b_mod": nrm(ks[5], (DEPTH, 6 * D_MODEL), 0.02),
        "g_norm1": 1.0 + nrm(ks[6], (DEPTH, D_MODEL), 0.02),
        "g_norm2": 1.0 + nrm(ks[7], (DEPTH, D_MODEL), 0.02),
        "w_in_even": nrm(ks[8], (N_EVEN, D_MODEL, EVEN_IN), D_MODEL ** -0.5),
        "w_out_even": nrm(ks[9], (N_EVEN, MIX_W, D_MODEL), MIX_W ** -0.5),
        "g_qnorm": 1.0 + nrm(ks[10], (N_EVEN, A_HEAD_DIM), 0.02),
        "g_knorm": 1.0 + nrm(ks[11], (N_EVEN, A_HEAD_DIM), 0.02),
        "w_conv": nrm(ks[12], (N_EVEN, B_CONV, 2 * B_W), B_CONV ** -0.5),
        "b_gate": gate_base[None] + nrm(ks[13], (N_EVEN, N_GATES), 0.1),
        "g_hnorm": 1.0 + nrm(ks[14], (N_EVEN, B_W), 0.02),
        "w_in_odd": nrm(ks[15], (N_ODD, D_MODEL, D_MODEL), D_MODEL ** -0.5),
        "w_pool_grp": nrm(ks[16], (N_ODD, 4, POOL_GROUP, POOL_GROUP), POOL_GROUP ** -0.5),
        "s_pool": 1.0 + nrm(ks[17], (N_ODD, D_MODEL), 0.1),
        "w_router": nrm(ks[18], (DEPTH, D_MODEL, N_EXPERTS), D_MODEL ** -0.5),
        "w_exp_gate": nrm(ks[19], (DEPTH, N_EXPERTS, D_MODEL, D_EXPERT), D_MODEL ** -0.5),
        "w_exp_up": nrm(ks[20], (DEPTH, N_EXPERTS, D_MODEL, D_EXPERT), D_MODEL ** -0.5),
        "w_exp_down": nrm(ks[21], (DEPTH, N_EXPERTS, D_EXPERT, D_MODEL), D_EXPERT ** -0.5),
        "g_final": 1.0 + nrm(ks[22], (D_MODEL,), 0.02),
    }

def first_block(x, c, ctx, c_ctx, w_mod, b_mod, g_norm1, g_norm2, w_in_even, w_out_even, g_qnorm, g_knorm,
              w_conv, b_gate, g_hnorm, w_in_odd, w_pool_grp, s_pool, w_router, w_exp_gate, w_exp_up,
              w_exp_down, g_final):
    xc = ctx
    for i in range(DEPTH):
        ctx_next = any(j % 2 == 0 for j in range(i + 1, DEPTH))
        ctx_used = (i % 2 == 0) or ctx_next
        m_lat = adaln(c, w_mod[i], b_mod[i])
        h = modulate(x, g_norm1[i], m_lat[..., 0, :], m_lat[..., 1, :])
        yc = None
        if ctx_used:
            m_ctx = adaln(c_ctx, w_mod[i], b_mod[i])
            hc = modulate(xc, g_norm1[i], m_ctx[..., 0, :], m_ctx[..., 1, :])
        if i % 2 == 0:
            e = i // 2
            y, yc = even_mixer(h, hc, ctx_next, w_in_even[e], w_out_even[e], g_qnorm[e], g_knorm[e],
                               w_conv[e], b_gate[e], g_hnorm[e])
        else:
            o = i // 2
            y = pool_mixer(h, w_in_odd[o], w_pool_grp[o], s_pool[o])
            if ctx_next:
                yc = pool_mixer(hc, w_in_odd[o], w_pool_grp[o], s_pool[o])
        x = x + m_lat[..., 2, :] * y
        h = modulate(x, g_norm2[i], m_lat[..., 3, :], m_lat[..., 4, :])
        x = x + m_lat[..., 5, :] * ec_moe(h, w_router[i], w_exp_gate[i], w_exp_up[i], w_exp_down[i])
        if ctx_next:
            xc = xc + m_ctx[..., 2, :] * yc
            hc = modulate(xc, g_norm2[i], m_ctx[..., 3, :], m_ctx[..., 4, :])
            xc = xc + m_ctx[..., 5, :] * ec_moe(hc, w_router[i], w_exp_gate[i], w_exp_up[i], w_exp_down[i])
    return rmsnorm(x, g_final)


CHUNK = 64
D_FF = 2816

A_HEADS_2 = 4
A_QK_DIM = 64
A_V_DIM = 2 * A_QK_DIM
A_WIDTH = A_HEADS_2 * A_V_DIM
A_COLS = 3 * A_WIDTH

B_HEAD_DIM_2 = 64
B_WIDTH = D_MODEL - A_WIDTH
B_HEADS_2 = B_WIDTH // B_HEAD_DIM_2
B_DECAY_RANK = 64
B_A_RANK = 64
B_GATE_RANK = 128
B_VRES_RANK = 32
B_LN_EPS = 64e-5
B_COLS = 3 * B_WIDTH + B_DECAY_RANK + B_A_RANK + B_GATE_RANK
B_SPLITS = [B_WIDTH, 2 * B_WIDTH, 3 * B_WIDTH, 3 * B_WIDTH + B_DECAY_RANK,
            3 * B_WIDTH + B_DECAY_RANK + B_A_RANK]
EVEN_IN_2 = A_COLS + B_COLS

C_HEADS = 4
C_QK_DIM = D_MODEL // C_HEADS
C_V_DIM = 2 * C_QK_DIM
C_QK_WIDTH = C_HEADS * C_QK_DIM
C_V_WIDTH = C_HEADS * C_V_DIM
ODD_IN = 2 * C_QK_WIDTH + 2 * C_V_WIDTH

N_EVEN_2 = (DEPTH + 1) // 2
N_ODD_2 = DEPTH // 2


def rms_norm(x, g, eps=NORM_EPS):
    xf = x.astype(jnp.float32)
    y = xf * lax.rsqrt(jnp.mean(xf * xf, axis=-1, keepdims=True) + eps)
    return (y * g.astype(jnp.float32)).astype(x.dtype)

def swiglu(x, w_gu, w_d):
    gate, up = jnp.split(x @ w_gu, 2, axis=-1)
    return (jax.nn.silu(gate) * up) @ w_d

def token_shift(z, mu):
    z_prev = jnp.pad(z, ((0, 0), (1, 0), (0, 0)))[:, :-1]
    return z + (z_prev - z) * mu

def diff_attention(q, k, v, lam):
    S_ = q.shape[1]
    q = q * (A_QK_DIM ** -0.5)
    slopes = 2.0 ** (-8.0 / A_HEADS_2 * jnp.arange(1, A_HEADS_2 + 1, dtype=jnp.float32))
    pos = jnp.arange(S_)
    chunk_id = pos // CHUNK
    outs = []
    for s0 in range(0, S_, Q_BLOCK):
        kend = s0 + Q_BLOCK
        scores = jnp.einsum('bqhmd,bkhmd->bhmqk', q[:, s0:kend], k[:, :kend]).astype(jnp.float32)
        dist = jnp.abs(pos[s0:kend][:, None] - pos[:kend][None, :]).astype(jnp.float32)
        bias = -slopes[:, None, None, None] * dist
        allowed = chunk_id[:kend][None, :] <= chunk_id[s0:kend][:, None]
        scores = jnp.where(allowed, scores + bias, -jnp.inf)
        p = jax.nn.softmax(scores, axis=-1)
        p = p[:, :, 0] - lam * p[:, :, 1]
        outs.append(jnp.einsum('bhqk,bkhe->bqhe', p.astype(v.dtype), v[:, :kend]))
    return jnp.concatenate(outs, axis=1)

def rwkv7_recurrence(r, w, k, v, kk, a):
    Bn, _, H, N = r.shape

    def step(state, inp):
        r_t, w_t, k_t, v_t, kk_t, a_t = inp
        sa = jnp.einsum('bhvk,bhk->bhv', state, -kk_t)
        state = (state * w_t[:, :, None, :]
                 + sa[..., None] * (kk_t * a_t)[:, :, None, :]
                 + v_t[..., None] * k_t[:, :, None, :])
        return state, jnp.einsum('bhvk,bhk->bhv', state, r_t)

    xs = tuple(jnp.moveaxis(t, 1, 0) for t in (r, w, k, v, kk, a))
    state0 = jnp.zeros((Bn, H, N, N), jnp.float32)
    _, y = lax.scan(step, state0, xs)
    return jnp.moveaxis(y, 0, 1)

def head_group_norm(y, w, b):
    Bn, S_ = y.shape[:2]
    mean = jnp.mean(y, axis=-1, keepdims=True)
    var = jnp.mean(jnp.square(y - mean), axis=-1, keepdims=True)
    yn = (y - mean) * lax.rsqrt(var + B_LN_EPS)
    return yn.reshape(Bn, S_, -1) * w + b

def rwkv7_time_mix(zb, mu, vec, w_up, a_up, g_up, v_first, vres):
    Bn, S_, _ = zb.shape
    f32 = jnp.float32
    zs = token_shift(zb.astype(f32), mu.astype(f32))
    r, k, v, xw, xa, xg = jnp.split(zs, B_SPLITS, axis=-1)
    w0, a0, k_k, k_a, r_k, ln_w, ln_b = vec.astype(f32)
    w = -jax.nn.softplus(-(w0 + jnp.tanh(xw) @ w_up.astype(f32))) - 0.5
    decay = jnp.exp(-jnp.exp(w))
    if vres is not None:
        v0, v_down, v_up = vres
        v = v + (v_first - v) * jax.nn.sigmoid(v0.astype(f32) + (v @ v_down.astype(f32)) @ v_up.astype(f32))
    a = jax.nn.sigmoid(a0 + xa @ a_up.astype(f32))
    g = jax.nn.sigmoid(xg) @ g_up.astype(f32)
    heads = lambda t: t.reshape(Bn, S_, B_HEADS_2, B_HEAD_DIM_2)
    kk = heads(k * k_k)
    kk = kk / jnp.maximum(jnp.sqrt(jnp.sum(kk * kk, axis=-1, keepdims=True)), 1e-12)
    k = k * (1.0 + (a - 1.0) * k_a)
    rh, kh, vh = heads(r), heads(k), heads(v)
    y = rwkv7_recurrence(rh, heads(decay), kh, vh, kk, heads(a))
    y = head_group_norm(y, ln_w, ln_b)
    r_k_h = r_k.reshape(B_HEADS_2, B_HEAD_DIM_2)
    bonus = jnp.sum(rh * kh * r_k_h, axis=-1, keepdims=True) * vh
    y = y + bonus.reshape(Bn, S_, B_WIDTH)
    return y * g, v

def diff_rwkv_mixer(h, w_in, w_out, lam_vecs, subln, lam_init, mu, vec, w_up, a_up, g_up, v_first, vres):
    Bn, S_, _ = h.shape
    z = h @ w_in
    za, zb = z[..., :A_COLS], z[..., A_COLS:]
    qa, ka, va = jnp.split(za, 3, axis=-1)
    qa = qa.reshape(Bn, S_, A_HEADS_2, 2, A_QK_DIM)
    ka = ka.reshape(Bn, S_, A_HEADS_2, 2, A_QK_DIM)
    va = va.reshape(Bn, S_, A_HEADS_2, A_V_DIM)
    lv = lam_vecs.astype(jnp.float32)
    lam = jnp.exp(jnp.sum(lv[0] * lv[1])) - jnp.exp(jnp.sum(lv[2] * lv[3])) + lam_init
    oa = diff_attention(qa, ka, va, lam)
    oa = rms_norm(oa, subln) * (1.0 - lam_init)
    ob, v_b = rwkv7_time_mix(zb, mu, vec, w_up, a_up, g_up, v_first, vres)
    mix = jnp.concatenate([oa.reshape(Bn, S_, A_WIDTH), ob.astype(h.dtype)], axis=-1)
    return mix @ w_out, v_b

def retention(q, k, v):
    Bn, S_, H, _ = q.shape
    dk, dv = q.shape[-1], v.shape[-1]
    n_chunks = S_ // CHUNK
    log_g = jnp.log(1.0 - 2.0 ** (-5.0 - jnp.arange(H, dtype=jnp.float32)))
    idx = jnp.arange(CHUNK, dtype=jnp.float32)
    intra = jnp.exp(log_g[:, None, None] * jnp.abs(idx[:, None] - idx[None, :]))
    q_decay = jnp.exp(log_g[:, None] * (idx + 1.0))
    k_decay = jnp.exp(log_g[:, None] * (CHUNK - 1.0 - idx))
    chunk_decay = jnp.exp(log_g * CHUNK)

    def to_chunks(t):
        return t.reshape(Bn, n_chunks, CHUNK, H, t.shape[-1]).transpose(1, 0, 3, 2, 4)

    def step(state, inp):
        qc, kc, vc = inp
        scores = jnp.einsum('bhid,bhjd->bhij', qc, kc) * intra
        y = (jnp.einsum('bhij,bhjv->bhiv', scores, vc)
             + jnp.einsum('bhid,bhdv->bhiv', qc, state) * q_decay[:, :, None])
        state = (state * chunk_decay[:, None, None]
                 + jnp.einsum('bhjd,bhjv->bhdv', kc * k_decay[:, :, None], vc))
        return state, y

    state0 = jnp.zeros((Bn, H, dk, dv), jnp.float32)
    _, y = lax.scan(step, state0, (to_chunks(q), to_chunks(k), to_chunks(v)))
    return y.transpose(1, 0, 3, 2, 4).reshape(Bn, S_, H, dv)

def retention_mixer(h, w_in, w_out):
    Bn, S_, _ = h.shape
    z = (h @ w_in).astype(jnp.float32)
    q, k, v, g = jnp.split(z, [C_QK_WIDTH, 2 * C_QK_WIDTH, 2 * C_QK_WIDTH + C_V_WIDTH], axis=-1)
    q = q.reshape(Bn, S_, C_HEADS, C_QK_DIM)
    k = k.reshape(Bn, S_, C_HEADS, C_QK_DIM) * (C_QK_DIM ** -0.5)
    v = v.reshape(Bn, S_, C_HEADS, C_V_DIM)
    y = retention(q, k, v)
    y = y * lax.rsqrt(jnp.mean(y * y, axis=-1, keepdims=True) + NORM_EPS)
    y = jax.nn.silu(g) * y.reshape(Bn, S_, C_V_WIDTH)
    return y.astype(h.dtype) @ w_out

def second_inputs(seed: int = 0) -> dict:
    key = jax.random.key(seed)
    ks = jax.random.split(key, 24)
    nrm = lambda k, shape, s: s * jax.random.normal(k, shape, jnp.float32)
    x = nrm(ks[0], (BATCH, SEQ, D_MODEL), 1.0)
    norms = 1.0 + nrm(ks[1], (DEPTH, 6, D_MODEL), 0.05)
    ffn_wgu = nrm(ks[2], (DEPTH, 2, D_MODEL, 2 * D_FF), D_MODEL ** -0.5)
    ffn_wd = nrm(ks[3], (DEPTH, 2, D_FF, D_MODEL), D_FF ** -0.5)
    even_w_in = nrm(ks[4], (N_EVEN_2, D_MODEL, EVEN_IN_2), D_MODEL ** -0.5)
    even_w_out = nrm(ks[5], (N_EVEN_2, D_MODEL, D_MODEL), D_MODEL ** -0.5)
    diff_lam = nrm(ks[6], (N_EVEN_2, 4, A_QK_DIM), 0.1)
    diff_subln = 1.0 + nrm(ks[7], (N_EVEN_2, A_V_DIM), 0.05)
    rwkv_mu = jax.random.uniform(ks[8], (N_EVEN_2, B_COLS), jnp.float32)
    vshape = (N_EVEN_2, B_WIDTH)
    w0 = jnp.linspace(-6.0, -1.0, B_WIDTH, dtype=jnp.float32)[None, :] + nrm(ks[9], vshape, 0.1)
    a0 = nrm(ks[10], vshape, 0.1)
    k_k = 0.85 + nrm(ks[11], vshape, 0.05)
    k_a = 1.0 + nrm(ks[12], vshape, 0.05)
    r_k = nrm(ks[13], vshape, 0.1)
    ln_w = 1.0 + nrm(ks[14], vshape, 0.05)
    ln_b = nrm(ks[15], vshape, 0.02)
    rwkv_vec = jnp.stack([w0, a0, k_k, k_a, r_k, ln_w, ln_b], axis=1)
    rwkv_w_up = nrm(ks[16], (N_EVEN_2, B_DECAY_RANK, B_WIDTH), 0.1 * B_DECAY_RANK ** -0.5)
    rwkv_a_up = nrm(ks[17], (N_EVEN_2, B_A_RANK, B_WIDTH), 0.5 * B_A_RANK ** -0.5)
    rwkv_g_up = nrm(ks[18], (N_EVEN_2, B_GATE_RANK, B_WIDTH), B_GATE_RANK ** -0.5)
    rwkv_v0 = nrm(ks[19], (N_EVEN_2 - 1, B_WIDTH), 0.1)
    rwkv_v_down = nrm(ks[20], (N_EVEN_2 - 1, B_WIDTH, B_VRES_RANK), B_WIDTH ** -0.5)
    rwkv_v_up = nrm(ks[21], (N_EVEN_2 - 1, B_VRES_RANK, B_WIDTH), 0.5 * B_VRES_RANK ** -0.5)
    odd_w_in = nrm(ks[22], (N_ODD_2, D_MODEL, ODD_IN), D_MODEL ** -0.5)
    odd_w_out = nrm(ks[23], (N_ODD_2, C_V_WIDTH, D_MODEL), C_V_WIDTH ** -0.5)
    return {'x': x, 'norms': norms, 'ffn_wgu': ffn_wgu, 'ffn_wd': ffn_wd,
            'even_w_in': even_w_in, 'even_w_out': even_w_out,
            'diff_lam': diff_lam, 'diff_subln': diff_subln,
            'rwkv_mu': rwkv_mu, 'rwkv_vec': rwkv_vec,
            'rwkv_w_up': rwkv_w_up, 'rwkv_a_up': rwkv_a_up, 'rwkv_g_up': rwkv_g_up,
            'rwkv_v0': rwkv_v0, 'rwkv_v_down': rwkv_v_down, 'rwkv_v_up': rwkv_v_up,
            'odd_w_in': odd_w_in, 'odd_w_out': odd_w_out}

def second_block(x, norms, ffn_wgu, ffn_wd, even_w_in, even_w_out, diff_lam, diff_subln,
              rwkv_mu, rwkv_vec, rwkv_w_up, rwkv_a_up, rwkv_g_up,
              rwkv_v0, rwkv_v_down, rwkv_v_up, odd_w_in, odd_w_out):
    v_first = None
    for i in range(DEPTH):
        g = norms[i]
        x = x + 0.5 * rms_norm(swiglu(rms_norm(x, g[0]), ffn_wgu[i, 0], ffn_wd[i, 0]), g[1])
        h = rms_norm(x, g[2])
        j = i // 2
        if i % 2 == 0:
            lam_init = 0.8 - 0.6 * math.exp(-0.3 * i)
            vres = None if j == 0 else (rwkv_v0[j - 1], rwkv_v_down[j - 1], rwkv_v_up[j - 1])
            mix, v_b = diff_rwkv_mixer(h, even_w_in[j], even_w_out[j], diff_lam[j], diff_subln[j],
                                       lam_init, rwkv_mu[j], rwkv_vec[j], rwkv_w_up[j],
                                       rwkv_a_up[j], rwkv_g_up[j], v_first, vres)
            if j == 0:
                v_first = v_b
        else:
            mix = retention_mixer(h, odd_w_in[j], odd_w_out[j])
        x = x + rms_norm(mix, g[3])
        x = x + 0.5 * rms_norm(swiglu(rms_norm(x, g[4]), ffn_wgu[i, 1], ffn_wd[i, 1]), g[5])
    return x


def setup_inputs(seed=0):
    out = dict(first_inputs(seed))
    for name, value in second_inputs(seed + 1).items():
        if name != "x":
            out[name + "_2"] = value
    return out


def reference(
    x, c, ctx, c_ctx, w_mod, b_mod, g_norm1, g_norm2, w_in_even, w_out_even, g_qnorm, g_knorm,
    w_conv, b_gate, g_hnorm, w_in_odd, w_pool_grp, s_pool, w_router, w_exp_gate, w_exp_up,
    w_exp_down, g_final, norms_2, ffn_wgu_2, ffn_wd_2, even_w_in_2, even_w_out_2, diff_lam_2,
    diff_subln_2, rwkv_mu_2, rwkv_vec_2, rwkv_w_up_2, rwkv_a_up_2, rwkv_g_up_2, rwkv_v0_2,
    rwkv_v_down_2, rwkv_v_up_2, odd_w_in_2, odd_w_out_2,
):
    x = first_block(
        x, c, ctx, c_ctx, w_mod, b_mod, g_norm1, g_norm2, w_in_even, w_out_even, g_qnorm,
        g_knorm, w_conv, b_gate, g_hnorm, w_in_odd, w_pool_grp, s_pool, w_router, w_exp_gate,
        w_exp_up, w_exp_down, g_final,
    )
    return second_block(
        x, norms_2, ffn_wgu_2, ffn_wd_2, even_w_in_2, even_w_out_2, diff_lam_2, diff_subln_2,
        rwkv_mu_2, rwkv_vec_2, rwkv_w_up_2, rwkv_a_up_2, rwkv_g_up_2, rwkv_v0_2, rwkv_v_down_2,
        rwkv_v_up_2, odd_w_in_2, odd_w_out_2,
    )


_drawn_inputs = setup_inputs


def setup_inputs(seed=0):
    import zlib

    import numpy as np

    out = dict(_drawn_inputs(seed))
    spreads = {}
    factors = {'g_norm1': 3.933,
     'g_qnorm': 8.0,
     'g_knorm': 8.0,
     'g_hnorm': 5.078,
     'rwkv_w_up_2': 8.0,
     'g_norm2': 4.744}
    for name, (base, spread) in spreads.items():
        noise = np.random.default_rng([zlib.crc32(name.encode()), seed]).standard_normal(out[name].shape)
        drawn = base * np.exp(spread * noise) if base else spread * noise
        out[name] = __import__('jax').numpy.asarray(drawn.astype(out[name].dtype))
    for name, factor in factors.items():
        out[name] = (out[name] * factor).astype(out[name].dtype)
    return out
```

```python
from contextlib import ExitStack

import numpy as np
import concourse.bass as bass
from concourse import mybir

F32 = mybir.dt.float32
U32 = mybir.dt.uint32
ALU = mybir.AluOpType
ACT = mybir.ActivationFunctionType
AX = mybir.AxisListType.X

D = 1024
T = 256
EPS = 1e-6
NSLOT = 6
SLOT = 4096
NEG = 1e30
A_COLS = 1536
ZB = 1792
D_FF = 2816
WINDOWS = (2, 4, 8, 16)
LAM0 = 0.8 - 0.6


def column_table():
    at, n = {}, 0
    for name, k in (("cc", 16), ("g1", 16), ("g2", 16), ("bm", 64), ("nrm", 48), ("conv", 24), ("bgate", 1),
                    ("mu", 14), ("vec", 28)):
        at[name] = n
        n += k
    return at, n


def shape_constants():
    f = np.float32
    cst = {}
    p = np.arange(128)
    base = np.zeros((128, 1024), f)
    base[:, 0:128] = np.eye(128, dtype=f)
    base[:, 128:384] = np.arange(256, dtype=f)[None, :]
    base[:, 384] = p
    base[:, 385] = p + 128
    base[:, 386] = EPS
    base[:, 387] = 64e-5
    base[:, 388] = 1.0
    base[:, 400:528] = (p[:, None] // 64 == p[None, :] // 64)
    base[:, 528:656] = np.eye(128, dtype=f)[:, ::-1]
    base[:, 656:784] = 1.0
    cst["base"] = base
    rows = (np.arange(256) // 64).astype(f)
    cols = (np.arange(256) % 64).astype(f)
    inv = (10000.0 ** (-np.arange(0, 32, 2, dtype=f) / f(32))).astype(f)
    ang = np.stack([rows[:, None] * inv, cols[:, None] * inv], 1).astype(f)
    c, s = np.cos(ang).astype(f), np.sin(ang).astype(f)
    cs = np.zeros((2, 256, 2, 2, 16), f)
    cs[0] = c[:, :, None, :]
    cs[1, :, :, 0] = -s
    cs[1, :, :, 1] = s
    cst["rope"] = cs.reshape(2, 2, 128, 64).transpose(2, 0, 1, 3).reshape(128, 256).copy()
    ml = np.zeros((128, 2, 128), f)
    ml[:, 0] = np.where(p[:, None] <= p[None, :], 0.0, NEG)
    ml[:, 1] = np.where(p[:, None] >= p[None, :], 0.0, NEG)
    cst["mmask"] = ml.reshape(128, 256)
    sel = np.zeros((128, 10, 128), f)
    for d in range(2):
        for h in range(4):
            sel[8 * d + h, 8, 32 * d + h] = 1.0
            sel[8 * d + 4 + h, 9, 32 * d + h] = 1.0
            sel[32 * d + h, 4 * d + h, :] = 1.0
    cst["sel"] = sel.reshape(128, 1280)
    band = np.zeros((4, 256, 256), f)
    t = np.arange(256)
    for g, w in enumerate(WINDOWS):
        lo, hi = w // 2, w - 1 - w // 2
        a, e = np.clip(t - lo, 0, 255), np.clip(t + hi, 0, 255)
        inside = (t[:, None] >= a[None, :]) & (t[:, None] <= e[None, :])
        band[g] = inside / (e - a + 1).astype(f)[None, :] - np.eye(256, dtype=f)
    cst["band"] = band.reshape(4, 2, 128, 256).transpose(2, 0, 1, 3).reshape(128, 2048).copy()
    slopes = 2.0 ** (-2.0 * np.arange(1, 5))
    allowed = (t[None, :] // 64) <= (t[:, None] // 64)
    bias = np.where(allowed[None], -slopes[:, None, None] * np.abs(t[:, None] - t[None, :])[None], -NEG).astype(f)
    cst["dbias"] = np.concatenate([bias[:, 0:128, 0:128], bias[:, 128:256, :]], 2).transpose(1, 0, 2).reshape(128, 1536).copy()
    logg = np.log(1.0 - 2.0 ** (-5.0 - np.arange(4)))
    dist = np.abs(t[:, None] - t[None, :])
    dec = np.where(allowed[None], np.exp(logg[:, None, None] * dist[None]), 0.0).astype(f)
    cst["decay"] = dec.transpose(0, 2, 1).reshape(4, 2, 128, 256).transpose(2, 0, 1, 3).reshape(128, 2048).copy()
    q = np.arange(128) % 64
    u = np.arange(64)
    wm = np.zeros((128, 5, 64), f)
    wm[:, 0] = q[:, None] < u[None, :]
    wm[:, 1] = q[:, None] <= u[None, :]
    wm[:, 2] = (q[:, None] > u[None, :]) & (q[:, None] // 16 == u[None, :] // 16)
    wm[:, 3] = (q[:, None] // 16) > (u[None, :] // 16)
    wm[:, 4] = q[:, None] == u[None, :]
    blk = np.zeros((128, 1, 64), f)
    blk[:, 0] = (q[:, None] // 16) == (u[None, :] // 16)
    cst["wmask"] = np.concatenate([wm, blk], 1).reshape(128, 384).copy()
    return cst


CONST_NAMES = ["base", "rope", "mmask", "sel", "band", "dbias", "decay", "wmask"]


class Program:

    def __init__(self, nc, ctx):
        self.nc = nc
        self.queues = {k: [] for k in "tvags"}
        self.sems = {k: ctx.enter_context(nc.semaphore("done_" + k)) for k in "tvag"}
        self.count = {k: 0 for k in "tvag"}
        self.small = {k: [ctx.enter_context(nc.semaphore(f"small_{k}{i}")) for i in range(12)] for k in "gs"}
        self.small_used = {k: [0] * 12 for k in "gs"}
        self.small_n = {k: 0 for k in "gs"}

    def put(self, k, fn, after, inc=True):
        after = [m for m in after if m is not None]
        if inc:
            self.count[k] += 1
            self.queues[k].append((after, fn, (self.sems[k], 1)))
            return (self.sems[k], self.count[k])
        self.queues[k].append((after, fn, None))
        return None

    def t(self, fn, *after, inc=True):
        return self.put("t", fn, after, inc)

    def v(self, fn, *after):
        return self.put("v", fn, after)

    def a(self, fn, *after):
        return self.put("a", fn, after)

    def g(self, fn, *after):
        return self.put("g", fn, after)

    def mm(self, out, pairs, *after, start=True, stop=True):
        n = len(pairs)
        mark = None
        for i, (l, r) in enumerate(pairs):
            mark = self.t(lambda e, o=out, l=l, r=r, s=start and i == 0, q=stop and i == n - 1:
                          e.matmul(o, l, r, start=s, stop=q, skip_group_check=True),
                          *(after if i == 0 else ()), inc=i == n - 1)
        return mark

    def tr(self, out, src, ident, *after, inc=True):
        return self.t(lambda e: e.transpose(out, src, ident), *after, inc=inc)

    def dma(self, k, out, src, *after, **kw):
        sems, used = self.small[k], self.small_used[k]
        i = self.small_n[k] % len(sems)
        self.small_n[k] += 1
        before = (sems[i], 16 * used[i]) if used[i] else None
        used[i] += 1
        after = [m for m in list(after) + [before] if m is not None]
        self.queues[k].append((after, lambda e: e.dma_start(out, src, **kw), (sems[i], 16)))
        return (sems[i], 16 * used[i])

    def last(self, k):
        return (self.sems[k], self.count[k]) if self.count[k] else None

    def fence(self):
        marks = [self.last(k) for k in "tvag"] + [(self.small[k][i], 16 * n) for k in "gs"
                                                   for i, n in enumerate(self.small_used[k]) if n]
        for k in "tvag":
            self.queues[k].append(([m for m in marks if m is not None], None, None))

    def emit(self, k, eng):
        seen = {}
        for after, fn, inc in self.queues[k]:
            need = {}
            for sem, n in after:
                if n > seen.get(sem.num, 0):
                    need[sem.num] = (sem, max(n, need.get(sem.num, (sem, 0))[1]))
            for num, (sem, n) in need.items():
                eng.wait_ge(sem, n)
                seen[num] = n
            if fn is not None:
                ins = fn(eng)
                if inc is not None:
                    ins.then_inc(*inc)


class Banks:

    def __init__(self, ps, ids):
        self.ps, self.ids, self.n = ps, ids, 0
        self.freed = {i: None for i in ids}

    def take(self):
        i = self.ids[self.n % len(self.ids)]
        self.n += 1
        return i, self.ps[:, i, :], self.freed[i]

    def free(self, i, mark):
        self.freed[i] = mark


class Ring:

    def __init__(self, P, tile, ctx):
        self.P, self.tile = P, tile
        self.sems = [ctx.enter_context(P.nc.semaphore(f"slot{i}")) for i in range(NSLOT)]
        self.fills = [0] * NSLOT
        self.freed = [None] * NSLOT
        self.n = 0

    def load(self, *pieces):
        i = self.n % NSLOT
        self.n += 1
        for k, (view, src) in enumerate(pieces):
            self.P.queues["s"].append(([self.freed[i]] if k == 0 and self.freed[i] else [],
                                       lambda e, o=view(self.tile[:, i, :]), s=src: e.dma_start(o, s),
                                       (self.sems[i], 16)))
            self.fills[i] += 16
        return i, self.tile[:, i, :], (self.sems[i], self.fills[i])

    def free(self, i, mark):
        self.freed[i] = mark


class Arena:
    def __init__(self, tile, n):
        self.tile, self.n, self.at = tile, n, 0

    def take(self, *shape):
        n = int(np.prod(shape))
        a = self.tile[:, self.at:self.at + n]
        self.at += n
        assert self.at <= self.n, (self.at, self.n)
        if len(shape) == 2:
            a = a.rearrange("p (a b) -> p a b", a=shape[0])
        elif len(shape) == 3:
            a = a.rearrange("p (a b c) -> p a b c", a=shape[0], b=shape[1])
        elif len(shape) == 4:
            a = a.rearrange("p (a b c d) -> p a b c d", a=shape[0], b=shape[1], c=shape[2])
        return a

    def mark(self):
        return self.at

    def back(self, at):
        self.at = at


class Kernel:
    def __init__(self, nc, ctx, I, out):
        self.nc, self.I, self.out = nc, I, out
        self.P = Program(nc, ctx)
        total = 53000
        big = ctx.enter_context(nc.sbuf_tensor("big", [128, total], F32))
        self.ps = ctx.enter_context(nc.psum_tensor("ps", [128, 8, 512], F32))
        self.R = Ring(self.P, big[:, 0:NSLOT * SLOT].rearrange("p (a b) -> p a b", a=NSLOT), ctx)
        self.A = Arena(big, total)
        self.A.take(NSLOT * SLOT)

    def evac(self, k, out, src, *after):
        if k == "v":
            return self.P.v(lambda e: e.tensor_copy(out, src), *after)
        return self.P.a(lambda e: e.activation(out, src, ACT.Copy), *after)

    def affine(self, k, out, src, scale, bias, *after):
        if k == "v":
            if bias is None:
                return self.P.v(lambda e: e.tensor_scalar(out, src, scale, None, ALU.mult), *after)
            return self.P.v(lambda e: e.tensor_scalar(out, src, scale, bias, ALU.mult, ALU.add), *after)
        if bias is None:
            return self.P.a(lambda e: e.activation(out, src, ACT.Copy, scale=scale), *after)
        return self.P.a(lambda e: e.activation(out, src, ACT.Identity, scale=scale, bias=bias), *after)

    def rstd(self, out, sums, n, eps, *after):
        m = self.P.a(lambda e: e.activation(out, sums, ACT.Sqrt, scale=1.0 / n, bias=eps), *after)
        return self.P.v(lambda e: e.reciprocal(out, out), m)

    def rms_rows(self, srcs, outs, junk, stat, after):
        P = self.P
        marks = []
        n = len(srcs)
        for i, (s, j) in enumerate(zip(srcs, junk)):
            marks.append(P.a(lambda e, s=s, j=j, i=i: e.activation(j, s, ACT.Square, accum_out=stat[:, i:i + 1]),
                             *after[i]))
        m = self.rstd(stat[:, n:2 * n], stat[:, 0:n], D, self.eps, *marks)
        return [P.v(lambda e, s=s, o=o, i=i: e.tensor_scalar(o, s, stat[:, n + i:n + i + 1], None, ALU.mult), m)
                for i, (s, o) in enumerate(zip(srcs, outs))]

    def to_columns(self, rows, dst, off, scale, bias, banks, after):
        P = self.P
        marks = []
        nk = dst.shape[1]
        for kc in range(0, nk, 2):
            b, ps, free = banks.take()
            for u in range(2):
                for tt in range(2):
                    m = P.tr(ps[:, (2 * u + tt) * 128:(2 * u + tt + 1) * 128],
                             rows[tt][:, (kc + u) * 128:(kc + u + 1) * 128], self.ident, free, *after,
                             inc=(u == 1 and tt == 1))
            ms = []
            if scale is None:
                ms.append(self.evac("va"[kc // 2 % 2], dst[:, kc:kc + 2, off:off + 256],
                                    ps.rearrange("p (a b) -> p a b", a=2), m))
            else:
                for u in range(2):
                    ms.append(self.affine("va"[kc // 2 % 2], dst[:, kc + u, off:off + 256],
                                          ps[:, u * 256:(u + 1) * 256], scale(kc + u),
                                          None if bias is None else bias(kc + u), m))
            banks.free(b, ms[-1])
            marks += ms
        return marks

    def cols(self, W, c0, n):
        view = lambda s: s[:, 0:8 * n].rearrange("p (k n) -> p k n", k=8)
        i, s, m = self.R.load((view, W[0:1024, c0:c0 + n].rearrange("(k p) n -> p k n", p=128)))
        return i, view(s), m

    def rows(self, W, k0, nk):
        view = lambda s: s[:, 0:nk * 1024].rearrange("p (k n) -> p k n", k=nk)
        i, s, m = self.R.load((view, W[k0 * 128:(k0 + nk) * 128, 0:1024].rearrange("(k p) n -> p k n", p=128)))
        return i, view(s), m

    def load_constants(self):
        P, A, I = self.P, self.A, self.I
        self.X = A.take(2, D)
        base = A.take(1024)
        self.col_at, ncol = column_table()
        self.vc = A.take(ncol)
        m = [P.dma("g", base, I["k_base"]), P.dma("g", self.vc, I["vc"])]
        self.m_x = [P.dma("g", self.X[:, i, :], I["x"][0, i * 128:(i + 1) * 128, :]) for i in range(2)]
        self.ident = base[:, 0:128]
        self.iota = base[:, 128:384]
        self.iota_p = [base[:, 384:385], base[:, 385:386]]
        self.eps = base[:, 386:387]
        self.eps_ln = base[:, 387:388]
        self.onecol = base[:, 388:389]
        self.bones = base[:, 400:528]
        self.anti = base[:, 528:656]
        self.ones = base[:, 656:784]
        self.keep = A.mark()
        self.gate = A.take(2, D)
        self.colm = A.take(64)
        self.AC = A.take(2, 8, 2)
        for k in "tvag":
            self.P.queues[k].append((m, None, None))
        sc = A.take(16)
        self.screp = A.take(8, 128)
        m = P.a(lambda e: e.activation(sc, self.col("cc", 16), ACT.Silu))
        self.sc = sc
        self.m_sc = P.v(lambda e: e.tensor_copy(self.screp, sc.rearrange("p (k t) -> p k t", t=2)[:, :, 0:1]
                                                .broadcast_to([128, 8, 128])), m)

    def col(self, name, n, off=0):
        a = self.col_at[name] + off
        return self.vc[:, a:a + n]

    def adaln(self, i):
        P, A, I = self.P, self.A, self.I
        at = A.mark()
        bm = A.take(2, D)
        W = I["w_mod"][i]
        mb = [P.dma("g", bm[:, j, :], I["b_mod"][i:i + 1, s * D:(s + 1) * D].broadcast_to([128, D]), P.last("v"))
              for j, s in enumerate((2, 5))]
        cb = self.ps[:, 7, :]
        banks = Banks(self.ps, [0, 1, 2, 3])
        done = []
        for blk in range(12):
            sec = blk // 2
            s, w, mw = self.cols(W, blk * 512, 512)
            if sec in (2, 5):
                b, ps, free = banks.take()
                m = P.mm(ps, [(self.screp[:, k, :], w[:, k, :]) for k in range(8)], mw, free, self.m_sc)
                j = sec == 5
                sl = slice((blk % 2) * 512, (blk % 2) * 512 + 512)
                m2 = P.v(lambda e, ps=ps, j=j, sl=sl: e.tensor_tensor(self.gate[:, int(j), sl], ps, bm[:, int(j), sl], ALU.add),
                         m, mb[int(j)])
                banks.free(b, m2)
                done.append(m2)
            else:
                for q in range(4):
                    tile = {0: 0, 1: 8, 3: 16, 4: 24}[sec] + (blk % 2) * 4 + q
                    m = P.mm(cb[:, 2 * tile:2 * tile + 2],
                             [(w[:, k, q * 128:(q + 1) * 128], self.sc[:, 2 * k:2 * k + 2]) for k in range(8)],
                             mw, self.m_sc)
            self.R.free(s, m)
            last = m
        cm = self.colm
        m = P.v(lambda e: e.tensor_tensor(cm.rearrange("p (a b) -> p a b", b=2), cb[:, 0:64].rearrange("p (a b) -> p a b", b=2),
                                          self.col("bm", 32, 32 * i).unsqueeze(2).broadcast_to([128, 32, 2]), ALU.add), last)
        c4 = cm.rearrange("p (s k t) -> p s k t", s=4, t=2)
        ms = []
        for w, (g, s) in enumerate((("g1", 1), ("g2", 3))):
            ms.append(P.v(lambda e, w=w, g=g, s=s: e.scalar_tensor_tensor(
                self.AC[:, w, :, :], c4[:, s, :, :], 1.0, self.col(g, 8, 8 * i).unsqueeze(2).broadcast_to([128, 8, 2]),
                ALU.add, ALU.mult), m))
        self.m_mod = ms + done
        self.B = lambda w, kc, t: c4[:, 2 * w, kc, t:t + 1]
        self.Ac = lambda w, kc, t: self.AC[:, w, kc, t:t + 1]
        A.back(at)
        P.fence()

    def even_mixer(self):
        P, A, I = self.P, self.A, self.I
        banks = Banks(self.ps, [0, 1, 2, 3, 4, 5, 6])
        at0 = A.mark()
        stat = A.take(96)
        rope = A.take(2, 2, 64)
        mmask = A.take(2, 128)
        sel = A.take(10, 128)
        grow = A.take(2, 64)
        ghn = A.take(512)
        m_c = [P.dma("g", rope, I["k_rope"].rearrange("p (a b c) -> p a b c", a=2, b=2)),
               P.dma("g", mmask, I["k_mmask"].rearrange("p (a b) -> p a b", a=2)),
               P.dma("g", sel, I["k_sel"].rearrange("p (a b) -> p a b", a=10)),
               P.dma("g", grow[:, 0, :], I["g_qnorm"][0:1, :].broadcast_to([128, 64])),
               P.dma("g", grow[:, 1, :], I["g_knorm"][0:1, :].broadcast_to([128, 64])),
               P.dma("g", ghn, I["g_hnorm"][0:1, :].broadcast_to([128, 512]))]
        for k in "tvag":
            P.queues[k].append((m_c, None, None))
        QK = A.take(8, 512)
        V1 = A.take(4, 4, 129)
        OB = A.take(2, 512)
        QA = A.take(2, 512)
        KA = A.take(4, 2, 2, 64)
        VA = A.take(4, 128)
        G16 = A.take(512)
        at1 = A.mark()
        HT = A.take(8, 512)
        at2 = A.mark()
        XN = A.take(2, D)
        CTX = A.take(2, D)
        junk = QK[:, 0:4, :].rearrange("p (a b) c -> p a (b c)", a=2)
        m_ctx = [P.dma("g", CTX[:, i, :], I["ctx"][0, i * 128:(i + 1) * 128, :]) for i in range(2)]
        rows = lambda t: [t[:, 0, :], t[:, 1, :]]
        m = self.rms_rows(rows(self.X), rows(XN), rows(junk), stat[:, 0:4], [(x,) for x in self.m_x])
        m_h = self.to_columns(rows(XN), HT, 256, lambda k: self.Ac(0, k, 0), lambda k: self.B(0, k, 0), banks,
                              m + self.m_mod)
        m = self.rms_rows(rows(CTX), rows(CTX), rows(junk), stat[:, 4:8], [(x, P.last("v")) for x in m_ctx])
        m_h += self.to_columns(rows(CTX), HT, 0, lambda k: self.Ac(0, k, 1), lambda k: self.B(0, k, 1), banks, m)
        W = I["w_in_even"][0]

        def row_form(c0, n, tiles, use):
            s, w, mw = self.cols(W, c0, n)
            for t in tiles:
                b, ps, free = banks.take()
                m = P.mm(ps[:, 0:n], [(HT[:, k, t * 128:(t + 1) * 128], w[:, k, :]) for k in range(8)],
                         mw, free, *m_h)
                banks.free(b, use(t, ps, m))
            self.R.free(s, m)

        s, w, mw = self.cols(W, 2816, 16)
        b, ps, free = banks.take()
        m = P.mm(ps[0:16, :], [(w[:, k, :], HT[:, k, :]) for k in range(8)], mw, free, *m_h)
        self.R.free(s, m)
        m_g16 = P.v(lambda e, ps=ps: e.tensor_scalar(G16[0:16, :], ps[0:16, :], self.col("bgate", 1)[0:16, :], None, ALU.add), m)
        banks.free(b, m_g16)

        A.back(at2)
        RAW = A.take(8, 512)
        P.fence()
        m_raw = {}
        for c0, base, lo in ((1280, 4, 0), (768, 0, 256)):
            s, w, mw = self.cols(W, c0, 512)
            for q in range(4):
                b, ps, free = banks.take()
                n = 512 - lo
                m = P.mm(ps[:, 0:n], [(w[:, k, q * 128:(q + 1) * 128], HT[:, k, lo:512]) for k in range(8)], mw, free)
                m_raw[base + q] = self.evac("av"[q % 2], RAW[:, base + q, lo:512], ps[:, 0:n], m)
                banks.free(b, m_raw[base + q])
            self.R.free(s, m)
        for j in (4, 5, 6, 7, 0, 1, 2, 3):
            for lo in ((0, 256) if j >= 4 else (256,)):
                w0, w1, w2 = (self.col("conv", 1, 8 * i + j) for i in range(3))
                src, dst = RAW[:, j, lo:lo + 256], QK[:, j, lo:lo + 256]
                m = P.v(lambda e, s=src, d=dst, w=w1: e.tensor_scalar(d, s, w, None, ALU.mult), m_raw[j])
                m = P.v(lambda e, s=src, d=dst, w=w0: e.scalar_tensor_tensor(d[:, 1:256], s[:, 0:255], w, d[:, 1:256],
                                                                             ALU.mult, ALU.add), m)
                m = P.v(lambda e, s=src, d=dst, w=w2: e.scalar_tensor_tensor(d[:, 0:255], s[:, 1:256], w, d[:, 0:255],
                                                                             ALU.mult, ALU.add), m)
                m_qk = P.a(lambda e, d=dst: e.activation(d, d, ACT.Silu), m)
        m_k = []
        for j in range(4, 8):
            m_k.append(P.g(lambda e, j=j: e.tensor_scalar(QK[:, j, :], QK[:, j, :], 128.0 ** -0.5, None, ALU.mult), m_qk))
        m_one = P.g(lambda e: e.memset(V1[:, :, :, 128:129], 1.0))
        m_v1 = {}

        def use_v(t, ps, m):
            m_v1[t] = self.evac("a", V1[:, t, :, 0:128], ps.rearrange("p (h d) -> p h d", h=4), m)
            return m_v1[t]

        row_form(1792, 512, range(4), use_v)

        def use_o(t, ps, m):
            return P.a(lambda e: e.activation(OB[:, t - 2, :], ps, ACT.Sigmoid), m)

        row_form(2304, 512, (2, 3), use_o)
        m_kv = {}

        def use_kv(t, ps, m):
            P.v(lambda e: e.tensor_copy(KA[:, t, :, 0, :], ps[:, 0:128].rearrange("p (h d) -> p h d", h=2)), m)
            m_kv[t] = P.v(lambda e: e.tensor_copy(VA[:, t, :], ps[:, 128:256]), m)
            return m_kv[t]

        row_form(512, 256, range(4), use_kv)

        def use_q(t, ps, m):
            m_kv[t + 2] = self.evac("a", QA[:, t - 2, :], ps, m)
            return m_kv[t + 2]

        row_form(0, 512, (2, 3), use_q)
        P.fence()
        A.back(at1)
        MT = A.take(8, 256)
        self.mlstm(QK, V1, OB, G16, stat, mmask, sel, ghn, MT, banks)
        P.fence()
        self.attention(QA, KA, VA, stat, rope, grow, MT, banks)
        P.fence()
        tmp = A.take(2, 512)
        W = I["w_out_even"][0]
        for half in range(2):
            s, w, mw = self.cols(W, half * 512, 512)
            for t in range(2):
                b, ps, free = banks.take()
                sl = slice(half * 512, half * 512 + 512)
                m = P.mm(ps, [(MT[:, k, t * 128:(t + 1) * 128], w[:, k, :]) for k in range(8)], mw, free)
                m1 = P.v(lambda e, ps=ps, t=t, sl=sl: e.tensor_tensor(tmp[:, t, :], ps, self.gate[:, 0, sl], ALU.mult),
                         m, P.last("g"))
                banks.free(b, m1)
                P.g(lambda e, t=t, sl=sl: e.tensor_tensor(self.X[:, t, sl], self.X[:, t, sl], tmp[:, t, :], ALU.add), m1)
            self.R.free(s, m)
        P.fence()
        A.back(at0)

    def mlstm(self, QK, V1, OB, G16, stat, mmask, sel, ghn, MT, banks):
        P, A = self.P, self.A
        at = A.mark()
        IG, LF, BB, MM = (A.take(512) for _ in range(4))
        GG, MB = IG, LF
        P.g(lambda e: e.memset(IG, 0.0))
        mz = P.g(lambda e: e.memset(LF, 0.0))
        for which, dst in ((8, IG), (9, LF)):
            b, ps, free = banks.take()
            m = P.mm(ps[0:64, :], [(sel[0:16, which, 0:64], G16[0:16, :])], free)
            P.v(lambda e, ps=ps, d=dst: e.tensor_copy(d[0:4, :], ps[0:4, :]), m, mz)
            flip = lambda a: a.rearrange("p (c t) -> p c t", c=2)[:, :, ::-1]
            mf = P.v(lambda e, ps=ps, d=dst: e.tensor_copy(d[32:36, :].rearrange("p (c t) -> p c t", c=2), flip(ps[32:36, :])), m, mz)
            banks.free(b, mf)
        R = slice(0, 36)
        m = P.v(lambda e: e.scalar_tensor_tensor(BB[R, :], LF[R, :], -1.0, LF[R, :], ALU.mult, ALU.max), mf)
        m = P.a(lambda e: e.activation(BB[R, :], BB[R, :], ACT.Exp, scale=-1.0), m)
        m = P.a(lambda e: e.activation(BB[R, :], BB[R, :], ACT.Ln, bias=self.onecol[R, :]), m)
        m = P.v(lambda e: e.scalar_tensor_tensor(LF[R, :], LF[R, :], 0.0, BB[R, :], ALU.min, ALU.subtract), m)
        m = P.v(lambda e: e.tensor_tensor_scan(BB[R, :], self.onecol[R, :].broadcast_to([36, 512]), LF[R, :], 0.0, ALU.mult, ALU.add), m)
        mb = m
        m = P.v(lambda e: e.tensor_tensor(GG[R, :], IG[R, :], BB[R, :], ALU.subtract), m)
        mg = m
        m = P.v(lambda e: e.tensor_tensor_scan(MM[R, :], GG[R, :], GG[R, :], -NEG, ALU.max, ALU.max), m)
        mm_ = m
        m_mb = P.v(lambda e: e.tensor_tensor(MB[R, :], MM[R, :], BB[R, :], ALU.add), m)
        for src, dst in ((GG, BB), (MM, IG), (MB, MM)):
            P.v(lambda e, s=src, o=dst: e.tensor_copy(o[0:4, :], s[0:4, :]), P.last("v"))
            m_mb = P.v(lambda e, s=src, o=dst: e.tensor_copy(o[32:36, :].rearrange("p (c t) -> p c t", c=2), flip(s[32:36, :])), P.last("v"))
        GT, MX, MBT = BB, IG, MM
        GC = A.take(4, 36)
        EM = A.take(4, 36)
        for src, dst in ((GT, GC), (MBT, EM)):
            b, ps, free = banks.take()
            for c in range(4):
                m = P.tr(ps[:, c * 36:c * 36 + 36], src[R, c * 128:(c + 1) * 128], self.ident[0:36, 0:36], free, m_mb, inc=c == 3)
            if dst is GC:
                m = P.v(lambda e, ps=ps: e.tensor_copy(GC, ps[:, 0:144].rearrange("p (a b) -> p a b", a=4)), m)
                m_gc = m
            else:
                m = P.a(lambda e, ps=ps: e.activation(EM, ps[:, 0:144].rearrange("p (a b) -> p a b", a=4), ACT.Exp, scale=-1.0), m)
                m_em = m
            banks.free(b, m)
        order = [[0, 1, 2, 3], [1, 0, 3, 2]]
        KR = A.take(4, 4, 128)
        HO = A.take(2, 2, 512)
        CS = A.take(2, 129)
        ME = A.take(2, 4)
        W2 = A.take(8)
        DT, ST, QS, KW = (MT[:, i:i + 1, :].rearrange("p a (b c) -> p (a b) c", b=2) for i in range(4))
        DN = A.take(16)
        WS = A.take(2, 8)
        for c in range(4):
            b, ps, free = banks.take()
            for h in range(4):
                m = P.tr(ps[:, h * 128:(h + 1) * 128], QK[:, 4 + h, c * 128:(c + 1) * 128], self.ident, free, inc=h == 3)
            m_kr = self.evac("av"[c % 2], KR[:, :, c, :], ps.rearrange("p (h d) -> p h d", h=4), m)
            banks.free(b, m_kr)
        qt = lambda h, c: QK[:, h, c * 128:(c + 1) * 128]
        kt = lambda h, c: QK[:, 4 + h, c * 128:(c + 1) * 128]
        for d in range(2):
            P.fence()
            for h in range(4):
                r = 32 * d + h
                bc = self.ps[:, 7, :]
                m = P.mm(bc, [(sel[R, 4 * d + h, :], MX[R, :])], P.last("v"), P.last("a"))
                me = ME[:, h % 2, :]
                m_me = P.v(lambda e, d=d, me=me: e.tensor_copy(me, bc.rearrange("p (c t) -> p c t", c=4)[:, :, 0 if d else 127]),
                           m, P.last("a"))
                mw = P.v(lambda e, r=r, me=me: e.tensor_tensor(W2[:, 0:4], GC[:, :, r], me, ALU.subtract), m_me, m_gc, P.last("a"))
                for c in (1, 2):
                    p0, p1 = order[d][c - 1], order[d][c]
                    mw = P.v(lambda e, c=c, p0=p0, p1=p1, me=me: e.tensor_tensor(
                        W2[:, 3 + c:4 + c], me[:, p0:p0 + 1], me[:, p1:p1 + 1], ALU.subtract), m_me)
                w = WS[:, h % 2, :]
                m_w = P.a(lambda e, w=w: e.activation(w[:, 0:6], W2[:, 0:6], ACT.Exp), mw, P.last("v"))
                m_state = None
                for c in range(4):
                    oc = order[d][c]
                    cs = CS[:, c % 2, :]
                    pc = CS[:, (c + 1) % 2, :]
                    if c >= 2:
                        u = c % 2
                        dt, st, qs = DT[:, u, :], ST[:, u, :], QS[:, u, :]
                        bcc = bc[:, oc * 128:(oc + 1) * 128]
                        m1 = P.v(lambda e, oc=oc, r=r, dt=dt, bcc=bcc, d=d: e.scalar_tensor_tensor(
                            dt, bcc, GC[:, oc, r:r + 1], mmask[:, d, :], ALU.subtract, ALU.max), m_gc, m_me)
                        m1 = P.a(lambda e, dt=dt: e.activation(dt, dt, ACT.Exp, scale=-1.0), m1)
                        b, ps, free = banks.take()
                        m2 = P.mm(ps[:, 0:128], [(kt(h, oc), qt(h, oc))], free)
                        m3 = P.v(lambda e, ps=ps, dt=dt, st=st: e.tensor_tensor(st, dt, ps[:, 0:128], ALU.mult), m1, m2, P.last("t"))
                        pe = order[d][c - 1]
                        m4 = P.a(lambda e, qs=qs, bcc=bcc, me=me, pe=pe: e.activation(qs, bcc, ACT.Exp, scale=-1.0, bias=me[:, pe:pe + 1]),
                                 m_me, P.last("t"))
                        m5 = P.v(lambda e, h=h, oc=oc, qs=qs: e.tensor_tensor(qs, qs, qt(h, oc), ALU.mult), m4)
                        m6 = P.mm(ps[:, 256:385], [(st, V1[:, oc, h, :]), (qs, pc)], m3, m5, m_state)
                        dn = DN[:, 4 * u:4 * u + 1]
                        m7 = P.v(lambda e, ps=ps, dn=dn, oc=oc, r=r: e.tensor_scalar(dn, ps[:, 384:385], -1.0, EM[:, oc, r:r + 1], ALU.mult, ALU.max),
                                 m6, m_em)
                        m7 = P.v(lambda e, ps=ps, dn=dn: e.tensor_tensor(dn, dn, ps[:, 384:385], ALU.max), m7)
                        m7 = P.v(lambda e, dn=dn: e.reciprocal(dn, dn), m7)
                        m8 = P.v(lambda e, ps=ps, dn=dn, h=h, oc=oc, d=d: e.tensor_scalar(
                            HO[:, d, oc - 2, h * 128:(h + 1) * 128], ps[:, 256:384], dn, None, ALU.mult), m7)
                        banks.free(b, m8)
                    if c < 3:
                        kw = KW[:, c % 2, :]
                        m1 = P.v(lambda e, h=h, oc=oc, w=w, kw=kw: e.tensor_scalar(kw, KR[:, h, oc, :], w[:, oc:oc + 1], None, ALU.mult),
                                 m_w, P.last("t"))
                        b, ps, free = banks.take()
                        m2 = P.mm(ps[:, 0:129], [(kw, V1[:, oc, h, :])], m1, free)
                        if c == 0:
                            m_state = P.v(lambda e, ps=ps, cs=cs: e.tensor_copy(cs, ps[:, 0:129]), m2, P.last("t"))
                        else:
                            m_state = P.v(lambda e, ps=ps, cs=cs, pc=pc, c=c, w=w: e.scalar_tensor_tensor(
                                cs, pc, w[:, 3 + c:4 + c], ps[:, 0:129], ALU.mult, ALU.add), m2, m_state, P.last("t"))
                        banks.free(b, m_state)
        P.fence()
        sq = LF
        HM = KR.rearrange("p a b c -> p (a b c)")[:, 0:1024].rearrange("p (a b) -> p a b", a=2)
        for t in range(2):
            b, ps, free = banks.take()
            m = P.mm(ps, [(self.ident, HO[:, 0, t, :]), (self.ident, HO[:, 1, t, :])], free)
            m1 = P.a(lambda e, ps=ps: e.activation(sq, ps, ACT.Square), m, P.last("v"))
            s4 = stat[:, 16 + 8 * t:20 + 8 * t]
            m2 = P.v(lambda e, s4=s4: e.tensor_reduce(s4, sq.rearrange("p (h d) -> p h d", h=4), AX, ALU.add), m1)
            m3 = self.rstd(s4, s4, 128, self.eps, m2)
            m4 = P.v(lambda e, ps=ps, t=t, s4=s4: e.tensor_tensor(HM[:, t, :].rearrange("p (h d) -> p h d", h=4),
                                                           ps.rearrange("p (h d) -> p h d", h=4),
                                                           s4.unsqueeze(2).broadcast_to([128, 4, 128]), ALU.mult), m3)
            banks.free(b, m4)
            m5 = P.v(lambda e, t=t: e.tensor_tensor(HM[:, t, :], HM[:, t, :], ghn, ALU.mult), m4)
            m_hm = P.v(lambda e, t=t: e.tensor_tensor(HM[:, t, :], HM[:, t, :], OB[:, t, :], ALU.mult), m5)
        self.to_columns([HM[:, 0, :], HM[:, 1, :]], MT[:, 4:8, :], 0, None, None, banks, [m_hm])
        P.fence()
        A.back(at)

    def attention(self, QA, KA, VA, stat, rope, grow, MT, banks):
        P, A = self.P, self.A
        at = A.mark()
        sq = A.take(512)
        t1 = A.take(512)
        t2 = A.take(512)
        KT = A.take(2, 512)
        QT = A.take(4, 256)
        kview = lambda t: KA[:, t, :, 0, :]
        qview = lambda t: QA[:, t, :].rearrange("p (h d) -> p h d", h=8)
        m_fin = []
        for which, (view, heads, tiles, lat) in enumerate(((qview, 8, (0, 1), (0, 1)), (kview, 2, (0, 1, 2, 3), (2, 3)))):
            for t in tiles:
                x = view(t)
                n = heads * 64
                as3 = lambda a, heads=heads, n=n: a[:, 0:n].rearrange("p (h d) -> p h d", h=heads)
                st = stat[:, 32:32 + heads]
                m = P.a(lambda e, x=x, as3=as3: e.activation(as3(sq), x, ACT.Square), P.last("v"))
                m = P.v(lambda e, as3=as3, st=st: e.tensor_reduce(st, as3(sq), AX, ALU.add), m)
                m = self.rstd(st, st, 64, self.eps, m)
                m = P.v(lambda e, x=x, st=st, heads=heads: e.tensor_tensor(x, x, st.unsqueeze(2).broadcast_to([128, heads, 64]), ALU.mult), m)
                m = P.v(lambda e, x=x, heads=heads, which=which: e.tensor_tensor(
                    x, x, grow[:, which:which + 1, :].broadcast_to([128, heads, 64]), ALU.mult), m)
                if t in lat:
                    lt = t - lat[0]
                    cosv, sinv = rope[:, 0, lt, :], rope[:, 1, lt, :]
                    ma = P.g(lambda e, x=x, as3=as3, c=cosv, heads=heads: e.tensor_tensor(
                        as3(t1), x, c.unsqueeze(1).broadcast_to([128, heads, 64]), ALU.mult), m)
                    for half in range(2):
                        mb = P.v(lambda e, x=x, as3=as3, s=sinv, heads=heads, half=half: e.tensor_tensor(
                            as3(t2).rearrange("p h (a b c) -> p h a b c", a=2, b=2)[:, :, :, half, :],
                            x.rearrange("p h (a b c) -> p h a b c", a=2, b=2)[:, :, :, 1 - half, :],
                            s.rearrange("p (a b c) -> p a b c", a=2, b=2)[:, :, half, :].unsqueeze(1).broadcast_to([128, heads, 2, 16]),
                            ALU.mult), m)
                    m = P.v(lambda e, x=x, as3=as3: e.tensor_tensor(x, as3(t1), as3(t2), ALU.add), ma, mb)
                if which == 1:
                    m = P.v(lambda e, t=t: e.tensor_copy(KA[:, t, :, 1, :], KA[:, t, :, 0, :]), m)
                m_fin.append(m)
        mq = self.to_columns([QA[:, 0, :], QA[:, 1, :]], QT, 0, None, None, banks, [m_fin[1]])
        mk = []
        for kv in range(2):
            b, ps, free = banks.take()
            for t in range(4):
                m = P.tr(ps[:, t * 128:(t + 1) * 128], KA[:, t, kv, :, :].rearrange("p a d -> p (a d)"), self.ident, free,
                         *m_fin, inc=t == 3)
            mk.append(self.evac("a", KT[:, kv, :], ps, m))
            banks.free(b, mk[-1])
        SP_ = A.take(2, 512)
        PT = A.take(2, 512)
        OA = A.take(2, 512)
        mx = A.take(16)
        sm = A.take(16)
        rd = {0: None, 1: None}
        rp = {0: None, 1: None}
        ob = self.ps[:, 7, :]
        for t in range(2):
            for h in range(8):
                u = h % 2
                i = 8 * t + h
                hp = slice(64 * u, 64 * u + 64)
                b, ps, free = banks.take()
                m = P.mm(ps, [(QT[hp, h // 2, t * 128:(t + 1) * 128], KT[hp, h // 4, :])], free, *(mq + mk))
                m1 = P.v(lambda e, ps=ps, i=i: e.tensor_reduce(mx[:, i:i + 1], ps, AX, ALU.max), m)
                m1 = P.v(lambda e, i=i: e.tensor_scalar(mx[:, i:i + 1], mx[:, i:i + 1], -0.125, None, ALU.mult), m1)
                m2 = P.a(lambda e, ps=ps, i=i, u=u: e.activation(SP_[:, u, :], ps, ACT.Exp, scale=0.125, bias=mx[:, i:i + 1],
                                                                 accum_out=sm[:, i:i + 1]), m1, rd[u])
                banks.free(b, m2)
                b, ps, free = banks.take()
                for c in range(4):
                    m3 = P.tr(ps[:, c * 128:(c + 1) * 128], SP_[:, u, c * 128:(c + 1) * 128], self.ident, m2, free, inc=c == 3)
                rd[u] = m3
                m4 = self.evac("va"[u], PT[:, u, :], ps, m3, rp[u])
                banks.free(b, m4)
                kv = h // 4
                m5 = P.mm(ob[:, h * 64:(h + 1) * 64], [(PT[:, u, c * 128:(c + 1) * 128], VA[:, c, kv * 64:(kv + 1) * 64]) for c in range(4)],
                          m4, P.last("v") if h == 0 else None)
                rp[u] = m5
            m6 = P.v(lambda e, t=t: e.reciprocal(sm[:, 8 * t:8 * t + 8], sm[:, 8 * t:8 * t + 8]), m2)
            m7 = P.v(lambda e, t=t: e.tensor_tensor(OA[:, t, :].rearrange("p (h d) -> p h d", h=8), ob.rearrange("p (h d) -> p h d", h=8),
                                                    sm[:, 8 * t:8 * t + 8].unsqueeze(2).broadcast_to([128, 8, 64]), ALU.mult), m5, m6)
        self.to_columns([OA[:, 0, :], OA[:, 1, :]], MT[:, 0:4, :], 0, None, None, banks, [m7])
        P.fence()
        A.back(at)

    def moe(self, i):
        P, A, I = self.P, self.A, self.I
        at0 = A.mark()
        banks = Banks(self.ps, [0, 1, 2, 3, 4, 5])
        rows = lambda t: [t[:, 0, :], t[:, 1, :]]
        XS = A.take(8, 512)
        GR = A.take(16, 256)
        at1 = A.mark()
        XN = A.take(2, D)
        HT = A.take(8, 256)
        PN = A.take(2, 512)
        WR = A.take(8, 16)
        AF = A.take(2, 16)
        stat = A.take(24)
        CUR = A.take(2, 256)
        VL = A.take(32)
        IX = A.take(32)
        IF = A.take(32)
        REP = A.take(128)
        MI = A.take(16, 32)
        IC = A.take(16)
        VCOL = A.take(16)
        m_wr = P.dma("g", WR, I["w_router"][i].rearrange("(k p) e -> p k e", p=128))
        m = self.rms_rows(rows(self.X), rows(XN), [XS[:, 0:2, :].rearrange("p a b -> p (a b)"), XS[:, 2:4, :].rearrange("p a b -> p (a b)")],
                          stat[:, 0:4], [(), ()])
        m_xn = m
        mh = self.to_columns(rows(XN), HT, 0, lambda k: self.Ac(1, k, 0), lambda k: self.B(1, k, 0), banks, m + self.m_mod)
        b, lg, free = banks.take()
        ms = []
        for t in range(2):
            ms.append(P.mm(lg[:, 16 * t:16 * t + 16], [(HT[:, k, t * 128:(t + 1) * 128], WR[:, k, :]) for k in range(8)], free, m_wr, *mh))
        m = P.v(lambda e: e.tensor_reduce(stat[:, 8:10], lg[:, 0:32].rearrange("p (t e) -> p t e", t=2), AX, ALU.max), *ms)
        m = P.v(lambda e: e.tensor_scalar(stat[:, 10:12], stat[:, 8:10], -1.0, None, ALU.mult), m)
        for t in range(2):
            me = P.a(lambda e, t=t: e.activation(AF[:, t, :], lg[:, 16 * t:16 * t + 16], ACT.Exp, bias=stat[:, 10 + t:11 + t],
                                                 accum_out=stat[:, 12 + t:13 + t]), m)
        banks.free(b, me)
        m = P.v(lambda e: e.reciprocal(stat[:, 14:16], stat[:, 12:14]), me)
        m = P.v(lambda e: e.tensor_tensor(AF, AF, stat[:, 14:16].unsqueeze(2).broadcast_to([128, 2, 16]), ALU.mult), m)
        b, ps, free = banks.take()
        for t in range(2):
            m2 = P.tr(ps[0:16, t * 128:(t + 1) * 128], AF[:, t, :], self.ident, free, m, inc=t == 1)
        E = slice(0, 16)
        m = P.v(lambda e, ps=ps: e.tensor_copy(CUR[E, 0, :], ps[E, 0:256]), m2)
        banks.free(b, m)
        for r in range(4):
            cur, nxt = CUR[E, r % 2, :], CUR[E, (r + 1) % 2, :]
            v8 = VL[E, 8 * r:8 * r + 8]
            i8 = IX[E, 8 * r:8 * r + 8].bitcast(U32)
            mv = P.v(lambda e, v8=v8, cur=cur: e.max(v8, cur), m)
            P.v(lambda e, v8=v8, cur=cur, i8=i8: e.max_index(i8, v8, cur), mv)
            m = P.v(lambda e, v8=v8, cur=cur, nxt=nxt: e.match_replace(nxt, v8, cur, -1.0), mv)
        m = P.v(lambda e: e.tensor_copy(IF[E, :], IX[E, :].bitcast(U32)), P.last("v"))
        for src, dst in ((IF, IC), (VL, VCOL)):
            m1 = P.v(lambda e, src=src: e.tensor_copy(REP[E, :].rearrange("p (a b) -> p a b", a=4),
                                                      src[E, :].unsqueeze(1).broadcast_to([16, 4, 32])), m, P.last("t"))
            b, ps2, free = banks.take()
            m2 = P.tr(ps2[:, 0:16], REP[E, :], self.ident[E, 0:16], free, m1)
            m_ic = P.v(lambda e, dst=dst, ps2=ps2: e.tensor_copy(dst, ps2[:, 0:16]), m2)
            banks.free(b, m_ic)
        m1 = P.v(lambda e: e.tensor_tensor(MI[E, :, :], IF[E, :].unsqueeze(1).broadcast_to([16, 16, 32]),
                                           self.ident[E, 0:16].unsqueeze(2).broadcast_to([16, 16, 32]), ALU.mult), m)
        b, ps3, free = banks.take()
        m2 = P.mm(ps3, [(self.ones[E, :], MI[E, :, :].rearrange("p a b -> p (a b)"))], m1, free)
        for t in range(2):
            m_p = P.v(lambda e, t=t: e.tensor_scalar(PN[:, t, :], ps3, self.iota_p[t], None, ALU.is_equal), m2)
        banks.free(b, m_p)
        for k in range(8):
            b, ps, free = banks.take()
            m = P.mm(ps, [(XN[:, t, k * 128:(k + 1) * 128], PN[:, t, :]) for t in range(2)], m_p, free, *m_xn)
            m_xs = self.affine("av"[k % 2], XS[:, k, :], ps, self.Ac(1, k, 0), self.B(1, k, 0), m)
            banks.free(b, m_xs)
        for e_ in range(16):
            m_gr = P.v(lambda e, n=e_: e.tensor_scalar(GR[:, n, :], self.iota, IC[:, n:n + 1], VCOL[:, n:n + 1],
                                                       ALU.is_equal, ALU.mult), m_ic)
        P.fence()
        A.back(at1)
        SG = A.take(256)
        AA = A.take(256)
        AT = A.take(2, 4, 32)
        OS = A.take(D)
        GU = [self.ps[:, 0, 0:256], self.ps[:, 1, 0:256]]
        TR = self.ps[:, 0, 256:512]
        O = [self.ps[:, 2, :], self.ps[:, 3, :]]
        Y = self.ps[:, 4:8, :]
        free_gu = free_tr = None
        free_o = ()
        m_comb = None
        pend = None

        def combine(n, *mo):
            for t in range(2):
                for hf in range(2):
                    m = P.mm(Y[:, 2 * t + hf, :], [(GR[:, n, t * 128:(t + 1) * 128], OS[:, hf * 512:(hf + 1) * 512])], *mo,
                             start=n == 0, stop=n == 15)
            return m

        for n in range(16):
            for which, name in enumerate(("w_exp_gate", "w_exp_up")):
                for hk in range(2):
                    s, w, mw = self.rows(I[name][i, n], 4 * hk, 4)
                    for k in range(4):
                        for j in range(4):
                            first = k == 0 and j == 0
                            m = P.t(lambda e, j=j, k=k, hk=hk, w=w, which=which, n=n: e.matmul(
                                GU[which][32 * j:32 * j + 32, :], XS[:, 4 * hk + k, 32 * n:32 * n + 32],
                                w[:, k, 256 * j:256 * j + 256], start=hk == 0 and k == 0, stop=hk == 1 and k == 3, skip_group_check=True),
                                *((mw, free_gu) if first else ()), inc=k == 3 and j == 3)
                    self.R.free(s, m)
                if which == 0:
                    mg = P.a(lambda e: e.activation(SG, GU[0], ACT.Silu), m, P.last("v"))
                    if pend is not None:
                        m_comb = combine(*pend)
            ma = P.v(lambda e: e.tensor_tensor(AA, SG, GU[1], ALU.mult), mg, m, P.last("t"))
            free_gu = ma
            for hh in range(2):
                mt = P.tr(TR[:, 128 * hh:128 * hh + 128], AA[:, 128 * hh:128 * hh + 128], self.ident, ma, free_tr, inc=hh == 1)
            m_at = self.evac("v", AT.rearrange("p a b c -> p (a b c)"), TR, mt)
            free_tr = m_at
            for hk in range(2):
                s, w, mw = self.rows(I["w_exp_down"][i, n], 4 * hk, 4)
                for hf in range(2):
                    for j in range(4):
                        kk = 4 * hk + j
                        m = P.t(lambda e, j=j, hf=hf, hk=hk, w=w, kk=kk: e.matmul(
                            O[hf][32 * j:32 * j + 32, :], AT[:, kk % 2, kk // 2, :], w[:, j, 512 * hf:512 * hf + 512],
                            start=hk == 0, stop=hk == 1, skip_group_check=True),
                            *((mw, m_at, *free_o) if j == 0 else ()), inc=hf == 1 and j == 3)
                self.R.free(s, m)
            m1 = P.a(lambda e: e.activation(OS[:, 0:512], O[0], ACT.Copy), m, m_comb)
            m2 = P.v(lambda e: e.tensor_copy(OS[:, 512:1024], O[1]), m, m_comb)
            free_o = (m1, m2)
            pend = (n, m1, m2)
        m = combine(*pend)
        P.fence()
        A.back(at0)
        tmp = A.take(2, 2, 512)
        for t in range(2):
            for hf in range(2):
                sl = slice(512 * hf, 512 * hf + 512)
                m1 = P.v(lambda e, t=t, hf=hf, sl=sl: e.tensor_tensor(tmp[:, t, hf, :], Y[:, 2 * t + hf, :], self.gate[:, 1, sl], ALU.mult), m)
                P.g(lambda e, t=t, hf=hf, sl=sl: e.tensor_tensor(self.X[:, t, sl], self.X[:, t, sl], tmp[:, t, hf, :], ALU.add), m1)
        P.fence()
        A.back(at0)

    def pool_mixer(self):
        P, A, I = self.P, self.A, self.I
        at0 = A.mark()
        banks = Banks(self.ps, list(range(8)))
        rows = lambda t: [t[:, 0, :], t[:, 1, :]]
        XN = A.take(2, D)
        HT = A.take(8, 256)
        U = A.take(2, D)
        BD = A.take(4, 2, 256)
        PT = A.take(8, 256)
        WG = A.take(4, 2, 256)
        SPG = A.take(D)
        stat = A.take(8)
        m_bd = P.dma("g", BD, I["k_band"].rearrange("p (a b c) -> p a b c", a=4, b=2))
        m_wg = P.dma("g", WG, I["w_pool_grp"][0].rearrange("g (k p) n -> p g k n", p=128))
        m_sp = P.dma("g", SPG, I["s_pool"][0:1, :].broadcast_to([128, D]))
        m_sg = P.v(lambda e: e.tensor_tensor(SPG, SPG, self.gate[:, 0, :], ALU.mult), m_sp, *self.m_mod)
        m = self.rms_rows(rows(self.X), rows(XN), rows(U), stat[:, 0:4], [(), ()])
        mh = self.to_columns(rows(XN), HT, 0, lambda k: self.Ac(0, k, 0), lambda k: self.B(0, k, 0), banks, m + self.m_mod)
        for half in range(2):
            s, w, mw = self.cols(I["w_in_odd"][0], half * 512, 512)
            for t in range(2):
                b, ps, free = banks.take()
                m = P.mm(ps, [(HT[:, k, t * 128:(t + 1) * 128], w[:, k, :]) for k in range(8)], mw, free, *mh)
                m_u = self.evac("av"[t], U[:, t, half * 512:half * 512 + 512], ps, m)
                banks.free(b, m_u)
            self.R.free(s, m)
        marks = [P.last("v"), P.last("a")]
        mp = []
        for c in range(0, 8, 2):
            b, ps, free = banks.take()
            for u in range(2):
                m = P.mm(ps[:, 256 * u:256 * u + 256], [(U[:, t, (c + u) * 128:(c + u + 1) * 128], BD[:, c // 2, t, :]) for t in range(2)],
                         free, m_bd, *marks)
            mp.append(self.evac("av"[c // 2 % 2], PT[:, c:c + 2, :], ps.rearrange("p (a b) -> p a b", a=2), m))
            banks.free(b, mp[-1])
        for t in range(2):
            for g2 in range(2):
                b, ps, free = banks.take()
                for u in range(2):
                    g = 2 * g2 + u
                    m = P.mm(ps[:, 256 * u:256 * u + 256], [(PT[:, 2 * g + k, t * 128:(t + 1) * 128], WG[:, g, k, :]) for k in range(2)],
                             free, m_wg, *mp)
                sl = slice(512 * g2, 512 * g2 + 512)
                tmp = XN[:, t, sl]
                m1 = P.v(lambda e, ps=ps, sl=sl, tmp=tmp: e.tensor_tensor(tmp, ps, SPG[:, sl], ALU.mult), m, m_sg)
                banks.free(b, m1)
                P.g(lambda e, t=t, sl=sl, tmp=tmp: e.tensor_tensor(self.X[:, t, sl], self.X[:, t, sl], tmp, ALU.add), m1)
        P.fence()
        A.back(at0)

    def final_norm(self):
        P, A, I = self.P, self.A, self.I
        at0 = A.mark()
        g = A.take(D)
        junk = A.take(2, D)
        stat = A.take(4)
        mg = P.dma("g", g, I["g_final"].rearrange("(a n) -> a n", a=1).broadcast_to([128, D]))
        rows = lambda t: [t[:, 0, :], t[:, 1, :]]
        m = self.rms_rows(rows(self.X), rows(junk), rows(junk), stat, [(), ()])
        for t in range(2):
            P.v(lambda e, t=t: e.tensor_tensor(self.X[:, t, :], junk[:, t, :], g, ALU.mult), mg, m[t])
        P.fence()
        A.back(at0)

    def second_block_memory(self):
        self.A.back(self.keep)

    def pre_norm(self, at, banks, XN, HT, junk, stat):
        rows = lambda t: [t[:, 0, :], t[:, 1, :]]
        m = self.rms_rows(rows(self.X), rows(XN), rows(junk), stat, [(), ()])
        return self.to_columns(rows(XN), HT, 0, lambda k: self.col("nrm", 1, 8 * at + k), None, banks, m)

    def post_norm_add(self, Y, layer, k, factor, junk, stat, m_y, grow, m_g):
        P = self.P
        for t in range(2):
            y = Y[:, 2 * t:2 * t + 2, :].rearrange("p a b -> p (a b)")
            m = P.a(lambda e, t=t, y=y: e.activation(junk[:, t, :], y, ACT.Square, accum_out=stat[:, t:t + 1]), *m_y)
        m = self.rstd(stat[:, 2:4], stat[:, 0:2], D, self.eps, m)
        if factor != 1.0:
            m = P.v(lambda e: e.tensor_scalar(stat[:, 2:4], stat[:, 2:4], factor, None, ALU.mult), m)
        for t in range(2):
            y = Y[:, 2 * t:2 * t + 2, :].rearrange("p a b -> p (a b)")
            m1 = P.v(lambda e, t=t, y=y: e.scalar_tensor_tensor(junk[:, t, :], y, stat[:, 2 + t:3 + t], grow, ALU.mult, ALU.mult), m, m_g)
            P.g(lambda e, t=t: e.tensor_tensor(self.X[:, t, :], self.X[:, t, :], junk[:, t, :], ALU.add), m1)
        P.fence()

    def ffn(self, i, j):
        P, A, I = self.P, self.A, self.I
        at0 = A.mark()
        banks = Banks(self.ps, [0, 1, 2, 3])
        XN, junk = A.take(2, D), A.take(2, D)
        HT = A.take(8, 256)
        HA = A.take(22, 256)
        SG = A.take(4, 256)
        grow = A.take(D)
        stat = A.take(8)
        mg = P.dma("g", grow, I["norms_2"][i, 1 + 4 * j:2 + 4 * j, :].broadcast_to([128, D]))
        mh = self.pre_norm(3 * i + 2 * j, banks, XN, HT, junk, stat[:, 0:4])
        W = I["ffn_wgu_2"][i, j]
        view = lambda c: (lambda s: s.rearrange("p (k n) -> p k n", k=8)[:, :, c:c + 256])
        src = lambda c: W[:, c:c + 256].rearrange("(k p) n -> p k n", p=128)
        m_sg = [None] * 4
        m_ha = []
        for blk in range(11):
            s, w, mw = self.R.load((view(0), src(256 * blk)), (view(256), src(D_FF + 256 * blk)))
            w = w.rearrange("p (k n) -> p k n", k=8)
            for q in range(2):
                f = 2 * blk + q
                b, ps, free = banks.take()
                for u in range(2):
                    m = P.mm(ps[:, 256 * u:256 * u + 256],
                             [(w[:, k, 256 * u + 128 * q:256 * u + 128 * q + 128], HT[:, k, :]) for k in range(8)], mw, free, *mh)
                m1 = P.a(lambda e, ps=ps, f=f: e.activation(SG[:, f % 4, :], ps[:, 0:256], ACT.Silu), m, m_sg[f % 4])
                m2 = P.v(lambda e, ps=ps, f=f: e.tensor_tensor(HA[:, f, :], SG[:, f % 4, :], ps[:, 256:512], ALU.mult), m1)
                m_sg[f % 4] = m2
                banks.free(b, m2)
                m_ha.append(m2)
            self.R.free(s, m)
        Y = self.ps[:, 4:8, :]
        for k0 in range(0, 22, 4):
            nk = min(4, 22 - k0)
            s, w, mw = self.rows(I["ffn_wd_2"][i, j], k0, nk)
            for k in range(nk):
                for t in range(2):
                    for hf in range(2):
                        m = P.mm(Y[:, 2 * t + hf, :], [(HA[:, k0 + k, t * 128:(t + 1) * 128], w[:, k, hf * 512:(hf + 1) * 512])],
                                 mw, m_ha[k0 + k], start=k0 + k == 0, stop=k0 + k == 21)
            self.R.free(s, m)
        self.post_norm_add(Y, i, 1, 0.5, junk, stat[:, 4:8], [m], grow, mg)
        A.back(at0)

    def diff_attention(self, HT, mh, MT, banks):
        P, A, I = self.P, self.A, self.I
        at = A.mark()
        W = I["even_w_in_2"][0]
        QT, KT = A.take(4, 256), A.take(4, 256)
        VA = A.take(2, 512)
        OA = A.take(2, 512)
        bias = A.take(4, 384)
        lam = A.take(256)
        sub = A.take(128)
        S = A.take(2, 512)
        Pm = A.take(2, 256)
        PT = A.take(2, 256)
        stat = A.take(2, 16)
        st8 = A.take(24)
        m_b = P.dma("g", bias, I["k_dbias"].rearrange("p (a b) -> p a b", a=4))
        m_l = P.dma("g", lam, I["diff_lam_2"].rearrange("a b c -> a (b c)").broadcast_to([128, 256]))
        m_s = P.dma("g", sub, I["diff_subln_2"].broadcast_to([128, 128]))
        l4 = lam.rearrange("p (a b c) -> p a b c", a=2, b=2)
        m = P.v(lambda e: e.tensor_tensor(l4[:, :, 0, :], l4[:, :, 0, :], l4[:, :, 1, :], ALU.mult), m_l)
        m = P.v(lambda e: e.tensor_reduce(st8[:, 0:2], l4[:, :, 0, :], AX, ALU.add), m)
        m = P.a(lambda e: e.activation(st8[:, 0:2], st8[:, 0:2], ACT.Exp), m)
        m = P.v(lambda e: e.tensor_tensor(st8[:, 2:3], st8[:, 0:1], st8[:, 1:2], ALU.subtract), m)
        m_lam = P.v(lambda e: e.tensor_scalar(st8[:, 2:3], st8[:, 2:3], LAM0, None, ALU.add), m)
        m_p = []
        for c0, dst, sc in ((0, QT, 0.125), (512, KT, 1.0)):
            s, w, mw = self.cols(W, c0, 512)
            for q in range(4):
                b, ps, free = banks.take()
                m = P.mm(ps[:, 0:256], [(w[:, k, q * 128:(q + 1) * 128], HT[:, k, :]) for k in range(8)], mw, free, *mh)
                m_p.append(P.a(lambda e, ps=ps, dst=dst, q=q, sc=sc: e.activation(dst[:, q, :], ps[:, 0:256], ACT.Copy, scale=sc), m))
                banks.free(b, m_p[-1])
            self.R.free(s, m)
        s, w, mw = self.cols(W, 1024, 512)
        for t in range(2):
            b, ps, free = banks.take()
            m = P.mm(ps, [(HT[:, k, t * 128:(t + 1) * 128], w[:, k, :]) for k in range(8)], mw, free)
            m_p.append(self.evac("a", VA[:, t, :], ps, m))
            banks.free(b, m_p[-1])
        self.R.free(s, m)
        rs, rp, rt = [None] * 2, [None] * 2, [None] * 2
        m_o = None
        for t in range(2):
            n = 128 * (t + 1)
            ob = self.ps[:, 7, :]
            for h in range(4):
                u = h % 2
                sv = S[:, u, 0:2 * n].rearrange("p (a b) -> p a b", a=2)
                off = 128 * t
                for mp in range(2):
                    hp = slice(64 * mp, 64 * mp + 64)
                    b, ps, free = banks.take()
                    m = P.mm(ps[:, 0:n], [(QT[hp, h, t * 128:(t + 1) * 128], KT[hp, h, 0:n])], free, *m_p)
                    m1 = P.v(lambda e, sv=sv, ps=ps, h=h, off=off, n=n, mp=mp: e.tensor_tensor(
                        sv[:, mp, :], ps[:, 0:n], bias[:, h, off:off + n], ALU.add), m, m_b, rp[u])
                    banks.free(b, m1)
                st = stat[:, u, :]
                m1 = P.v(lambda e, sv=sv, st=st: e.tensor_reduce(st[:, 0:2], sv, AX, ALU.max), m1)
                m1 = P.v(lambda e, st=st: e.tensor_scalar(st[:, 0:2], st[:, 0:2], -1.0, None, ALU.mult), m1)
                for mp in range(2):
                    m2 = P.a(lambda e, sv=sv, st=st, mp=mp: e.activation(sv[:, mp, :], sv[:, mp, :], ACT.Exp, bias=st[:, mp:mp + 1],
                                                                        accum_out=st[:, 2 + mp:3 + mp]), m1)
                m3 = P.v(lambda e, st=st: e.reciprocal(st[:, 4:6], st[:, 2:4]), m2)
                m3 = P.v(lambda e, st=st: e.tensor_tensor(st[:, 5:6], st[:, 5:6], st8[:, 2:3], ALU.mult), m3, m_lam)
                m3 = P.v(lambda e, sv=sv, st=st: e.tensor_scalar(sv[:, 1, :], sv[:, 1, :], st[:, 5:6], None, ALU.mult), m3)
                pm = Pm[:, u, 0:n]
                m3 = P.v(lambda e, sv=sv, st=st, pm=pm: e.scalar_tensor_tensor(pm, sv[:, 0, :], st[:, 4:5], sv[:, 1, :], ALU.mult,
                                                                              ALU.subtract), m3, rs[u])
                rp[u] = m3
                b, ps, free = banks.take()
                for c in range(t + 1):
                    m4 = P.tr(ps[:, c * 128:(c + 1) * 128], pm[:, c * 128:(c + 1) * 128], self.ident, m3, free, inc=c == t)
                rs[u] = m4
                m5 = self.evac("a", PT[:, u, 0:n], ps[:, 0:n], m4, rt[u])
                banks.free(b, m5)
                m6 = P.mm(ob[:, h * 128:(h + 1) * 128], [(PT[:, u, c * 128:(c + 1) * 128], VA[:, c, h * 128:(h + 1) * 128])
                                                        for c in range(t + 1)], m5, m_o)
                rt[u] = m6
            sq = S[:, 0, :]
            m7 = P.a(lambda e, ob=ob, sq=sq: e.activation(sq, ob, ACT.Square), m6, rp[0], P.last("v"))
            s4 = st8[:, 8 + 4 * t:12 + 4 * t]
            m7 = P.v(lambda e, s4=s4, sq=sq: e.tensor_reduce(s4, sq.rearrange("p (h d) -> p h d", h=4), AX, ALU.add), m7)
            m7 = self.rstd(s4, s4, 128, self.eps, m7)
            m7 = P.v(lambda e, s4=s4: e.tensor_scalar(s4, s4, 1.0 - LAM0, None, ALU.mult), m7)
            as4 = lambda a: a.rearrange("p (h d) -> p h d", h=4)
            m_o = P.v(lambda e, ob=ob, s4=s4, t=t: e.tensor_tensor(as4(OA[:, t, :]), as4(ob), s4.unsqueeze(2).broadcast_to([128, 4, 128]),
                                                                  ALU.mult), m7)
            rp[0] = m_o
            m8 = P.v(lambda e, t=t: e.tensor_tensor(as4(OA[:, t, :]), as4(OA[:, t, :]), sub.unsqueeze(1).broadcast_to([128, 4, 128]),
                                                    ALU.mult), m_o, m_s)
        self.to_columns([OA[:, 0, :], OA[:, 1, :]], MT[:, 0:4, :], 0, None, None, banks, [m8])
        P.fence()
        A.back(at)

    def diff_rwkv_mixer(self):
        P, A, I = self.P, self.A, self.I
        at0 = A.mark()
        banks = Banks(self.ps, [0, 1, 2, 3, 4, 5, 6])
        MT = A.take(8, 256)
        grow = A.take(D)
        stat = A.take(16)
        QRf = A.take(2048)
        mg = P.dma("g", grow, I["norms_2"][0, 3:4, :].broadcast_to([128, D]))
        HT = QRf.rearrange("p (a b) -> p a b", a=8)
        at1 = A.mark()
        XN, junk = A.take(2, D), A.take(2, D)
        mh = self.pre_norm(1, banks, XN, HT, junk, stat[:, 0:4])
        P.fence()
        A.back(at1)
        self.diff_attention(HT, mh, MT, banks)
        self.rwkv(HT, QRf, MT, banks)
        A.back(at1)
        junk = A.take(2, D)
        Y = self.ps[:, 4:8, :]
        for half in range(2):
            s, w, mw = self.cols(I["even_w_out_2"][0], half * 512, 512)
            for t in range(2):
                m = P.mm(Y[:, 2 * t + half, :], [(MT[:, k, t * 128:(t + 1) * 128], w[:, k, :]) for k in range(8)], mw)
            self.R.free(s, m)
        self.post_norm_add(Y, 0, 3, 1.0, junk, stat[:, 4:8], [m], grow, mg)
        A.back(at0)

    def rwkv(self, HT, QRf, MT, banks):
        P, A, I = self.P, self.A, self.I
        W = I["even_w_in_2"][0]
        buf = [A.take(D) for _ in range(6)]
        gbuf = [A.take(D) for _ in range(4)]
        BT, KT_, BR, KR, VR, BON = (A.take(4, 256) for _ in range(6))
        XWA, XG = A.take(256), A.take(256)
        Z = A.take(2, 257)
        ups, gup = A.take(512), A.take(512)
        wm = A.take(6, 64)
        d0 = A.take(256)
        UB, SA, S = A.take(4, 64), A.take(4, 64), A.take(4, 64)
        m_c = [P.dma("g", ups[0:64, :], I["rwkv_w_up_2"][0]), P.dma("g", ups[64:128, :], I["rwkv_a_up_2"][0]),
               P.dma("g", gup, I["rwkv_g_up_2"][0]), P.dma("g", wm, I["k_wmask"].rearrange("p (a b) -> p a b", a=6))]
        for k in "tvag":
            P.queues[k].append((m_c, None, None))
        P.g(lambda e: e.memset(Z[:, :, 0:1], 0.0))
        P.g(lambda e: e.memset(d0, 1.0))
        m_z0 = P.g(lambda e: e.memset(d0.rearrange("p (a b) -> p a b", b=64)[:, :, 0:1], 0.0), P.last("g"))
        t4 = lambda a: a.rearrange("p (a b) -> p a b", a=4)
        r, k, v = t4(buf[0]), t4(buf[1]), t4(buf[2])
        dst = [r[:, i, :] for i in range(4)] + [k[:, i, :] for i in range(4)] + [v[:, i, :] for i in range(4)] + [XWA, XG]
        rz = [None, None]
        for n0, n in ((0, 4), (4, 4), (8, 4), (12, 2)):
            s, w, mw = self.cols(W, A_COLS + 128 * n0, 128 * n)
            for q in range(n):
                j = n0 + q
                z = Z[:, j % 2, :]
                b, ps, free = banks.take()
                m = P.mm(ps[:, 0:256], [(w[:, kc, q * 128:(q + 1) * 128], HT[:, kc, :]) for kc in range(8)], mw, free)
                m1 = P.a(lambda e, z=z, ps=ps: e.activation(z[:, 1:257], ps[:, 0:256], ACT.Copy), m, rz[j % 2], m_z0)
                banks.free(b, m1)
                m2 = P.v(lambda e, z=z, o=dst[j]: e.tensor_tensor(o, z[:, 0:256], z[:, 1:257], ALU.subtract), m1)
                m_zs = P.v(lambda e, z=z, o=dst[j], j=j: e.scalar_tensor_tensor(o, o, self.col("mu", 1, j), z[:, 1:257], ALU.mult, ALU.add), m2)
                rz[j % 2] = m_zs
            self.R.free(s, m)
        vec = lambda i, p: self.col("vec", 1, 4 * i + p)
        SG, AA, KK = t4(buf[3]), t4(buf[4]), t4(buf[5])
        P0, P1, PI, TM = (t4(g) for g in gbuf)
        m_th = P.a(lambda e: e.activation(XWA[0:64, :], XWA[0:64, :], ACT.Tanh), m_zs)
        m_xg = P.a(lambda e: e.activation(XG, XG, ACT.Sigmoid), m_zs)
        ms, mk = [], []
        for p in range(4):
            for lo, dd, vi, out in ((0, m_th, 0, SG), (64, m_zs, 1, AA)):
                b, ps, free = banks.take()
                m = P.mm(ps[:, 0:256], [(ups[lo:lo + 64, p * 128:(p + 1) * 128], XWA[lo:lo + 64, :])], dd, free)
                m = P.a(lambda e, ps=ps, out=out, p=p, vi=vi: e.activation(out[:, p, :], ps[:, 0:256], ACT.Sigmoid, bias=vec(vi, p)), m)
                banks.free(b, m)
                ms.append(m)
            mk.append(P.v(lambda e, p=p: e.tensor_tensor_scan(P0[:, p, :], d0, SG[:, p, :], 0.0, ALU.mult, ALU.add), ms[-2], m_z0))
        m1 = P.v(lambda e: e.tensor_tensor(P1, P0, SG, ALU.subtract), mk[-1])
        C = float(np.exp(-0.5))
        m_pi = P.a(lambda e: e.activation(PI, P0, ACT.Exp, scale=C), mk[-1])
        m_p1 = P.a(lambda e: e.activation(P1, P1, ACT.Exp, scale=-C), m1)
        m_p0 = P.a(lambda e: e.activation(P0, P0, ACT.Exp, scale=-C), m_pi)
        for p in range(4):
            m = P.v(lambda e, p=p: e.tensor_scalar(KK[:, p, :], k[:, p, :], vec(2, p), None, ALU.mult), m_zs)
        m = P.a(lambda e: e.activation(TM, KK, ACT.Square), m)
        for hf in range(2):
            b, ps, free = banks.take()
            m2 = P.mm(ps, [(self.bones, TM[:, 2 * hf:2 * hf + 2, :])], m, free)
            sl = TM[:, 2 * hf:2 * hf + 2, :].rearrange("p a b -> p (a b)")
            m3 = P.a(lambda e, ps=ps, sl=sl: e.activation(sl, ps, ACT.Sqrt), m2)
            banks.free(b, m3)
        m3 = P.v(lambda e: e.tensor_scalar(TM, TM, 1e-12, None, ALU.max), m3)
        m3 = P.v(lambda e: e.reciprocal(TM, TM), m3)
        m_kk = P.v(lambda e: e.tensor_tensor(KK, KK, TM, ALU.mult), m3)
        for p in range(4):
            m = P.v(lambda e, p=p: e.tensor_scalar(TM[:, p, :], AA[:, p, :], -1.0, vec(3, p), ALU.add, ALU.mult), m_kk, ms[-1])
        m_k = P.v(lambda e: e.scalar_tensor_tensor(k, TM, 1.0, k, ALU.add, ALU.mult), m)
        QR = QRf.rearrange("p (a c w t) -> p a c w t", a=4, c=4, w=2)
        c4 = lambda a, p: a[:, p, :].rearrange("p (c t) -> p c t", c=4)
        fence_h = P.last("t")
        for p in range(4):
            P.v(lambda e, p=p: e.tensor_tensor(QR[:, p, :, 0, :], c4(KK, p), c4(P1, p), ALU.mult), m_p1, fence_h)
            m_qr = P.v(lambda e, p=p: e.tensor_tensor(QR[:, p, :, 1, :], c4(r, p), c4(P0, p), ALU.mult), m_p0)
        PE_ = A.take(4, 4)
        m_pe = P.v(lambda e: e.tensor_copy(PE_, P0.rearrange("p a (c t) -> p a c t", c=4)[:, :, :, 63]), m_p0)
        m = P.v(lambda e: e.tensor_tensor(BT, KK, AA, ALU.mult), m_kk)
        m_bt = P.v(lambda e: e.tensor_tensor(BT, BT, PI, ALU.mult), m, m_pi)
        m_kt = P.v(lambda e: e.tensor_tensor(KT_, k, PI, ALU.mult), m_k)
        for p in range(4):
            m = P.v(lambda e, p=p: e.scalar_tensor_tensor(TM[:, p, :], r[:, p, :], vec(4, p), k[:, p, :], ALU.mult, ALU.mult), m_k)
        for hf in range(2):
            b, ps, free = banks.take()
            m2 = P.mm(ps, [(self.bones, TM[:, 2 * hf:2 * hf + 2, :])], m, free)
            m3 = P.v(lambda e, ps=ps, hf=hf: e.tensor_tensor(BON[:, 2 * hf:2 * hf + 2, :].rearrange("p a b -> p (a b)"), ps,
                                                             v[:, 2 * hf:2 * hf + 2, :].rearrange("p a b -> p (a b)"), ALU.mult), m2)
            banks.free(b, m3)
        H = [slice(0, 64), slice(64, 128)]

        def each(out, lhs, rhs, marks, width=64):
            for p in range(4):
                for h in H:
                    m = P.t(lambda e, p=p, h=h: e.matmul(out[h, p, :], lhs(h, p), rhs(h, p), start=True, stop=True, skip_group_check=True),
                            *(marks if p == 0 and h is H[0] else ()), inc=p == 3 and h is H[1])
            return m

        def product(lhs, rhs, marks, use):
            last = []
            for c0 in (0, 2):
                b, ps, free = banks.take()
                pv = ps.rearrange("p (c a b) -> p c a b", c=2, a=4)
                for c in range(2):
                    m = each(pv[:, c, :, :], lambda h, p, c=c0 + c: lhs(h, c, p), lambda h, p, c=c0 + c: rhs(h, c, p),
                             tuple(marks) + (free,))
                mm_ = use(c0, ps, m)
                banks.free(b, mm_[-1])
                last += mm_
            return last

        four = lambda a: a.rearrange("p (c a b) -> p c a b", c=4, a=4)
        half = lambda a, c0: a[:, 256 * c0:256 * c0 + 512]
        m_rows = []
        flat = lambda a: a.rearrange("p a b -> p (a b)")
        for src, out, mk_ in ((BT, flat(BR), m_bt), (KT_, flat(KR), m_kt), (v, flat(VR), m_zs)):
            m_rows += product(lambda h, c, p, src=src: src[h, p, 64 * c:64 * c + 64], lambda h, c, p: self.ident[h, h], [mk_],
                              lambda c0, ps, m, out=out: [self.evac("a", half(out, c0), ps, m)])
        P.fence()
        GB = gbuf[0].tensor[:, self.off(gbuf[0]):self.off(gbuf[0]) + 2048].rearrange("p (c a w t) -> p c a w t", c=4, a=4, w=2)
        GK = gbuf[0].tensor[:, self.off(gbuf[2]):self.off(gbuf[2]) + 2048].rearrange("p (c a w t) -> p c a w t", c=4, a=4, w=2)
        m_g = []
        for src, out in ((BT, GB), (KT_, GK)):
            for c in range(4):
                b, ps, free = banks.take()
                m = each(ps.rearrange("p (a b) -> p a b", a=4), lambda h, p, src=src, c=c: src[h, p, 64 * c:64 * c + 64],
                         lambda h, p, c=c: QR[h, p, c, :, :].rearrange("p a b -> p (a b)"), (free,))
                m = P.v(lambda e, ps=ps, out=out, c=c: e.tensor_tensor(
                    out[:, c, :, :, :].rearrange("p a w t -> p a (w t)"), ps.rearrange("p (a b) -> p a b", a=4),
                    wm[:, 0:2, :].rearrange("p a b -> p (a b)").unsqueeze(1).broadcast_to([128, 4, 128]), ALU.mult), m)
                banks.free(b, m)
                m_g.append(m)
        mask = lambda i: wm[:, i, :].unsqueeze(1).broadcast_to([128, 8, 64])
        e8 = lambda a: a.rearrange("p (a b) -> p a b", a=8)
        Ld, LdT, Lo, A2, A2T, ZT = buf

        def tiles(a):
            v4 = four(a)
            return lambda h, c, p: v4[h, c, p, :]

        m_l = product(lambda h, c, p: QR[h, p, c, 0, :], lambda h, c, p: BT[h, p, 64 * c:64 * c + 64], [],
                      lambda c0, ps, m: [P.v(lambda e: e.tensor_tensor(e8(half(Ld, c0)), e8(ps), mask(2), ALU.mult), m),
                                         P.v(lambda e: e.tensor_tensor(e8(half(Lo, c0)), e8(ps), mask(3), ALU.mult), m)])
        m_t = []
        for c in range(4):
            m = P.v(lambda e, c=c: e.tensor_tensor(four(LdT)[:, c, :, :], GB[:, c, :, 0, :],
                                                   wm[:, 5, :].unsqueeze(1).broadcast_to([128, 4, 64]), ALU.mult), *m_g)
            m_t.append(P.v(lambda e, c=c: e.tensor_tensor(four(ZT)[:, c, :, :], wm[:, 4, :].unsqueeze(1).broadcast_to([128, 4, 64]),
                                                          four(LdT)[:, c, :, :], ALU.subtract), m))

        def copy(out, k="a"):
            return lambda c0, ps, m: [self.evac(k, half(out, c0), ps, m)]

        def plus(out, base):
            return lambda c0, ps, m: [P.v(lambda e: e.tensor_tensor(half(out, c0), ps, half(base, c0), ALU.add), m)]

        mA2 = product(tiles(LdT), tiles(Ld), m_l + m_t, copy(A2))
        mA2T = product(tiles(Ld), tiles(LdT), [], copy(A2T, "v"))
        both = mA2 + mA2T
        mZ = product(tiles(A2), tiles(ZT), both, plus(ZT, ZT))
        A4, A4T = Ld, LdT
        mA4 = product(tiles(A2T), tiles(A2), both, copy(A4))
        mA4T = product(tiles(A2), tiles(A2T), [], copy(A4T))
        mZ = product(tiles(A4), tiles(ZT), mZ + mA4, plus(ZT, ZT))
        A8 = A2T
        mA8 = product(tiles(A4T), tiles(A4), mA4T, copy(A8))
        mZ = product(tiles(A8), tiles(ZT), mZ + mA8, plus(ZT, ZT))
        XX, F, FT, F2, T1, INV = Ld, LdT, A2, A2T, Lo, buf[1]
        mX = product(tiles(ZT), lambda h, c, p: self.ident[h, h], mZ, copy(XX))
        mF = product(tiles(ZT), tiles(Lo), mZ, copy(F))
        mFT = product(tiles(Lo), tiles(ZT), mZ, copy(FT, "v"))
        mF2 = product(tiles(FT), tiles(F), mF + mFT, copy(F2))
        mT = P.v(lambda e: e.tensor_tensor(T1.rearrange("p (a b) -> p a b", a=16), wm[:, 4, :].unsqueeze(1).broadcast_to([128, 16, 64]),
                                           FT.rearrange("p (a b) -> p a b", a=16), ALU.subtract), *(mF2 + mFT))
        mT = product(tiles(F2), tiles(T1), mF2 + [mT], plus(T1, T1))
        m_inv = product(tiles(XX), tiles(T1), mT + mX, copy(INV))
        INV4, BR4, KR4, VR4 = four(INV), four(flat(BR)), four(flat(KR)), four(flat(VR))
        YT = t4(buf[0])
        P.fence()
        m_s = None
        m_ub = m_sa = None
        for c in range(4):
            def group(out, terms, marks):
                for p in range(4):
                    for h in H:
                        for i, (l, q) in enumerate(terms):
                            m = P.t(lambda e, p=p, h=h, l=l, q=q, i=i: e.matmul(out[h, p, :], l(h, p), q(h, p), start=i == 0,
                                                                                stop=i == len(terms) - 1, skip_group_check=True),
                                    *(marks if p == 0 and h is H[0] and i == 0 else ()),
                                    inc=p == 3 and h is H[1] and i == len(terms) - 1)
                return m

            def bank():
                b, ps, free = banks.take()
                return b, ps[:, 0:256].rearrange("p (a b) -> p a b", a=4), free

            b, ps, free = bank()
            terms = [(lambda h, p, c=c: GK[h, c, p, 0, :], lambda h, p, c=c: VR4[h, c, p, :])]
            if c:
                terms.append((lambda h, p, c=c: QR[h, p, c, 0, :], lambda h, p: S[h, p, :]))
            m = group(ps, terms, (free, m_s))
            m_ub = P.v(lambda e, ps=ps: e.tensor_copy(UB, ps), m, m_sa)
            banks.free(b, m_ub)
            b, ps, free = bank()
            m = group(ps, [(lambda h, p, c=c: INV4[h, c, p, :], lambda h, p: UB[h, p, :])], (free, m_ub))
            m_sa = P.v(lambda e, ps=ps: e.tensor_scalar(SA, ps, -1.0, None, ALU.mult), m, P.last("t"))
            banks.free(b, m_sa)
            b, ps, free = bank()
            terms = [(lambda h, p: SA[h, p, :], lambda h, p, c=c: GB[h, c, p, 1, :]),
                     (lambda h, p, c=c: VR4[h, c, p, :], lambda h, p, c=c: GK[h, c, p, 1, :])]
            if c:
                terms.append((lambda h, p: S[h, p, :], lambda h, p, c=c: QR[h, p, c, 1, :]))
            m_y = group(ps, terms, (free, m_sa))
            m = P.a(lambda e, ps=ps, c=c: e.activation(YT[:, :, 64 * c:64 * c + 64], ps, ACT.Copy), m_y)
            banks.free(b, m)
            if c < 3:
                b, ps, free = bank()
                m = group(ps, [(lambda h, p, c=c: BR4[h, c, p, :], lambda h, p: SA[h, p, :]),
                               (lambda h, p, c=c: KR4[h, c, p, :], lambda h, p, c=c: VR4[h, c, p, :])], (free,))
                if c:
                    m = P.v(lambda e, ps=ps: e.tensor_tensor(S, S, ps, ALU.add), m, m_y)
                else:
                    m = P.v(lambda e, ps=ps: e.tensor_copy(S, ps), m)
                banks.free(b, m)
                m_s = P.v(lambda e, c=c: e.tensor_tensor(S, S, PE_[:, :, c].unsqueeze(2).broadcast_to([128, 4, 64]), ALU.mult), m)
        P.fence()
        YC, SQ = t4(buf[2]), t4(buf[3])
        for hf in range(2):
            yt, yc, sq = (a[:, 2 * hf:2 * hf + 2, :].rearrange("p a b -> p (a b)") for a in (YT, YC, SQ))
            b, ps, free = banks.take()
            m = P.mm(ps, [(self.bones, yt)], free)
            m1 = P.v(lambda e, ps=ps, yt=yt, yc=yc: e.scalar_tensor_tensor(yc, ps, -1.0 / 64, yt, ALU.mult, ALU.add), m)
            banks.free(b, m1)
            m2 = P.a(lambda e, sq=sq, yc=yc: e.activation(sq, yc, ACT.Square), m1)
            b, ps, free = banks.take()
            m3 = P.mm(ps, [(self.bones, sq)], m2, free)
            m4 = P.a(lambda e, ps=ps, sq=sq: e.activation(sq, ps, ACT.Sqrt, scale=1.0 / 64, bias=self.eps_ln), m3)
            banks.free(b, m4)
            m5 = P.v(lambda e, sq=sq: e.reciprocal(sq, sq), m4)
            m6 = P.v(lambda e, sq=sq, yc=yc: e.tensor_tensor(yc, yc, sq, ALU.mult), m5)
        for p in range(4):
            m = self.affine("v", YC[:, p, :], YC[:, p, :], vec(5, p), vec(6, p), m6)
            m = P.v(lambda e, p=p: e.tensor_tensor(YC[:, p, :], YC[:, p, :], BON[:, p, :], ALU.add), m)
            b, ps, free = banks.take()
            m2 = P.mm(ps[:, 0:256], [(gup[:, p * 128:(p + 1) * 128], XG)], free)
            m = P.v(lambda e, p=p, ps=ps: e.tensor_tensor(MT[:, 4 + p, :], YC[:, p, :], ps[:, 0:256], ALU.mult), m, m2)
            banks.free(b, m)
        P.fence()

    def off(self, a):
        return a.offset

    def retention_mixer(self):
        P, A, I = self.P, self.A, self.I
        at0 = A.mark()
        banks = Banks(self.ps, [0, 1, 2, 3])
        grow = A.take(D)
        stat = A.take(32)
        mg = P.dma("g", grow, I["norms_2"][1, 3:4, :].broadcast_to([128, D]))
        DC = A.take(4, 2, 256)
        m_dc = P.dma("g", DC, I["k_decay"].rearrange("p (a b c) -> p a b c", a=4, b=2))
        QK = A.take(16, 256)
        HT = A.take(8, 256)
        V, G = A.take(2, 2048), A.take(2, 2048)
        ST = A.take(2, 2, 256)
        junk = A.take(2, D)
        mh = self.pre_norm(4, banks, G[:, :, 0:1024], HT, junk, stat[:, 0:4])
        P.fence()
        banks = Banks(self.ps, list(range(8)))
        W = I["odd_w_in_2"][0]
        m_p = []
        for blk in range(4):
            s, w, mw = self.cols(W, blk * 512, 512)
            for q in range(4):
                j = 4 * blk + q
                b, ps, free = banks.take()
                m = P.mm(ps[:, 0:256], [(w[:, k, q * 128:(q + 1) * 128], HT[:, k, :]) for k in range(8)], mw, free)
                if j < 8:
                    m1 = self.evac("a", QK[:, j, :], ps[:, 0:256], m)
                else:
                    m1 = P.a(lambda e, ps=ps, j=j: e.activation(QK[:, j, :], ps[:, 0:256], ACT.Copy, scale=1.0 / 16), m)
                banks.free(b, m1)
                m_p.append(m1)
            self.R.free(s, m)
        for blk in range(8):
            s, w, mw = self.cols(W, 2048 + blk * 512, 512)
            for t in range(2):
                b, ps, free = banks.take()
                m = P.mm(ps, [(HT[:, k, t * 128:(t + 1) * 128], w[:, k, :]) for k in range(8)], mw, free)
                if blk < 4:
                    m1 = self.evac("v", V[:, t, blk * 512:blk * 512 + 512], ps, m)
                else:
                    m1 = P.a(lambda e, ps=ps, t=t, blk=blk: e.activation(G[:, t, (blk - 4) * 512:(blk - 3) * 512], ps, ACT.Silu), m)
                banks.free(b, m1)
                m_p.append(m1)
            self.R.free(s, m)
        P.fence()
        banks = Banks(self.ps, [0, 1, 2, 3])
        yb = Banks(self.ps, [4, 5, 6, 7])
        r_st = [None, None]
        for h in range(4):
            u = h % 2
            for sT in range(2):
                b, ps, free = banks.take()
                m = P.mm(ps[:, 0:256], [(QK[:, 8 + 2 * h + k, sT * 128:(sT + 1) * 128], QK[:, 2 * h + k, :]) for k in range(2)], free)
                m_st = P.v(lambda e, ps=ps, h=h, sT=sT, u=u: e.tensor_tensor(ST[:, u, sT, :], ps[:, 0:256], DC[:, h, sT, :], ALU.mult),
                           m, m_dc, r_st[u])
                banks.free(b, m_st)
            for t in range(2):
                b, ps, free = yb.take()
                m = P.mm(ps, [(ST[:, u, sT, t * 128:(t + 1) * 128], V[:, sT, h * 512:(h + 1) * 512]) for sT in range(t + 1)], m_st, free)
                if t == 1:
                    r_st[u] = m
                st = stat[:, 8 + 2 * h + t:9 + 2 * h + t]
                m = P.a(lambda e, ps=ps, st=st, t=t: e.activation(junk[:, t, 0:512], ps, ACT.Square, accum_out=st), m, P.last("a"))
                m = self.rstd(st, st, 512, self.eps, m)
                g = G[:, t, h * 512:(h + 1) * 512]
                m = P.v(lambda e, ps=ps, st=st, g=g: e.scalar_tensor_tensor(g, ps, st, g, ALU.mult, ALU.mult), m)
                yb.free(b, m)
        P.fence()
        self.to_columns([G[:, 0, :], G[:, 1, :]], QK, 0, None, None, banks, [])
        P.fence()
        Y = self.ps[:, 4:8, :]
        for k0 in range(0, 16, 4):
            s, w, mw = self.rows(I["odd_w_out_2"][0], k0, 4)
            for k in range(4):
                for t in range(2):
                    for hf in range(2):
                        m = P.mm(Y[:, 2 * t + hf, :], [(QK[:, k0 + k, t * 128:(t + 1) * 128], w[:, k, hf * 512:(hf + 1) * 512])],
                                 mw, start=k0 + k == 0, stop=k0 + k == 15)
            self.R.free(s, m)
        self.post_norm_add(Y, 1, 3, 1.0, junk, stat[:, 4:8], [m], grow, mg)
        A.back(at0)

    def stages(self):
        return [lambda: self.adaln(0), self.even_mixer, lambda: self.moe(0), lambda: self.adaln(1), self.pool_mixer,
                lambda: self.moe(1), self.final_norm, self.second_block_memory, lambda: self.ffn(0, 0), self.diff_rwkv_mixer,
                lambda: self.ffn(0, 1), lambda: self.ffn(1, 0), self.retention_mixer, lambda: self.ffn(1, 1)]

    def program(self):
        P = self.P
        self.load_constants()
        for stage in self.stages():
            stage()
        self.write_out()

    def write_out(self):
        P = self.P
        m = [P.last(k) for k in "tvag"]
        marks = [P.dma("s", self.out[0, t * 128:(t + 1) * 128, :], self.X[:, t, :], *m) for t in range(2)]
        P.queues["s"].append((marks, None, None))

    def finish(self, ctx):
        P = self.P
        block = ctx.enter_context(self.nc.Block())

        @block.sync
        def _(e):
            P.emit("s", e)

        @block.tensor
        def _(e):
            P.emit("t", e)

        @block.vector
        def _(e):
            P.emit("v", e)

        @block.scalar
        def _(e):
            P.emit("a", e)

        @block.gpsimd
        def _(e):
            P.emit("g", e)


def build_program(nc, I, out):
    with ExitStack() as ctx:
        k = Kernel(nc, ctx, I, out)
        k.program()
        k.finish(ctx)


_BIG = ["x", "ctx", "w_mod", "b_mod", "w_in_even", "w_out_even", "g_qnorm", "g_knorm", "g_hnorm", "w_in_odd", "w_pool_grp",
        "s_pool", "w_router", "w_exp_gate", "w_exp_up", "w_exp_down", "g_final", "norms_2", "ffn_wgu_2", "ffn_wd_2",
        "even_w_in_2", "even_w_out_2", "diff_lam_2", "diff_subln_2", "rwkv_w_up_2", "rwkv_a_up_2", "rwkv_g_up_2",
        "odd_w_in_2", "odd_w_out_2"]


def _pack_columns(inp):
    a = {k: np.asarray(inp[k]) for k in ("c", "c_ctx", "g_norm1", "g_norm2", "b_mod", "norms_2", "w_conv", "b_gate",
                                         "rwkv_mu_2", "rwkv_vec_2")}
    cc = np.stack([a["c"].reshape(8, 128).T, a["c_ctx"].reshape(8, 128).T], 2).reshape(128, 16)
    g1 = a["g_norm1"].reshape(16, 128).T
    g2 = a["g_norm2"].reshape(16, 128).T
    bm = a["b_mod"].reshape(2, 6, 8, 128)[:, [0, 1, 3, 4]].reshape(64, 128).T
    nrm = a["norms_2"].reshape(2, 6, 8, 128)[:, [0, 2, 4]].reshape(48, 128).T
    conv = a["w_conv"].reshape(24, 128).T
    bgate = np.pad(a["b_gate"].reshape(16, 1), ((0, 112), (0, 0)))
    mu = a["rwkv_mu_2"].reshape(14, 128).T
    vec = a["rwkv_vec_2"].reshape(28, 128).T
    return np.ascontiguousarray(np.concatenate([cc, g1, g2, bm, nrm, conv, bgate, mu, vec], 1))


def kernel(**inputs):
    import concourse.bacc as bacc
    from concourse.bass_utils import run_bass_kernel_spmd

    nc = bacc.Bacc("TRN2", target_bir_lowering=False, num_devices=1)
    arrays = {n: np.ascontiguousarray(inputs[n]) for n in _BIG}
    arrays["vc"] = _pack_columns(inputs)
    for n, a in shape_constants().items():
        arrays["k_" + n] = a
    aps = {}
    for n, a in arrays.items():
        aps[n] = nc.dram_tensor("in_" + n, a.shape, mybir.dt.from_np(a.dtype), kind="ExternalInput").ap()
    out = nc.dram_tensor("out_x", (1, T, D), F32, kind="ExternalOutput").ap()
    build_program(nc, aps, out)
    r = run_bass_kernel_spmd(nc, [{"in_" + n: a for n, a in arrays.items()}], core_ids=[0])
    return r.results[0]["out_x"]
```

```python
from contextlib import ExitStack

import numpy as np
import concourse.bass as bass
from concourse import mybir

F32 = mybir.dt.float32
U32 = mybir.dt.uint32
ALU = mybir.AluOpType
ACT = mybir.ActivationFunctionType
AX = mybir.AxisListType.X

D = 1024
T = 256
EPS = 1e-6
NSLOT = 6
SLOT = 4096
NEG = 1e30
A_COLS = 1536
ZB = 1792
D_FF = 2816
WINDOWS = (2, 4, 8, 16)
LAM0 = 0.8 - 0.6


def column_table():
    at, n = {}, 0
    for name, k in (("cc", 16), ("g1", 16), ("g2", 16), ("bm", 96), ("nrm", 48), ("conv", 24), ("bgate", 1),
                    ("mu", 14), ("vec", 28)):
        at[name] = n
        n += k
    return at, n


def shape_constants():
    f = np.float32
    cst = {}
    p = np.arange(128)
    base = np.zeros((128, 1024), f)
    base[:, 0:128] = np.eye(128, dtype=f)
    base[:, 128:384] = np.arange(256, dtype=f)[None, :]
    base[:, 384] = p
    base[:, 385] = p + 128
    base[:, 386] = EPS
    base[:, 387] = 64e-5
    base[:, 388] = 1.0
    base[:, 400:528] = (p[:, None] // 64 == p[None, :] // 64)
    base[:, 528:656] = np.eye(128, dtype=f)[:, ::-1]
    base[:, 656:784] = 1.0
    cst["base"] = base
    rows = (np.arange(256) // 64).astype(f)
    cols = (np.arange(256) % 64).astype(f)
    inv = (10000.0 ** (-np.arange(0, 32, 2, dtype=f) / f(32))).astype(f)
    ang = np.stack([rows[:, None] * inv, cols[:, None] * inv], 1).astype(f)
    c, s = np.cos(ang).astype(f), np.sin(ang).astype(f)
    cs = np.zeros((2, 256, 2, 2, 16), f)
    cs[0] = c[:, :, None, :]
    cs[1, :, :, 0] = -s
    cs[1, :, :, 1] = s
    cst["rope"] = cs.reshape(2, 2, 128, 64).transpose(2, 0, 1, 3).reshape(128, 256).copy()
    ml = np.zeros((128, 2, 128), f)
    ml[:, 0] = np.where(p[:, None] <= p[None, :], 0.0, NEG)
    ml[:, 1] = np.where(p[:, None] >= p[None, :], 0.0, NEG)
    cst["mmask"] = ml.reshape(128, 256)
    sel = np.zeros((128, 10, 128), f)
    for d in range(2):
        for h in range(4):
            sel[8 * d + h, 8, 32 * d + h] = 1.0
            sel[8 * d + 4 + h, 9, 32 * d + h] = 1.0
            sel[32 * d + h, 4 * d + h, :] = 1.0
    cst["sel"] = sel.reshape(128, 1280)
    band = np.zeros((4, 256, 256), f)
    t = np.arange(256)
    for g, w in enumerate(WINDOWS):
        lo, hi = w // 2, w - 1 - w // 2
        a, e = np.clip(t - lo, 0, 255), np.clip(t + hi, 0, 255)
        inside = (t[:, None] >= a[None, :]) & (t[:, None] <= e[None, :])
        band[g] = inside / (e - a + 1).astype(f)[None, :] - np.eye(256, dtype=f)
    cst["band"] = band.reshape(4, 2, 128, 256).transpose(2, 0, 1, 3).reshape(128, 2048).copy()
    slopes = 2.0 ** (-2.0 * np.arange(1, 5))
    allowed = (t[None, :] // 64) <= (t[:, None] // 64)
    bias = np.where(allowed[None], -slopes[:, None, None] * np.abs(t[:, None] - t[None, :])[None], -NEG).astype(f)
    cst["dbias"] = np.concatenate([bias[:, 0:128, 0:128], bias[:, 128:256, :]], 2).transpose(1, 0, 2).reshape(128, 1536).copy()
    logg = np.log(1.0 - 2.0 ** (-5.0 - np.arange(4)))
    dist = np.abs(t[:, None] - t[None, :])
    dec = np.where(allowed[None], np.exp(logg[:, None, None] * dist[None]), 0.0).astype(f)
    cst["decay"] = dec.transpose(0, 2, 1).reshape(4, 2, 128, 256).transpose(2, 0, 1, 3).reshape(128, 2048).copy()
    q = np.arange(128) % 64
    u = np.arange(64)
    wm = np.zeros((128, 5, 64), f)
    wm[:, 0] = q[:, None] < u[None, :]
    wm[:, 1] = q[:, None] <= u[None, :]
    wm[:, 2] = (q[:, None] > u[None, :]) & (q[:, None] // 16 == u[None, :] // 16)
    wm[:, 3] = (q[:, None] // 16) > (u[None, :] // 16)
    wm[:, 4] = q[:, None] == u[None, :]
    blk = np.zeros((128, 1, 64), f)
    blk[:, 0] = (q[:, None] // 16) == (u[None, :] // 16)
    cst["wmask"] = np.concatenate([wm, blk], 1).reshape(128, 384).copy()
    return cst


CONST_NAMES = ["base", "rope", "mmask", "sel", "band", "dbias", "decay", "wmask"]


class Program:

    def __init__(self, nc, ctx):
        self.nc = nc
        self.queues = {k: [] for k in "tvags"}
        self.sems = {k: ctx.enter_context(nc.semaphore("done_" + k)) for k in "tvag"}
        self.count = {k: 0 for k in "tvag"}
        self.small = {k: [ctx.enter_context(nc.semaphore(f"small_{k}{i}")) for i in range(12)] for k in "gsa"}
        self.small_used = {k: [0] * 12 for k in "gsa"}
        self.small_n = {k: 0 for k in "gsa"}

    def put(self, k, fn, after, inc=True):
        after = [m for m in after if m is not None]
        if inc:
            self.count[k] += 1
            self.queues[k].append((after, fn, (self.sems[k], 1)))
            return (self.sems[k], self.count[k])
        self.queues[k].append((after, fn, None))
        return None

    def t(self, fn, *after, inc=True):
        return self.put("t", fn, after, inc)

    def v(self, fn, *after):
        return self.put("v", fn, after)

    def a(self, fn, *after):
        return self.put("a", fn, after)

    def g(self, fn, *after):
        return self.put("g", fn, after)

    def mm(self, out, pairs, *after, start=True, stop=True):
        n = len(pairs)
        mark = None
        for i, (l, r) in enumerate(pairs):
            mark = self.t(lambda e, o=out, l=l, r=r, s=start and i == 0, q=stop and i == n - 1:
                          e.matmul(o, l, r, start=s, stop=q, skip_group_check=True),
                          *(after if i == 0 else ()), inc=i == n - 1)
        return mark

    def tr(self, out, src, ident, *after, inc=True):
        return self.t(lambda e: e.transpose(out, src, ident), *after, inc=inc)

    def dma(self, k, out, src, *after, **kw):
        sems, used = self.small[k], self.small_used[k]
        i = self.small_n[k] % len(sems)
        self.small_n[k] += 1
        before = (sems[i], 16 * used[i]) if used[i] else None
        used[i] += 1
        after = [m for m in list(after) + [before] if m is not None]
        self.queues[k].append((after, lambda e: e.dma_start(out, src, **kw), (sems[i], 16)))
        return (sems[i], 16 * used[i])

    def last(self, k):
        return (self.sems[k], self.count[k]) if self.count[k] else None

    def fence(self):
        marks = [self.last(k) for k in "tvag"] + [(self.small[k][i], 16 * n) for k in "gsa"
                                                   for i, n in enumerate(self.small_used[k]) if n]
        for k in "tvag":
            self.queues[k].append(([m for m in marks if m is not None], None, None))

    def emit(self, k, eng):
        seen = {}
        for after, fn, inc in self.queues[k]:
            need = {}
            for sem, n in after:
                if n > seen.get(sem.num, 0):
                    need[sem.num] = (sem, max(n, need.get(sem.num, (sem, 0))[1]))
            for num, (sem, n) in need.items():
                eng.wait_ge(sem, n)
                seen[num] = n
            if fn is not None:
                ins = fn(eng)
                if inc is not None:
                    ins.then_inc(*inc)


class Banks:

    def __init__(self, ps, ids):
        self.ps, self.ids, self.n = ps, ids, 0
        self.freed = {i: None for i in ids}

    def take(self):
        i = self.ids[self.n % len(self.ids)]
        self.n += 1
        return i, self.ps[:, i, :], self.freed[i]

    def free(self, i, mark):
        self.freed[i] = mark


class Ring:

    def __init__(self, P, tile, ctx):
        self.P, self.tile = P, tile
        self.sems = [ctx.enter_context(P.nc.semaphore(f"slot{i}")) for i in range(NSLOT)]
        self.fills = [0] * NSLOT
        self.freed = [[] for _ in range(NSLOT)]
        self.order = list(range(NSLOT))

    def load(self, *pieces):
        i = self.order.pop(0)
        self.order.append(i)
        for k, (view, src) in enumerate(pieces):
            self.P.queues["s"].append((self.freed[i] if k == 0 else [],
                                       lambda e, o=view(self.tile[:, i, :]), s=src: e.dma_start(o, s),
                                       (self.sems[i], 16)))
            self.fills[i] += 16
        return i, self.tile[:, i, :], (self.sems[i], self.fills[i])

    def free(self, i, mark):
        self.freed[i] = [mark]

    def lend(self, n):
        self.order = [i for i in self.order if i < NSLOT - n]
        marks = [m for i in range(NSLOT - n, NSLOT) for m in self.freed[i]]
        return self.tile[:, NSLOT - n:NSLOT, :].rearrange("p a b -> p (a b)"), marks

    def restore(self):
        marks = [m for m in (self.P.last(k) for k in "tvag") if m]
        for i in range(NSLOT):
            if i not in self.order:
                self.freed[i] = marks
                self.order.append(i)


def interleave(*gens):
    gens = list(gens)
    while gens:
        for g in list(gens):
            try:
                next(g)
            except StopIteration:
                gens.remove(g)


class Arena:
    def __init__(self, tile, n):
        self.tile, self.n, self.at = tile, n, 0
        self.extra, self.at_extra = None, 0

    def take(self, *shape):
        n = int(np.prod(shape))
        if self.extra is not None and self.at_extra + n <= self.extra.shape[1]:
            a = self.extra[:, self.at_extra:self.at_extra + n]
            self.at_extra += n
            return self.shaped(a, shape)
        a = self.tile[:, self.at:self.at + n]
        self.at += n
        assert self.at <= self.n, (self.at, self.n)
        return self.shaped(a, shape)

    def shaped(self, a, shape):
        if len(shape) == 2:
            a = a.rearrange("p (a b) -> p a b", a=shape[0])
        elif len(shape) == 3:
            a = a.rearrange("p (a b c) -> p a b c", a=shape[0], b=shape[1])
        elif len(shape) == 4:
            a = a.rearrange("p (a b c d) -> p a b c d", a=shape[0], b=shape[1], c=shape[2])
        return a

    def borrow(self, extra):
        self.extra, self.at_extra = extra, 0

    def mark(self):
        return self.at

    def back(self, at):
        self.at = at


class Kernel:
    def __init__(self, nc, ctx, I, out):
        self.nc, self.I, self.out = nc, I, out
        self.P = Program(nc, ctx)
        total = 53200
        big = ctx.enter_context(nc.sbuf_tensor("big", [128, total], F32))
        self.ps = ctx.enter_context(nc.psum_tensor("ps", [128, 8, 512], F32))
        self.R = Ring(self.P, big[:, 0:NSLOT * SLOT].rearrange("p (a b) -> p a b", a=NSLOT), ctx)
        self.A = Arena(big, total)
        self.A.take(NSLOT * SLOT)

    def evac(self, k, out, src, *after):
        if k == "v":
            return self.P.v(lambda e: e.tensor_copy(out, src), *after)
        return self.P.a(lambda e: e.activation(out, src, ACT.Copy), *after)

    def affine(self, k, out, src, scale, bias, *after):
        if k == "v":
            if bias is None:
                return self.P.v(lambda e: e.tensor_scalar(out, src, scale, None, ALU.mult), *after)
            return self.P.v(lambda e: e.tensor_scalar(out, src, scale, bias, ALU.mult, ALU.add), *after)
        if bias is None:
            return self.P.a(lambda e: e.activation(out, src, ACT.Copy, scale=scale), *after)
        return self.P.a(lambda e: e.activation(out, src, ACT.Identity, scale=scale, bias=bias), *after)

    def rstd(self, out, sums, n, eps, *after):
        m = self.P.a(lambda e: e.activation(out, sums, ACT.Sqrt, scale=1.0 / n, bias=eps), *after)
        return self.P.v(lambda e: e.reciprocal(out, out), m)

    def rms_rows(self, srcs, outs, junk, stat, after):
        P = self.P
        marks = []
        n = len(srcs)
        for i, (s, j) in enumerate(zip(srcs, junk)):
            marks.append(P.a(lambda e, s=s, j=j, i=i: e.activation(j, s, ACT.Square, accum_out=stat[:, i:i + 1]),
                             *after[i]))
        m = self.rstd(stat[:, n:2 * n], stat[:, 0:n], D, self.eps, *marks)
        return [P.v(lambda e, s=s, o=o, i=i: e.tensor_scalar(o, s, stat[:, n + i:n + i + 1], None, ALU.mult), m)
                for i, (s, o) in enumerate(zip(srcs, outs))]

    def to_columns(self, rows, dst, off, scale, bias, banks, after):
        P = self.P
        marks = []
        nk = dst.shape[1]
        for kc in range(0, nk, 2):
            b, ps, free = banks.take()
            for u in range(2):
                for tt in range(2):
                    m = P.tr(ps[:, (2 * u + tt) * 128:(2 * u + tt + 1) * 128],
                             rows[tt][:, (kc + u) * 128:(kc + u + 1) * 128], self.ident, free, *after,
                             inc=(u == 1 and tt == 1))
            ms = []
            if scale is None:
                ms.append(self.evac("va"[kc // 2 % 2], dst[:, kc:kc + 2, off:off + 256],
                                    ps.rearrange("p (a b) -> p a b", a=2), m))
            else:
                for u in range(2):
                    ms.append(self.affine("va"[kc // 2 % 2], dst[:, kc + u, off:off + 256],
                                          ps[:, u * 256:(u + 1) * 256], scale(kc + u),
                                          None if bias is None else bias(kc + u), m))
            banks.free(b, ms[-1])
            marks += ms
        return marks

    def cols(self, W, c0, n):
        view = lambda s: s[:, 0:8 * n].rearrange("p (k n) -> p k n", k=8)
        i, s, m = self.R.load((view, W[0:1024, c0:c0 + n].rearrange("(k p) n -> p k n", p=128)))
        return i, view(s), m

    def rows(self, W, k0, nk):
        view = lambda s: s[:, 0:nk * 1024].rearrange("p (k n) -> p k n", k=nk)
        i, s, m = self.R.load((view, W[k0 * 128:(k0 + nk) * 128, 0:1024].rearrange("(k p) n -> p k n", p=128)))
        return i, view(s), m

    def load_constants(self):
        P, A, I = self.P, self.A, self.I
        self.X = A.take(2, D)
        base = A.take(1024)
        self.col_at, ncol = column_table()
        self.vc = A.take(ncol)
        m = [P.dma("s", self.vc, I["vc"]), P.dma("s", base, I["k_base"])]
        self.m_x = [P.dma("a", self.X[:, i, :], I["x"][0, i * 128:(i + 1) * 128, :]) for i in range(2)]
        self.ident = base[:, 0:128]
        self.iota = base[:, 128:384]
        self.iota_p = [base[:, 384:385], base[:, 385:386]]
        self.eps = base[:, 386:387]
        self.eps_ln = base[:, 387:388]
        self.onecol = base[:, 388:389]
        self.bones = base[:, 400:528]
        self.ones = base[:, 656:784]
        self.keep = A.mark()
        self.gate = A.take(2, D)
        self.colm = [A.take(48, 2) for _ in range(2)]
        self.AC = [A.take(2, 8, 2) for _ in range(2)]
        self.PR = A.take(2, 512)
        self.sc = A.take(8, 32)
        for k in "tvag":
            P.queues[k].append((m, None, None))
        m = P.v(lambda e: e.memset(self.sc, 0.0))
        self.m_sc = P.a(lambda e: e.activation(self.sc[:, :, 0:2], self.col("cc", 16).rearrange("p (k t) -> p k t", t=2), ACT.Silu), m)
        self.mod_bank = Banks(self.ps, [7])
        self.mod_rows = [None, None]
        self.mod_n = 0
        self.mod_work = []

    def col(self, name, n, off=0):
        a = self.col_at[name] + off
        return self.vc[:, a:a + n]

    def adaln_block(self, i, blk):
        P, I = self.P, self.I
        s, w, mw = self.cols(I["w_mod"][i], blk * 512, 512)
        b, ps, free = self.mod_bank.take()
        for g in range(2):
            for j in range(4):
                k = 4 * g + j
                m = P.t(lambda e, j=j, k=k, g=g, w=w, ps=ps: e.matmul(ps[32 * j:32 * j + 32, :], self.sc[:, k, :], w[:, k, :], start=g == 0,
                                                                      stop=g == 1, skip_group_check=True),
                        *((mw, free, self.m_sc) if k == 0 else ()), inc=k == 7)
        self.R.free(s, m)
        u = self.mod_n % 2
        self.mod_n += 1
        row = self.PR[:, u, :]
        m = P.v(lambda e, ps=ps, row=row: e.tensor_copy(row, ps), m, self.mod_rows[u])
        for q in range(4):
            mt = P.tr(ps[:, 128 * q:128 * q + 128], row[:, 128 * q:128 * q + 128], self.ident, m, inc=q == 3)
        self.mod_rows[u] = mt
        out = self.colm[i][:, 4 * blk:4 * blk + 4, :]
        view = ps.rearrange("p (q j t) -> p q t j", q=4, j=4)[:, :, 0:2, :]
        m = P.v(lambda e, out=out, view=view: e.tensor_reduce(out, view, AX, ALU.add), mt)
        self.mod_bank.free(b, m)
        bias = self.col("bm", 4, 48 * i + 4 * blk).unsqueeze(2).broadcast_to([128, 4, 2])
        return P.v(lambda e, out=out, bias=bias: e.tensor_tensor(out, out, bias, ALU.add), m)

    def norm_columns(self, i, w, marks):
        P = self.P
        c = self.colm[i]
        g = self.col("g1" if w == 0 else "g2", 8, 8 * i).unsqueeze(2).broadcast_to([128, 8, 2])
        m = P.v(lambda e: e.scalar_tensor_tensor(self.AC[i][:, w, :, :], c[:, 24 * w + 8:24 * w + 16, :], 1.0, g, ALU.add, ALU.mult),
                *marks)
        return [m]

    def gate_rows(self, i, which, banks, marks):
        P = self.P
        for hf in range(2):
            b, ps, free = banks.take()
            for q in range(4):
                t = 24 * which + 16 + 4 * hf + q
                m = P.mm(ps[:, 128 * q:128 * q + 128], [(self.colm[i][:, t, 0:1].broadcast_to([128, 128]), self.ident)], free, *marks)
            m = self.evac("av"[hf], self.gate[:, which, 512 * hf:512 * hf + 512], ps, m)
            banks.free(b, m)

    def set_layer(self, i):
        self.layer = i
        self.B = lambda w, kc, t: self.colm[i][:, 24 * w + kc, t:t + 1]
        self.Ac = lambda w, kc, t: self.AC[i][:, w, kc, t:t + 1]

    def first_columns(self):
        for blk in range(4):
            m = self.adaln_block(0, blk)
        self.m_mod = self.norm_columns(0, 0, [m])
        self.set_layer(0)
        self.mod_work = [(0, b) for b in range(4, 12)] + [(1, b) for b in range(12)]

    def fill(self, n=1):
        for _ in range(n):
            if self.mod_work:
                self.adaln_block(*self.mod_work.pop(0))

    def even_mixer(self):
        P, A, I = self.P, self.A, self.I
        banks = Banks(self.ps, [0, 1, 2, 3, 4, 5])
        at0 = A.mark()
        stat = A.take(96)
        rope = A.take(2, 2, 64)
        mmask = A.take(2, 128)
        sel = A.take(10, 128)
        grow = A.take(2, 64)
        ghn = A.take(512)
        m_c = [P.dma("a", rope, I["k_rope"].rearrange("p (a b c) -> p a b c", a=2, b=2)),
               P.dma("a", mmask, I["k_mmask"].rearrange("p (a b) -> p a b", a=2)),
               P.dma("a", sel, I["k_sel"].rearrange("p (a b) -> p a b", a=10)),
               P.dma("a", grow[:, 0, :], I["g_qnorm"][0:1, :].broadcast_to([128, 64])),
               P.dma("a", grow[:, 1, :], I["g_knorm"][0:1, :].broadcast_to([128, 64])),
               P.dma("a", ghn, I["g_hnorm"][0:1, :].broadcast_to([128, 512]))]
        for k in "tvag":
            P.queues[k].append((m_c, None, None))
        QK = A.take(8, 512)
        V1 = A.take(4, 4, 129)
        OB = A.take(2, 512)
        QA = A.take(2, 512)
        KA = A.take(4, 2, 2, 64)
        VA = A.take(4, 128)
        G16 = A.take(512)
        at1 = A.mark()
        HT = A.take(8, 512)
        at2 = A.mark()
        XN = A.take(2, D)
        CTX = A.take(2, D)
        junk = QK[:, 0:4, :].rearrange("p (a b) c -> p a (b c)", a=2)
        m_ctx = [P.dma("a", CTX[:, i, :], I["ctx"][0, i * 128:(i + 1) * 128, :]) for i in range(2)]
        rows = lambda t: [t[:, 0, :], t[:, 1, :]]
        m = self.rms_rows(rows(self.X), rows(XN), rows(junk), stat[:, 0:4], [(x,) for x in self.m_x])
        m_h = self.to_columns(rows(XN), HT, 256, lambda k: self.Ac(0, k, 0), lambda k: self.B(0, k, 0), banks,
                              m + self.m_mod)
        m = self.rms_rows(rows(CTX), rows(CTX), rows(junk), stat[:, 4:8], [(x, P.last("v")) for x in m_ctx])
        m_h += self.to_columns(rows(CTX), HT, 0, lambda k: self.Ac(0, k, 1), lambda k: self.B(0, k, 1), banks, m)
        W = I["w_in_even"][0]
        P.fence()

        def row_form(c0, n, tiles, use):
            s, w, mw = self.cols(W, c0, n)
            for t in tiles:
                b, ps, free = banks.take()
                m = P.mm(ps[:, 0:n], [(HT[:, k, t * 128:(t + 1) * 128], w[:, k, :]) for k in range(8)], mw, free)
                banks.free(b, use(t, ps, m))
                if t == tiles[-1]:
                    self.R.free(s, m)
                yield

        s, w, mw = self.cols(W, 2816, 16)
        b, ps, free = banks.take()
        m = P.mm(ps[0:16, :], [(w[:, k, :], HT[:, k, :]) for k in range(8)], mw, free)
        self.R.free(s, m)
        m_g16 = P.v(lambda e, ps=ps: e.tensor_scalar(G16[0:16, :], ps[0:16, :], self.col("bgate", 1)[0:16, :], None, ALU.add), m)
        banks.free(b, m_g16)

        A.back(at2)
        RAW = A.take(8, 512)
        m_qk = [None] * 8
        for c0, base, lo in ((1280, 4, 0), (768, 0, 256)):
            s, w, mw = self.cols(W, c0, 512)
            for q in range(4):
                j = base + q
                b, ps, free = banks.take()
                n = 512 - lo
                m = P.mm(ps[:, 0:n], [(w[:, k, q * 128:(q + 1) * 128], HT[:, k, lo:512]) for k in range(8)], mw, free)
                m_raw = self.evac("a", RAW[:, j, lo:512], ps[:, 0:n], m)
                banks.free(b, m_raw)
                w0, w1, w2 = (self.col("conv", 1, 8 * i + j) for i in range(3))
                sv = RAW[:, j, lo:512].rearrange("p (a b) -> p a b", b=256)
                dv = QK[:, j, lo:512].rearrange("p (a b) -> p a b", b=256)
                m1 = P.v(lambda e, s=sv, d=dv, w=w1: e.tensor_scalar(d, s, w, None, ALU.mult), m_raw)
                m1 = P.v(lambda e, s=sv, d=dv, w=w0: e.scalar_tensor_tensor(d[:, :, 1:256], s[:, :, 0:255], w, d[:, :, 1:256],
                                                                            ALU.mult, ALU.add), m1)
                m1 = P.v(lambda e, s=sv, d=dv, w=w2: e.scalar_tensor_tensor(d[:, :, 0:255], s[:, :, 1:256], w, d[:, :, 0:255],
                                                                            ALU.mult, ALU.add), m1)
                m_qk[j] = P.a(lambda e, d=dv: e.activation(d, d, ACT.Silu), m1)
                if j >= 4:
                    m_qk[j] = P.g(lambda e, j=j: e.tensor_scalar(QK[:, j, :], QK[:, j, :], 128.0 ** -0.5, None, ALU.mult), m_qk[j])
            self.R.free(s, m)
        m_one = P.g(lambda e: e.memset(V1[:, :, :, 128:129], 1.0))
        m_v1 = {}

        def use_v(t, ps, m):
            m_v1[t] = self.evac("a", V1[:, t, :, 0:128], ps.rearrange("p (h d) -> p h d", h=4), m)
            return m_v1[t]

        def use_o(t, ps, m):
            return P.a(lambda e: e.activation(OB[:, t - 2, :], ps, ACT.Sigmoid), m)

        m_kv = {}

        def use_kv(t, ps, m):
            P.v(lambda e: e.tensor_copy(KA[:, t, :, 0, :], ps[:, 0:128].rearrange("p (h d) -> p h d", h=2)), m)
            m_kv[t] = P.v(lambda e: e.tensor_copy(VA[:, t, :], ps[:, 128:256]), m)
            return m_kv[t]

        def use_q(t, ps, m):
            m_kv[t + 2] = self.evac("a", QA[:, t - 2, :], ps, m)
            return m_kv[t + 2]

        for _ in row_form(1792, 512, range(4), use_v):
            pass
        lent, _ = self.R.lend(3)
        P.fence()
        A.back(at2)
        MT = A.take(8, 256)
        A.borrow(lent)
        abanks = Banks(self.ps, [4, 5])

        def attention():
            yield from row_form(512, 256, range(4), use_kv)
            yield from row_form(0, 512, (2, 3), use_q)
            yield from row_form(2304, 512, (2, 3), use_o)
            yield from self.attention(QA, KA, VA, stat, rope, grow, MT, abanks, list(m_kv.values()))

        def modulation():
            while self.mod_work:
                self.fill()
                yield
                yield
                yield
                yield

        banks = Banks(self.ps, [4, 5])
        parts = self.mlstm_gates(G16, sel, QK, [Banks(self.ps, [0, 1]), Banks(self.ps, [2, 3])])
        interleave(attention(), self.mlstm(0, parts, QK, V1, mmask, sel), self.mlstm(1, parts, QK, V1, mmask, sel), modulation())
        P.fence()
        banks = Banks(self.ps, [0, 1, 2, 3, 4, 5])
        self.mlstm_out(parts, OB, stat, ghn, MT, banks)
        P.fence()
        A.borrow(None)
        self.R.restore()
        self.gate_rows(0, 0, banks, [P.last("v")])
        self.gate_rows(0, 1, banks, [P.last("v")])
        self.norm_columns(0, 1, [P.last("v")])
        for w in range(2):
            self.m_mod = self.norm_columns(1, w, [P.last("v")])
        P.fence()
        tmp = A.take(2, 512)
        W = I["w_out_even"][0]
        for half in range(2):
            s, w, mw = self.cols(W, half * 512, 512)
            for t in range(2):
                b, ps, free = banks.take()
                sl = slice(half * 512, half * 512 + 512)
                m = P.mm(ps, [(MT[:, k, t * 128:(t + 1) * 128], w[:, k, :]) for k in range(8)], mw, free)
                m1 = P.v(lambda e, ps=ps, t=t, sl=sl: e.tensor_tensor(tmp[:, t, :], ps, self.gate[:, 0, sl], ALU.mult),
                         m, P.last("g"))
                banks.free(b, m1)
                P.g(lambda e, t=t, sl=sl: e.tensor_tensor(self.X[:, t, sl], self.X[:, t, sl], tmp[:, t, :], ALU.add), m1)
            self.R.free(s, m)
        P.fence()
        A.back(at0)

    def mlstm_gates(self, G16, sel, QK, banks2):
        P, A = self.P, self.A
        banks = Banks(self.ps, [0, 1, 2, 3])
        IG, LF, BB = (A.take(512) for _ in range(3))
        MM = G16
        P.g(lambda e: e.memset(IG, 0.0))
        mz = P.g(lambda e: e.memset(LF, 0.0))
        flip = lambda a: a.rearrange("p (c t) -> p c t", c=2)[:, :, ::-1]
        for which, dst in ((8, IG), (9, LF)):
            b, ps, free = banks.take()
            m = P.mm(ps[0:64, :], [(sel[0:16, which, 0:64], G16[0:16, :])], free)
            P.v(lambda e, ps=ps, d=dst: e.tensor_copy(d[0:4, :], ps[0:4, :]), m, mz)
            mf = P.v(lambda e, ps=ps, d=dst: e.tensor_copy(d[32:36, :].rearrange("p (c t) -> p c t", c=2), flip(ps[32:36, :])), m, mz)
            banks.free(b, mf)
        R = slice(0, 36)
        m = P.v(lambda e: e.scalar_tensor_tensor(BB[R, :], LF[R, :], -1.0, LF[R, :], ALU.mult, ALU.max), mf)
        m = P.a(lambda e: e.activation(BB[R, :], BB[R, :], ACT.Exp, scale=-1.0), m)
        m = P.a(lambda e: e.activation(BB[R, :], BB[R, :], ACT.Ln, bias=self.onecol[R, :]), m)
        m = P.v(lambda e: e.scalar_tensor_tensor(LF[R, :], LF[R, :], 0.0, BB[R, :], ALU.min, ALU.subtract), m)
        m = P.v(lambda e: e.tensor_tensor_scan(BB[R, :], self.onecol[R, :].broadcast_to([36, 512]), LF[R, :], 0.0, ALU.mult, ALU.add), m)
        m = P.v(lambda e: e.tensor_tensor(IG[R, :], IG[R, :], BB[R, :], ALU.subtract), m)
        m = P.v(lambda e: e.tensor_tensor_scan(MM[R, :], IG[R, :], IG[R, :], -NEG, ALU.max, ALU.max), m)
        m = P.v(lambda e: e.tensor_tensor(LF[R, :], MM[R, :], BB[R, :], ALU.add), m)
        for src, dst in ((IG, BB), (MM, IG), (LF, MM)):
            P.v(lambda e, s=src, o=dst: e.tensor_copy(o[0:4, :], s[0:4, :]), m)
            m = P.v(lambda e, s=src, o=dst: e.tensor_copy(o[32:36, :].rearrange("p (c t) -> p c t", c=2), flip(s[32:36, :])), m)
        m_mb = P.v(lambda e: e.tensor_copy(LF[0:1, 0:1], LF[0:1, 0:1]), m)
        GC = A.take(4, 36)
        EM = A.take(4, 36)
        marks = [m_mb]
        for src, dst in ((BB, GC), (MM, EM)):
            b, ps, free = banks.take()
            for c in range(4):
                m = P.tr(ps[:, c * 36:c * 36 + 36], src[R, c * 128:(c + 1) * 128], self.ident[0:36, 0:36], free, m_mb, inc=c == 3)
            if dst is GC:
                m = P.v(lambda e, ps=ps: e.tensor_copy(GC, ps[:, 0:144].rearrange("p (a b) -> p a b", a=4)), m)
            else:
                m = P.a(lambda e, ps=ps: e.activation(EM, ps[:, 0:144].rearrange("p (a b) -> p a b", a=4), ACT.Exp, scale=-1.0), m)
            marks.append(m)
            banks.free(b, m)
        KR = A.take(4, 4, 128)
        for c in range(4):
            b, ps, free = banks.take()
            for h in range(4):
                m = P.tr(ps[:, h * 128:(h + 1) * 128], QK[:, 4 + h, c * 128:(c + 1) * 128], self.ident, free, inc=h == 3)
            m = self.evac("av"[c % 2], KR[:, :, c, :], ps.rearrange("p (h d) -> p h d", h=4), m)
            marks.append(m)
            banks.free(b, m)
        HO = A.take(2, 2, 512)
        own = [dict(CS=A.take(2, 129), ME=A.take(2, 4), W2=A.take(8), DN=A.take(8), WS=A.take(2, 8), DT=A.take(2, 128), ST=A.take(2, 128),
                    QS=A.take(2, 128), KW=A.take(2, 128), bc=self.ps[:, 2 * d, :], work=Banks(self.ps, [2 * d + 1])) for d in range(2)]
        return dict(GC=GC, EM=EM, KR=KR, HO=HO, MX=IG, marks=marks, own=own, LF=LF)

    def mlstm(self, d, parts, QK, V1, mmask, sel):
        P = self.P
        GC, EM, KR, HO, MX, ready = (parts[k] for k in ("GC", "EM", "KR", "HO", "MX", "marks"))
        o = parts["own"][d]
        CS, ME, W2, DN, WS, DT, ST, QS, KW, bc, work = (o[k] for k in ("CS", "ME", "W2", "DN", "WS", "DT", "ST", "QS", "KW", "bc", "work"))
        order = [[0, 1, 2, 3], [1, 0, 3, 2]][d]
        qt = lambda h, c: QK[:, h, c * 128:(c + 1) * 128]
        kt = lambda h, c: QK[:, 4 + h, c * 128:(c + 1) * 128]
        R = slice(0, 36)
        w_free = [None, None]
        t_st = [None, None]
        t_kw = [None, None]
        t_cs = [None, None]
        bc_free = []
        a_w2 = None
        for h in range(4):
            r = 32 * d + h
            m = P.mm(bc, [(sel[R, 4 * d + h, :], MX[R, :])], *bc_free, *ready)
            me = ME[:, h % 2, :]
            m_me = P.v(lambda e, me=me: e.tensor_copy(me, bc.rearrange("p (c t) -> p c t", c=4)[:, :, 0 if d else 127]), m, *bc_free)
            yield
            mw = P.v(lambda e, r=r, me=me: e.tensor_tensor(W2[:, 0:4], GC[:, :, r], me, ALU.subtract), m_me, a_w2)
            for c in (1, 2):
                p0, p1 = order[c - 1], order[c]
                mw = P.v(lambda e, c=c, p0=p0, p1=p1, me=me: e.tensor_tensor(
                    W2[:, 3 + c:4 + c], me[:, p0:p0 + 1], me[:, p1:p1 + 1], ALU.subtract), m_me, a_w2)
            w = WS[:, h % 2, :]
            m_w = a_w2 = P.a(lambda e, w=w: e.activation(w[:, 0:6], W2[:, 0:6], ACT.Exp), mw, w_free[h % 2])
            m_dt, m_qs = {}, {}
            for c in (2, 3):
                oc, u, pe = order[c], c % 2, order[c - 1]
                dt, qs, bcc = DT[:, u, :], QS[:, u, :], bc[:, oc * 128:(oc + 1) * 128]
                m1 = P.v(lambda e, oc=oc, r=r, dt=dt, bcc=bcc: e.scalar_tensor_tensor(
                    dt, bcc, GC[:, oc, r:r + 1], mmask[:, d, :], ALU.subtract, ALU.max), m_me)
                m4 = P.a(lambda e, qs=qs, bcc=bcc, me=me, pe=pe: e.activation(qs, bcc, ACT.Exp, scale=-1.0, bias=me[:, pe:pe + 1]),
                         m_me, t_st[u], m1)
                m_dt[u] = P.a(lambda e, dt=dt: e.activation(dt, dt, ACT.Exp, scale=-1.0), m1)
                m_qs[u] = P.v(lambda e, h=h, oc=oc, qs=qs: e.tensor_tensor(qs, qs, qt(h, oc), ALU.mult), m4)
                bc_free = [m1, m4]
                yield
            m_state = None
            for c in range(4):
                oc = order[c]
                cs = CS[:, c % 2, :]
                pc = CS[:, (c + 1) % 2, :]
                if c >= 2:
                    u = c % 2
                    dt, st, qs = DT[:, u, :], ST[:, u, :], QS[:, u, :]
                    b, ps, free = work.take()
                    m2 = P.mm(ps[:, 0:128], [(kt(h, oc), qt(h, oc))], free)
                    m3 = P.v(lambda e, ps=ps, dt=dt, st=st: e.tensor_tensor(st, dt, ps[:, 0:128], ALU.mult), m_dt[u], m2, t_st[u])
                    yield
                    m6 = P.mm(ps[:, 256:385], [(st, V1[:, oc, h, :]), (qs, pc)], m3, m_qs[u], m_state)
                    t_st[u] = m6
                    t_cs[(c + 1) % 2] = m6
                    dn = DN[:, 4 * u:4 * u + 1]
                    m7 = P.v(lambda e, ps=ps, dn=dn, oc=oc, r=r: e.tensor_scalar(dn, ps[:, 384:385], -1.0, EM[:, oc, r:r + 1], ALU.mult, ALU.max),
                             m6)
                    m7 = P.v(lambda e, ps=ps, dn=dn: e.tensor_tensor(dn, dn, ps[:, 384:385], ALU.max), m7)
                    m7 = P.v(lambda e, dn=dn: e.reciprocal(dn, dn), m7)
                    m8 = P.v(lambda e, ps=ps, dn=dn, h=h, oc=oc: e.tensor_scalar(
                        HO[:, d, oc - 2, h * 128:(h + 1) * 128], ps[:, 256:384], dn, None, ALU.mult), m7)
                    work.free(b, m8)
                    yield
                if c < 3:
                    kw = KW[:, c % 2, :]
                    m1 = P.v(lambda e, h=h, oc=oc, w=w, kw=kw: e.tensor_scalar(kw, KR[:, h, oc, :], w[:, oc:oc + 1], None, ALU.mult),
                             m_w, t_kw[c % 2])
                    b, ps, free = work.take()
                    m2 = P.mm(ps[:, 0:129], [(kw, V1[:, oc, h, :])], m1, free)
                    t_kw[c % 2] = m2
                    if c == 0:
                        m_state = P.v(lambda e, ps=ps, cs=cs: e.tensor_copy(cs, ps[:, 0:129]), m2, t_cs[0])
                    else:
                        m_state = P.v(lambda e, ps=ps, cs=cs, pc=pc, c=c, w=w: e.scalar_tensor_tensor(
                            cs, pc, w[:, 3 + c:4 + c], ps[:, 0:129], ALU.mult, ALU.add), m2, m_state, t_cs[c % 2])
                    w_free[h % 2] = m_state
                    work.free(b, m_state)
                    yield

    def mlstm_out(self, parts, OB, stat, ghn, MT, banks):
        P = self.P
        HO, KR, sq = parts["HO"], parts["KR"], parts["LF"]
        HM = KR.rearrange("p a b c -> p (a b c)")[:, 0:1024].rearrange("p (a b) -> p a b", a=2)
        as4 = lambda a: a.rearrange("p (h d) -> p h d", h=4)
        m1 = None
        for t in range(2):
            m = P.v(lambda e, t=t: e.tensor_tensor(HM[:, t, :], HO[:, 0, t, :], HO[:, 1, t, :], ALU.add))
            s4 = stat[:, 16 + 8 * t:20 + 8 * t]
            m1 = P.a(lambda e, t=t: e.activation(sq, HM[:, t, :], ACT.Square), m, P.last("v"))
            m2 = P.v(lambda e, s4=s4: e.tensor_reduce(s4, as4(sq), AX, ALU.add), m1)
            m3 = self.rstd(s4, s4, 128, self.eps, m2)
            m4 = P.v(lambda e, t=t, s4=s4: e.tensor_tensor(as4(HM[:, t, :]), as4(HM[:, t, :]), s4.unsqueeze(2).broadcast_to([128, 4, 128]),
                                                           ALU.mult), m3)
            m5 = P.v(lambda e, t=t: e.tensor_tensor(HM[:, t, :], HM[:, t, :], ghn, ALU.mult), m4)
            m_hm = P.v(lambda e, t=t: e.tensor_tensor(HM[:, t, :], HM[:, t, :], OB[:, t, :], ALU.mult), m5)
        self.to_columns([HM[:, 0, :], HM[:, 1, :]], MT[:, 4:8, :], 0, None, None, banks, [m_hm])

    def attention(self, QA, KA, VA, stat, rope, grow, MT, banks, ready):
        P, A = self.P, self.A
        KT = A.take(2, 512)
        QT = A.take(8, 256)
        SP_ = MT[:, 4:8, :].rearrange("p (a b) c -> p a (b c)", a=2)
        PT = A.take(4, 256)
        sq, t1, t2 = SP_[:, 0, :], SP_[:, 1, :], PT[:, 0:2, :].rearrange("p a b -> p (a b)")
        mx = A.take(16)
        sm = A.take(16)
        m_z = P.g(lambda e: e.memset(QT, 0.0))
        kview = lambda t: KA[:, t, :, 0, :]
        qview = lambda t: QA[:, t, :].rearrange("p (h d) -> p h d", h=8)
        m_fin = []
        m_prev = None
        for which, (view, heads, tiles, lat) in enumerate(((qview, 8, (0, 1), (0, 1)), (kview, 2, (0, 1, 2, 3), (2, 3)))):
            for t in tiles:
                x = view(t)
                n = heads * 64
                as3 = lambda a, heads=heads, n=n: a[:, 0:n].rearrange("p (h d) -> p h d", h=heads)
                st = stat[:, 32:32 + heads]
                m = P.a(lambda e, x=x, as3=as3: e.activation(as3(sq), x, ACT.Square), m_prev, *ready)
                m = P.v(lambda e, as3=as3, st=st: e.tensor_reduce(st, as3(sq), AX, ALU.add), m, m_prev)
                m = self.rstd(st, st, 64, self.eps, m)
                yield
                m = P.v(lambda e, x=x, st=st, heads=heads: e.tensor_tensor(x, x, st.unsqueeze(2).broadcast_to([128, heads, 64]), ALU.mult), m)
                m = P.v(lambda e, x=x, heads=heads, which=which: e.tensor_tensor(
                    x, x, grow[:, which:which + 1, :].broadcast_to([128, heads, 64]), ALU.mult), m)
                if t in lat:
                    lt = t - lat[0]
                    cosv, sinv = rope[:, 0, lt, :], rope[:, 1, lt, :]
                    ma = P.g(lambda e, x=x, as3=as3, c=cosv, heads=heads: e.tensor_tensor(
                        as3(t1), x, c.unsqueeze(1).broadcast_to([128, heads, 64]), ALU.mult), m)
                    for half in range(2):
                        mb = P.v(lambda e, x=x, as3=as3, s=sinv, heads=heads, half=half: e.tensor_tensor(
                            as3(t2).rearrange("p h (a b c) -> p h a b c", a=2, b=2)[:, :, :, half, :],
                            x.rearrange("p h (a b c) -> p h a b c", a=2, b=2)[:, :, :, 1 - half, :],
                            s.rearrange("p (a b c) -> p a b c", a=2, b=2)[:, :, half, :].unsqueeze(1).broadcast_to([128, heads, 2, 16]),
                            ALU.mult), m)
                    m = P.v(lambda e, x=x, as3=as3: e.tensor_tensor(x, as3(t1), as3(t2), ALU.add), ma, mb)
                if which == 1:
                    m = P.v(lambda e, t=t: e.tensor_copy(KA[:, t, :, 1, :], KA[:, t, :, 0, :]), m)
                m_prev = m
                m_fin.append(m)
                yield
        mq, mk = [], []
        for p in range(4):
            b, ps, free = banks.take()
            for t in range(2):
                m = P.tr(ps[:, t * 128:(t + 1) * 128], QA[:, t, p * 128:(p + 1) * 128], self.ident, free, m_fin[1], inc=t == 1)
            mq.append(self.evac("a", QT[0:64, 2 * p, :], ps[0:64, 0:256], m, m_z))
            mq.append(self.evac("a", QT[64:128, 2 * p + 1, :], ps[64:128, 0:256], m, m_z))
            banks.free(b, mq[-1])
            yield
        for kv in range(2):
            b, ps, free = banks.take()
            for t in range(4):
                m = P.tr(ps[:, t * 128:(t + 1) * 128], KA[:, t, kv, :, :].rearrange("p a d -> p (a d)"), self.ident, free,
                         *m_fin, inc=t == 3)
            mk.append(self.evac("v", KT[:, kv, :], ps, m))
            banks.free(b, mk[-1])
            yield
        r_sp, r_pt = [None, None], None
        ob = self.ps[:, 6, :]
        m_ob = None
        for h in range(8):
            kv = h // 4
            for t in range(2):
                i = 8 * t + h
                sp = SP_[:, t, :]
                b, ps, free = banks.take()
                m = P.mm(ps, [(QT[:, h, t * 128:(t + 1) * 128], KT[:, kv, :])], free, *(mq + mk))
                m1 = P.v(lambda e, ps=ps, i=i: e.tensor_reduce(mx[:, i:i + 1], ps, AX, ALU.max), m)
                m1 = P.v(lambda e, i=i: e.tensor_scalar(mx[:, i:i + 1], mx[:, i:i + 1], -0.125, None, ALU.mult), m1)
                m2 = P.a(lambda e, ps=ps, i=i, sp=sp: e.activation(sp, ps, ACT.Exp, scale=0.125, bias=mx[:, i:i + 1],
                                                                   accum_out=sm[:, i:i + 1]), m1, r_sp[t])
                yield
                m3 = P.v(lambda e, i=i: e.reciprocal(sm[:, i:i + 1], sm[:, i:i + 1]), m2)
                m3 = P.v(lambda e, i=i, sp=sp: e.tensor_scalar(sp, sp, sm[:, i:i + 1], None, ALU.mult), m3)
                for c in range(4):
                    m4 = P.tr(ps[:, c * 128:(c + 1) * 128], sp[:, c * 128:(c + 1) * 128], self.ident, m3, inc=c == 3)
                r_sp[t] = m4
                m5 = self.evac("va"[t], PT[:, :, t * 128:(t + 1) * 128], ps.rearrange("p (c t) -> p c t", c=4), m4, r_pt)
                banks.free(b, m5)
                if t == 0:
                    m_p0 = m5
                yield
            hp = slice(64 * (h % 2), 64 * (h % 2) + 64)
            r_pt = P.mm(ob[hp, 0:256], [(VA[:, c, kv * 64:(kv + 1) * 64], PT[:, c, :]) for c in range(4)], m5, m_p0, m_ob)
            m_ob = self.evac("v", MT[hp, h // 2, :], ob[hp, 0:256], r_pt)
            yield

    def moe(self, i):
        P, A, I = self.P, self.A, self.I
        at0 = A.mark()
        banks = Banks(self.ps, [0, 1, 2, 3, 4, 5])
        rows = lambda t: [t[:, 0, :], t[:, 1, :]]
        XS = A.take(8, 512)
        GR = A.take(16, 256)
        at1 = A.mark()
        XN = A.take(2, D)
        HT = A.take(8, 256)
        PN = A.take(2, 512)
        WR = A.take(8, 16)
        AF = A.take(2, 16)
        stat = A.take(24)
        CUR = A.take(2, 256)
        VL = A.take(32)
        IX = A.take(32)
        IF = A.take(32)
        REP = A.take(128)
        MI = A.take(16, 32)
        IC = A.take(16)
        VCOL = A.take(16)
        m_wr = P.dma("a", WR, I["w_router"][i].rearrange("(k p) e -> p k e", p=128))
        m = self.rms_rows(rows(self.X), rows(XN), [XS[:, 0:2, :].rearrange("p a b -> p (a b)"), XS[:, 2:4, :].rearrange("p a b -> p (a b)")],
                          stat[:, 0:4], [(), ()])
        m_xn = m
        mh = self.to_columns(rows(XN), HT, 0, lambda k: self.Ac(1, k, 0), lambda k: self.B(1, k, 0), banks, m + self.m_mod)
        b, lg, free = banks.take()
        ms = []
        for t in range(2):
            ms.append(P.mm(lg[:, 16 * t:16 * t + 16], [(HT[:, k, t * 128:(t + 1) * 128], WR[:, k, :]) for k in range(8)], free, m_wr, *mh))
        m = P.v(lambda e: e.tensor_reduce(stat[:, 8:10], lg[:, 0:32].rearrange("p (t e) -> p t e", t=2), AX, ALU.max), *ms)
        m = P.v(lambda e: e.tensor_scalar(stat[:, 10:12], stat[:, 8:10], -1.0, None, ALU.mult), m)
        for t in range(2):
            me = P.a(lambda e, t=t: e.activation(AF[:, t, :], lg[:, 16 * t:16 * t + 16], ACT.Exp, bias=stat[:, 10 + t:11 + t],
                                                 accum_out=stat[:, 12 + t:13 + t]), m)
        banks.free(b, me)
        m = P.v(lambda e: e.reciprocal(stat[:, 14:16], stat[:, 12:14]), me)
        m = P.v(lambda e: e.tensor_tensor(AF, AF, stat[:, 14:16].unsqueeze(2).broadcast_to([128, 2, 16]), ALU.mult), m)
        b, ps, free = banks.take()
        for t in range(2):
            m2 = P.tr(ps[0:16, t * 128:(t + 1) * 128], AF[:, t, :], self.ident, free, m, inc=t == 1)
        E = slice(0, 16)
        m = P.v(lambda e, ps=ps: e.tensor_copy(CUR[E, 0, :], ps[E, 0:256]), m2)
        banks.free(b, m)
        for r in range(4):
            cur, nxt = CUR[E, r % 2, :], CUR[E, (r + 1) % 2, :]
            v8 = VL[E, 8 * r:8 * r + 8]
            i8 = IX[E, 8 * r:8 * r + 8].bitcast(U32)
            mv = P.v(lambda e, v8=v8, cur=cur: e.max(v8, cur), m)
            P.v(lambda e, v8=v8, cur=cur, i8=i8: e.max_index(i8, v8, cur), mv)
            m = P.v(lambda e, v8=v8, cur=cur, nxt=nxt: e.match_replace(nxt, v8, cur, -1.0), mv)
        m = P.v(lambda e: e.tensor_copy(IF[E, :], IX[E, :].bitcast(U32)), P.last("v"))
        for src, dst in ((IF, IC), (VL, VCOL)):
            m1 = P.v(lambda e, src=src: e.tensor_copy(REP[E, :].rearrange("p (a b) -> p a b", a=4),
                                                      src[E, :].unsqueeze(1).broadcast_to([16, 4, 32])), m, P.last("t"))
            b, ps2, free = banks.take()
            m2 = P.tr(ps2[:, 0:16], REP[E, :], self.ident[E, 0:16], free, m1)
            m_ic = P.v(lambda e, dst=dst, ps2=ps2: e.tensor_copy(dst, ps2[:, 0:16]), m2)
            banks.free(b, m_ic)
        m1 = P.v(lambda e: e.tensor_tensor(MI[E, :, :], IF[E, :].unsqueeze(1).broadcast_to([16, 16, 32]),
                                           self.ident[E, 0:16].unsqueeze(2).broadcast_to([16, 16, 32]), ALU.mult), m)
        b, ps3, free = banks.take()
        m2 = P.mm(ps3, [(self.ones[E, :], MI[E, :, :].rearrange("p a b -> p (a b)"))], m1, free)
        for t in range(2):
            m_p = P.v(lambda e, t=t: e.tensor_scalar(PN[:, t, :], ps3, self.iota_p[t], None, ALU.is_equal), m2)
        banks.free(b, m_p)
        for k in range(8):
            b, ps, free = banks.take()
            m = P.mm(ps, [(XN[:, t, k * 128:(k + 1) * 128], PN[:, t, :]) for t in range(2)], m_p, free, *m_xn)
            m_xs = self.affine("av"[k % 2], XS[:, k, :], ps, self.Ac(1, k, 0), self.B(1, k, 0), m)
            banks.free(b, m_xs)
        for e_ in range(16):
            m_gr = P.v(lambda e, n=e_: e.tensor_scalar(GR[:, n, :], self.iota, IC[:, n:n + 1], VCOL[:, n:n + 1],
                                                       ALU.is_equal, ALU.mult), m_ic)
        P.fence()
        A.back(at1)
        SG = A.take(256)
        AA = A.take(256)
        AT = A.take(2, 4, 32)
        OS = A.take(D)
        GU = [self.ps[:, 0, 0:256], self.ps[:, 1, 0:256]]
        TR = self.ps[:, 0, 256:512]
        O = [self.ps[:, 2, :], self.ps[:, 3, :]]
        Y = self.ps[:, 4:8, :]
        free_gu = free_tr = None
        free_o = ()
        m_comb = None
        pend = None

        def combine(n, *mo):
            for t in range(2):
                for hf in range(2):
                    m = P.mm(Y[:, 2 * t + hf, :], [(GR[:, n, t * 128:(t + 1) * 128], OS[:, hf * 512:(hf + 1) * 512])], *mo,
                             start=n == 0, stop=n == 15)
            return m

        for n in range(16):
            for which, name in enumerate(("w_exp_gate", "w_exp_up")):
                for hk in range(2):
                    s, w, mw = self.rows(I[name][i, n], 4 * hk, 4)
                    for k in range(4):
                        for j in range(4):
                            first = k == 0 and j == 0
                            m = P.t(lambda e, j=j, k=k, hk=hk, w=w, which=which, n=n: e.matmul(
                                GU[which][32 * j:32 * j + 32, :], XS[:, 4 * hk + k, 32 * n:32 * n + 32],
                                w[:, k, 256 * j:256 * j + 256], start=hk == 0 and k == 0, stop=hk == 1 and k == 3, skip_group_check=True),
                                *((mw, free_gu) if first else ()), inc=k == 3 and j == 3)
                    self.R.free(s, m)
                if which == 0:
                    mg = P.a(lambda e: e.activation(SG, GU[0], ACT.Silu), m, P.last("v"))
                    if pend is not None:
                        m_comb = combine(*pend)
            ma = P.v(lambda e: e.tensor_tensor(AA, SG, GU[1], ALU.mult), mg, m, P.last("t"))
            free_gu = ma
            for hh in range(2):
                mt = P.tr(TR[:, 128 * hh:128 * hh + 128], AA[:, 128 * hh:128 * hh + 128], self.ident, ma, free_tr, inc=hh == 1)
            m_at = self.evac("v", AT.rearrange("p a b c -> p (a b c)"), TR, mt)
            free_tr = m_at
            for hk in range(2):
                s, w, mw = self.rows(I["w_exp_down"][i, n], 4 * hk, 4)
                for hf in range(2):
                    for j in range(4):
                        kk = 4 * hk + j
                        m = P.t(lambda e, j=j, hf=hf, hk=hk, w=w, kk=kk: e.matmul(
                            O[hf][32 * j:32 * j + 32, :], AT[:, kk % 2, kk // 2, :], w[:, j, 512 * hf:512 * hf + 512],
                            start=hk == 0, stop=hk == 1, skip_group_check=True),
                            *((mw, m_at, *free_o) if j == 0 else ()), inc=hf == 1 and j == 3)
                self.R.free(s, m)
            m1 = P.a(lambda e: e.activation(OS[:, 0:512], O[0], ACT.Copy), m, m_comb)
            m2 = P.v(lambda e: e.tensor_copy(OS[:, 512:1024], O[1]), m, m_comb)
            free_o = (m1, m2)
            pend = (n, m1, m2)
        m = combine(*pend)
        P.fence()
        A.back(at0)
        tmp = A.take(2, 2, 512)
        for t in range(2):
            for hf in range(2):
                sl = slice(512 * hf, 512 * hf + 512)
                m1 = P.v(lambda e, t=t, hf=hf, sl=sl: e.tensor_tensor(tmp[:, t, hf, :], Y[:, 2 * t + hf, :], self.gate[:, 1, sl], ALU.mult), m)
                P.g(lambda e, t=t, hf=hf, sl=sl: e.tensor_tensor(self.X[:, t, sl], self.X[:, t, sl], tmp[:, t, hf, :], ALU.add), m1)
        P.fence()
        A.back(at0)

    def pool_mixer(self):
        P, A, I = self.P, self.A, self.I
        self.set_layer(1)
        at0 = A.mark()
        banks = Banks(self.ps, list(range(8)))
        self.gate_rows(1, 0, banks, [])
        self.gate_rows(1, 1, banks, [])
        P.fence()
        rows = lambda t: [t[:, 0, :], t[:, 1, :]]
        XN = A.take(2, D)
        HT = A.take(8, 256)
        U = A.take(2, D)
        BD = A.take(4, 2, 256)
        PT = A.take(8, 256)
        WG = A.take(4, 2, 256)
        SPG = A.take(D)
        stat = A.take(8)
        m_bd = P.dma("a", BD, I["k_band"].rearrange("p (a b c) -> p a b c", a=4, b=2))
        m_wg = P.dma("a", WG, I["w_pool_grp"][0].rearrange("g (k p) n -> p g k n", p=128))
        m_sp = P.dma("a", SPG, I["s_pool"][0:1, :].broadcast_to([128, D]))
        m_sg = P.v(lambda e: e.tensor_tensor(SPG, SPG, self.gate[:, 0, :], ALU.mult), m_sp, *self.m_mod)
        m = self.rms_rows(rows(self.X), rows(XN), rows(U), stat[:, 0:4], [(), ()])
        mh = self.to_columns(rows(XN), HT, 0, lambda k: self.Ac(0, k, 0), lambda k: self.B(0, k, 0), banks, m + self.m_mod)
        for half in range(2):
            s, w, mw = self.cols(I["w_in_odd"][0], half * 512, 512)
            for t in range(2):
                b, ps, free = banks.take()
                m = P.mm(ps, [(HT[:, k, t * 128:(t + 1) * 128], w[:, k, :]) for k in range(8)], mw, free, *mh)
                m_u = self.evac("av"[t], U[:, t, half * 512:half * 512 + 512], ps, m)
                banks.free(b, m_u)
            self.R.free(s, m)
        marks = [P.last("v"), P.last("a")]
        mp = []
        for c in range(0, 8, 2):
            b, ps, free = banks.take()
            for u in range(2):
                m = P.mm(ps[:, 256 * u:256 * u + 256], [(U[:, t, (c + u) * 128:(c + u + 1) * 128], BD[:, c // 2, t, :]) for t in range(2)],
                         free, m_bd, *marks)
            mp.append(self.evac("av"[c // 2 % 2], PT[:, c:c + 2, :], ps.rearrange("p (a b) -> p a b", a=2), m))
            banks.free(b, mp[-1])
        for t in range(2):
            for g2 in range(2):
                b, ps, free = banks.take()
                for u in range(2):
                    g = 2 * g2 + u
                    m = P.mm(ps[:, 256 * u:256 * u + 256], [(PT[:, 2 * g + k, t * 128:(t + 1) * 128], WG[:, g, k, :]) for k in range(2)],
                             free, m_wg, *mp)
                sl = slice(512 * g2, 512 * g2 + 512)
                tmp = XN[:, t, sl]
                m1 = P.v(lambda e, ps=ps, sl=sl, tmp=tmp: e.tensor_tensor(tmp, ps, SPG[:, sl], ALU.mult), m, m_sg)
                banks.free(b, m1)
                P.g(lambda e, t=t, sl=sl, tmp=tmp: e.tensor_tensor(self.X[:, t, sl], self.X[:, t, sl], tmp, ALU.add), m1)
        P.fence()
        A.back(at0)

    def final_norm(self):
        P, A, I = self.P, self.A, self.I
        at0 = A.mark()
        g = A.take(D)
        junk = A.take(2, D)
        stat = A.take(4)
        mg = P.dma("a", g, I["g_final"].rearrange("(a n) -> a n", a=1).broadcast_to([128, D]))
        rows = lambda t: [t[:, 0, :], t[:, 1, :]]
        m = self.rms_rows(rows(self.X), rows(junk), rows(junk), stat, [(), ()])
        for t in range(2):
            P.v(lambda e, t=t: e.tensor_tensor(self.X[:, t, :], junk[:, t, :], g, ALU.mult), mg, m[t])
        P.fence()
        A.back(at0)

    def second_block_memory(self):
        self.A.back(self.keep)

    def pre_norm(self, at, banks, XN, HT, junk, stat):
        rows = lambda t: [t[:, 0, :], t[:, 1, :]]
        m = self.rms_rows(rows(self.X), rows(XN), rows(junk), stat, [(), ()])
        return self.to_columns(rows(XN), HT, 0, lambda k: self.col("nrm", 1, 8 * at + k), None, banks, m)

    def post_norm_add(self, Y, layer, k, factor, junk, stat, m_y, grow, m_g):
        P = self.P
        for t in range(2):
            y = Y[:, 2 * t:2 * t + 2, :].rearrange("p a b -> p (a b)")
            m = P.a(lambda e, t=t, y=y: e.activation(junk[:, t, :], y, ACT.Square, accum_out=stat[:, t:t + 1]), *m_y)
        m = self.rstd(stat[:, 2:4], stat[:, 0:2], D, self.eps, m)
        if factor != 1.0:
            m = P.v(lambda e: e.tensor_scalar(stat[:, 2:4], stat[:, 2:4], factor, None, ALU.mult), m)
        for t in range(2):
            y = Y[:, 2 * t:2 * t + 2, :].rearrange("p a b -> p (a b)")
            m1 = P.v(lambda e, t=t, y=y: e.scalar_tensor_tensor(junk[:, t, :], y, stat[:, 2 + t:3 + t], grow, ALU.mult, ALU.mult), m, m_g)
            P.g(lambda e, t=t: e.tensor_tensor(self.X[:, t, :], self.X[:, t, :], junk[:, t, :], ALU.add), m1)
        P.fence()

    def ffn(self, i, j):
        P, A, I = self.P, self.A, self.I
        at0 = A.mark()
        banks = Banks(self.ps, [0, 1, 2, 3])
        XN, junk = A.take(2, D), A.take(2, D)
        HT = A.take(8, 256)
        HA = A.take(22, 256)
        SG = A.take(4, 256)
        grow = A.take(D)
        stat = A.take(8)
        mg = P.dma("a", grow, I["norms_2"][i, 1 + 4 * j:2 + 4 * j, :].broadcast_to([128, D]))
        mh = self.pre_norm(3 * i + 2 * j, banks, XN, HT, junk, stat[:, 0:4])
        W = I["ffn_wgu_2"][i, j]
        view = lambda c: (lambda s: s.rearrange("p (k n) -> p k n", k=8)[:, :, c:c + 256])
        src = lambda c: W[:, c:c + 256].rearrange("(k p) n -> p k n", p=128)
        m_sg = [None] * 4
        m_ha = []
        for blk in range(11):
            s, w, mw = self.R.load((view(0), src(256 * blk)), (view(256), src(D_FF + 256 * blk)))
            w = w.rearrange("p (k n) -> p k n", k=8)
            for q in range(2):
                f = 2 * blk + q
                b, ps, free = banks.take()
                for u in range(2):
                    m = P.mm(ps[:, 256 * u:256 * u + 256],
                             [(w[:, k, 256 * u + 128 * q:256 * u + 128 * q + 128], HT[:, k, :]) for k in range(8)], mw, free, *mh)
                m1 = P.a(lambda e, ps=ps, f=f: e.activation(SG[:, f % 4, :], ps[:, 0:256], ACT.Silu), m, m_sg[f % 4])
                m2 = P.v(lambda e, ps=ps, f=f: e.tensor_tensor(HA[:, f, :], SG[:, f % 4, :], ps[:, 256:512], ALU.mult), m1)
                m_sg[f % 4] = m2
                banks.free(b, m2)
                m_ha.append(m2)
            self.R.free(s, m)
        Y = self.ps[:, 4:8, :]
        for k0 in range(0, 22, 4):
            nk = min(4, 22 - k0)
            s, w, mw = self.rows(I["ffn_wd_2"][i, j], k0, nk)
            for k in range(nk):
                for t in range(2):
                    for hf in range(2):
                        m = P.mm(Y[:, 2 * t + hf, :], [(HA[:, k0 + k, t * 128:(t + 1) * 128], w[:, k, hf * 512:(hf + 1) * 512])],
                                 mw, m_ha[k0 + k], start=k0 + k == 0, stop=k0 + k == 21)
            self.R.free(s, m)
        self.post_norm_add(Y, i, 1, 0.5, junk, stat[:, 4:8], [m], grow, mg)
        A.back(at0)

    def diff_attention(self, HT, mh, MT, banks):
        P, A, I = self.P, self.A, self.I
        at = A.mark()
        W = I["even_w_in_2"][0]
        QT, KT = A.take(4, 256), A.take(4, 256)
        VA = A.take(2, 512)
        OA = A.take(2, 512)
        bias = A.take(4, 384)
        lam = A.take(256)
        sub = A.take(128)
        S = A.take(2, 512)
        Pm = A.take(2, 256)
        PT = A.take(2, 256)
        stat = A.take(2, 16)
        st8 = A.take(24)
        m_b = P.dma("a", bias, I["k_dbias"].rearrange("p (a b) -> p a b", a=4))
        m_l = P.dma("a", lam, I["diff_lam_2"].rearrange("a b c -> a (b c)").broadcast_to([128, 256]))
        m_s = P.dma("a", sub, I["diff_subln_2"].broadcast_to([128, 128]))
        l4 = lam.rearrange("p (a b c) -> p a b c", a=2, b=2)
        m = P.v(lambda e: e.tensor_tensor(l4[:, :, 0, :], l4[:, :, 0, :], l4[:, :, 1, :], ALU.mult), m_l)
        m = P.v(lambda e: e.tensor_reduce(st8[:, 0:2], l4[:, :, 0, :], AX, ALU.add), m)
        m = P.a(lambda e: e.activation(st8[:, 0:2], st8[:, 0:2], ACT.Exp), m)
        m = P.v(lambda e: e.tensor_tensor(st8[:, 2:3], st8[:, 0:1], st8[:, 1:2], ALU.subtract), m)
        m_lam = P.v(lambda e: e.tensor_scalar(st8[:, 2:3], st8[:, 2:3], LAM0, None, ALU.add), m)
        m_p = []
        for c0, dst, sc in ((0, QT, 0.125), (512, KT, 1.0)):
            s, w, mw = self.cols(W, c0, 512)
            for q in range(4):
                b, ps, free = banks.take()
                m = P.mm(ps[:, 0:256], [(w[:, k, q * 128:(q + 1) * 128], HT[:, k, :]) for k in range(8)], mw, free, *mh)
                m_p.append(P.a(lambda e, ps=ps, dst=dst, q=q, sc=sc: e.activation(dst[:, q, :], ps[:, 0:256], ACT.Copy, scale=sc), m))
                banks.free(b, m_p[-1])
            self.R.free(s, m)
        s, w, mw = self.cols(W, 1024, 512)
        for t in range(2):
            b, ps, free = banks.take()
            m = P.mm(ps, [(HT[:, k, t * 128:(t + 1) * 128], w[:, k, :]) for k in range(8)], mw, free)
            m_p.append(self.evac("a", VA[:, t, :], ps, m))
            banks.free(b, m_p[-1])
        self.R.free(s, m)
        rs, rp, rt = [None] * 2, [None] * 2, [None] * 2
        m_o = None
        for t in range(2):
            n = 128 * (t + 1)
            ob = self.ps[:, 7, :]
            for h in range(4):
                u = h % 2
                sv = S[:, u, 0:2 * n].rearrange("p (a b) -> p a b", a=2)
                off = 128 * t
                for mp in range(2):
                    hp = slice(64 * mp, 64 * mp + 64)
                    b, ps, free = banks.take()
                    m = P.mm(ps[:, 0:n], [(QT[hp, h, t * 128:(t + 1) * 128], KT[hp, h, 0:n])], free, *m_p)
                    m1 = P.v(lambda e, sv=sv, ps=ps, h=h, off=off, n=n, mp=mp: e.tensor_tensor(
                        sv[:, mp, :], ps[:, 0:n], bias[:, h, off:off + n], ALU.add), m, m_b, rp[u])
                    banks.free(b, m1)
                st = stat[:, u, :]
                m1 = P.v(lambda e, sv=sv, st=st: e.tensor_reduce(st[:, 0:2], sv, AX, ALU.max), m1)
                m1 = P.v(lambda e, st=st: e.tensor_scalar(st[:, 0:2], st[:, 0:2], -1.0, None, ALU.mult), m1)
                for mp in range(2):
                    m2 = P.a(lambda e, sv=sv, st=st, mp=mp: e.activation(sv[:, mp, :], sv[:, mp, :], ACT.Exp, bias=st[:, mp:mp + 1],
                                                                        accum_out=st[:, 2 + mp:3 + mp]), m1)
                m3 = P.v(lambda e, st=st: e.reciprocal(st[:, 4:6], st[:, 2:4]), m2)
                m3 = P.v(lambda e, st=st: e.tensor_tensor(st[:, 5:6], st[:, 5:6], st8[:, 2:3], ALU.mult), m3, m_lam)
                m3 = P.v(lambda e, sv=sv, st=st: e.tensor_scalar(sv[:, 1, :], sv[:, 1, :], st[:, 5:6], None, ALU.mult), m3)
                pm = Pm[:, u, 0:n]
                m3 = P.v(lambda e, sv=sv, st=st, pm=pm: e.scalar_tensor_tensor(pm, sv[:, 0, :], st[:, 4:5], sv[:, 1, :], ALU.mult,
                                                                              ALU.subtract), m3, rs[u])
                rp[u] = m3
                b, ps, free = banks.take()
                for c in range(t + 1):
                    m4 = P.tr(ps[:, c * 128:(c + 1) * 128], pm[:, c * 128:(c + 1) * 128], self.ident, m3, free, inc=c == t)
                rs[u] = m4
                m5 = self.evac("a", PT[:, u, 0:n], ps[:, 0:n], m4, rt[u])
                banks.free(b, m5)
                m6 = P.mm(ob[:, h * 128:(h + 1) * 128], [(PT[:, u, c * 128:(c + 1) * 128], VA[:, c, h * 128:(h + 1) * 128])
                                                        for c in range(t + 1)], m5, m_o)
                rt[u] = m6
            sq = S[:, 0, :]
            m7 = P.a(lambda e, ob=ob, sq=sq: e.activation(sq, ob, ACT.Square), m6, rp[0], P.last("v"))
            s4 = st8[:, 8 + 4 * t:12 + 4 * t]
            m7 = P.v(lambda e, s4=s4, sq=sq: e.tensor_reduce(s4, sq.rearrange("p (h d) -> p h d", h=4), AX, ALU.add), m7)
            m7 = self.rstd(s4, s4, 128, self.eps, m7)
            m7 = P.v(lambda e, s4=s4: e.tensor_scalar(s4, s4, 1.0 - LAM0, None, ALU.mult), m7)
            as4 = lambda a: a.rearrange("p (h d) -> p h d", h=4)
            m_o = P.v(lambda e, ob=ob, s4=s4, t=t: e.tensor_tensor(as4(OA[:, t, :]), as4(ob), s4.unsqueeze(2).broadcast_to([128, 4, 128]),
                                                                  ALU.mult), m7)
            rp[0] = m_o
            m8 = P.v(lambda e, t=t: e.tensor_tensor(as4(OA[:, t, :]), as4(OA[:, t, :]), sub.unsqueeze(1).broadcast_to([128, 4, 128]),
                                                    ALU.mult), m_o, m_s)
        self.to_columns([OA[:, 0, :], OA[:, 1, :]], MT[:, 0:4, :], 0, None, None, banks, [m8])
        P.fence()
        A.back(at)

    def diff_rwkv_mixer(self):
        P, A, I = self.P, self.A, self.I
        at0 = A.mark()
        banks = Banks(self.ps, [0, 1, 2, 3, 4, 5, 6])
        MT = A.take(8, 256)
        grow = A.take(D)
        stat = A.take(16)
        QRf = A.take(2048)
        mg = P.dma("a", grow, I["norms_2"][0, 3:4, :].broadcast_to([128, D]))
        HT = QRf.rearrange("p (a b) -> p a b", a=8)
        at1 = A.mark()
        XN, junk = A.take(2, D), A.take(2, D)
        mh = self.pre_norm(1, banks, XN, HT, junk, stat[:, 0:4])
        P.fence()
        A.back(at1)
        self.diff_attention(HT, mh, MT, banks)
        self.rwkv(HT, QRf, MT, banks)
        A.back(at1)
        junk = A.take(2, D)
        Y = self.ps[:, 4:8, :]
        for half in range(2):
            s, w, mw = self.cols(I["even_w_out_2"][0], half * 512, 512)
            for t in range(2):
                m = P.mm(Y[:, 2 * t + half, :], [(MT[:, k, t * 128:(t + 1) * 128], w[:, k, :]) for k in range(8)], mw)
            self.R.free(s, m)
        self.post_norm_add(Y, 0, 3, 1.0, junk, stat[:, 4:8], [m], grow, mg)
        A.back(at0)

    def rwkv(self, HT, QRf, MT, banks):
        P, A, I = self.P, self.A, self.I
        W = I["even_w_in_2"][0]
        buf = [A.take(D) for _ in range(6)]
        gbuf = [A.take(D) for _ in range(4)]
        BT, KT_, BR, KR, VR, BON = (A.take(4, 256) for _ in range(6))
        XWA, XG = A.take(256), A.take(256)
        Z = A.take(2, 257)
        ups, gup = A.take(512), A.take(512)
        wm = A.take(6, 64)
        d0 = A.take(256)
        UB, SA, S = A.take(4, 64), A.take(4, 64), A.take(4, 64)
        m_c = [P.dma("a", ups[0:64, :], I["rwkv_w_up_2"][0]), P.dma("a", ups[64:128, :], I["rwkv_a_up_2"][0]),
               P.dma("a", gup, I["rwkv_g_up_2"][0]), P.dma("a", wm, I["k_wmask"].rearrange("p (a b) -> p a b", a=6))]
        for k in "tvag":
            P.queues[k].append((m_c, None, None))
        P.g(lambda e: e.memset(Z[:, :, 0:1], 0.0))
        P.g(lambda e: e.memset(d0, 1.0))
        m_z0 = P.g(lambda e: e.memset(d0.rearrange("p (a b) -> p a b", b=64)[:, :, 0:1], 0.0), P.last("g"))
        t4 = lambda a: a.rearrange("p (a b) -> p a b", a=4)
        r, k, v = t4(buf[0]), t4(buf[1]), t4(buf[2])
        dst = [r[:, i, :] for i in range(4)] + [k[:, i, :] for i in range(4)] + [v[:, i, :] for i in range(4)] + [XWA, XG]
        rz = [None, None]
        for n0, n in ((0, 4), (4, 4), (8, 4), (12, 2)):
            s, w, mw = self.cols(W, A_COLS + 128 * n0, 128 * n)
            for q in range(n):
                j = n0 + q
                z = Z[:, j % 2, :]
                b, ps, free = banks.take()
                m = P.mm(ps[:, 0:256], [(w[:, kc, q * 128:(q + 1) * 128], HT[:, kc, :]) for kc in range(8)], mw, free)
                m1 = P.a(lambda e, z=z, ps=ps: e.activation(z[:, 1:257], ps[:, 0:256], ACT.Copy), m, rz[j % 2], m_z0)
                banks.free(b, m1)
                m2 = P.v(lambda e, z=z, o=dst[j]: e.tensor_tensor(o, z[:, 0:256], z[:, 1:257], ALU.subtract), m1)
                m_zs = P.v(lambda e, z=z, o=dst[j], j=j: e.scalar_tensor_tensor(o, o, self.col("mu", 1, j), z[:, 1:257], ALU.mult, ALU.add), m2)
                rz[j % 2] = m_zs
            self.R.free(s, m)
        vec = lambda i, p: self.col("vec", 1, 4 * i + p)
        SG, AA, KK = t4(buf[3]), t4(buf[4]), t4(buf[5])
        P0, P1, PI, TM = (t4(g) for g in gbuf)
        m_th = P.a(lambda e: e.activation(XWA[0:64, :], XWA[0:64, :], ACT.Tanh), m_zs)
        m_xg = P.a(lambda e: e.activation(XG, XG, ACT.Sigmoid), m_zs)
        ms, mk = [], []
        for p in range(4):
            for lo, dd, vi, out in ((0, m_th, 0, SG), (64, m_zs, 1, AA)):
                b, ps, free = banks.take()
                m = P.mm(ps[:, 0:256], [(ups[lo:lo + 64, p * 128:(p + 1) * 128], XWA[lo:lo + 64, :])], dd, free)
                m = P.a(lambda e, ps=ps, out=out, p=p, vi=vi: e.activation(out[:, p, :], ps[:, 0:256], ACT.Sigmoid, bias=vec(vi, p)), m)
                banks.free(b, m)
                ms.append(m)
            mk.append(P.v(lambda e, p=p: e.tensor_tensor_scan(P0[:, p, :], d0, SG[:, p, :], 0.0, ALU.mult, ALU.add), ms[-2], m_z0))
        m1 = P.v(lambda e: e.tensor_tensor(P1, P0, SG, ALU.subtract), mk[-1])
        C = float(np.exp(-0.5))
        m_pi = P.a(lambda e: e.activation(PI, P0, ACT.Exp, scale=C), mk[-1])
        m_p1 = P.a(lambda e: e.activation(P1, P1, ACT.Exp, scale=-C), m1)
        m_p0 = P.a(lambda e: e.activation(P0, P0, ACT.Exp, scale=-C), m_pi)
        for p in range(4):
            m = P.v(lambda e, p=p: e.tensor_scalar(KK[:, p, :], k[:, p, :], vec(2, p), None, ALU.mult), m_zs)
        m = P.a(lambda e: e.activation(TM, KK, ACT.Square), m)
        for hf in range(2):
            b, ps, free = banks.take()
            m2 = P.mm(ps, [(self.bones, TM[:, 2 * hf:2 * hf + 2, :])], m, free)
            sl = TM[:, 2 * hf:2 * hf + 2, :].rearrange("p a b -> p (a b)")
            m3 = P.a(lambda e, ps=ps, sl=sl: e.activation(sl, ps, ACT.Sqrt), m2)
            banks.free(b, m3)
        m3 = P.v(lambda e: e.tensor_scalar(TM, TM, 1e-12, None, ALU.max), m3)
        m3 = P.v(lambda e: e.reciprocal(TM, TM), m3)
        m_kk = P.v(lambda e: e.tensor_tensor(KK, KK, TM, ALU.mult), m3)
        for p in range(4):
            m = P.v(lambda e, p=p: e.tensor_scalar(TM[:, p, :], AA[:, p, :], -1.0, vec(3, p), ALU.add, ALU.mult), m_kk, ms[-1])
        m_k = P.v(lambda e: e.scalar_tensor_tensor(k, TM, 1.0, k, ALU.add, ALU.mult), m)
        QR = QRf.rearrange("p (a c w t) -> p a c w t", a=4, c=4, w=2)
        c4 = lambda a, p: a[:, p, :].rearrange("p (c t) -> p c t", c=4)
        fence_h = P.last("t")
        for p in range(4):
            P.v(lambda e, p=p: e.tensor_tensor(QR[:, p, :, 0, :], c4(KK, p), c4(P1, p), ALU.mult), m_p1, fence_h)
            m_qr = P.v(lambda e, p=p: e.tensor_tensor(QR[:, p, :, 1, :], c4(r, p), c4(P0, p), ALU.mult), m_p0)
        PE_ = A.take(4, 4)
        m_pe = P.v(lambda e: e.tensor_copy(PE_, P0.rearrange("p a (c t) -> p a c t", c=4)[:, :, :, 63]), m_p0)
        m = P.v(lambda e: e.tensor_tensor(BT, KK, AA, ALU.mult), m_kk)
        m_bt = P.v(lambda e: e.tensor_tensor(BT, BT, PI, ALU.mult), m, m_pi)
        m_kt = P.v(lambda e: e.tensor_tensor(KT_, k, PI, ALU.mult), m_k)
        for p in range(4):
            m = P.v(lambda e, p=p: e.scalar_tensor_tensor(TM[:, p, :], r[:, p, :], vec(4, p), k[:, p, :], ALU.mult, ALU.mult), m_k)
        for hf in range(2):
            b, ps, free = banks.take()
            m2 = P.mm(ps, [(self.bones, TM[:, 2 * hf:2 * hf + 2, :])], m, free)
            m3 = P.v(lambda e, ps=ps, hf=hf: e.tensor_tensor(BON[:, 2 * hf:2 * hf + 2, :].rearrange("p a b -> p (a b)"), ps,
                                                             v[:, 2 * hf:2 * hf + 2, :].rearrange("p a b -> p (a b)"), ALU.mult), m2)
            banks.free(b, m3)
        H = [slice(0, 64), slice(64, 128)]

        def each(out, lhs, rhs, marks, width=64):
            for p in range(4):
                for h in H:
                    m = P.t(lambda e, p=p, h=h: e.matmul(out[h, p, :], lhs(h, p), rhs(h, p), start=True, stop=True, skip_group_check=True),
                            *(marks if p == 0 and h is H[0] else ()), inc=p == 3 and h is H[1])
            return m

        def product(lhs, rhs, marks, use):
            last = []
            for c0 in (0, 2):
                b, ps, free = banks.take()
                pv = ps.rearrange("p (c a b) -> p c a b", c=2, a=4)
                for c in range(2):
                    m = each(pv[:, c, :, :], lambda h, p, c=c0 + c: lhs(h, c, p), lambda h, p, c=c0 + c: rhs(h, c, p),
                             tuple(marks) + (free,))
                mm_ = use(c0, ps, m)
                banks.free(b, mm_[-1])
                last += mm_
            return last

        four = lambda a: a.rearrange("p (c a b) -> p c a b", c=4, a=4)
        half = lambda a, c0: a[:, 256 * c0:256 * c0 + 512]
        m_rows = []
        flat = lambda a: a.rearrange("p a b -> p (a b)")
        for src, out, mk_ in ((BT, flat(BR), m_bt), (KT_, flat(KR), m_kt), (v, flat(VR), m_zs)):
            m_rows += product(lambda h, c, p, src=src: src[h, p, 64 * c:64 * c + 64], lambda h, c, p: self.ident[h, h], [mk_],
                              lambda c0, ps, m, out=out: [self.evac("a", half(out, c0), ps, m)])
        P.fence()
        GB = gbuf[0].tensor[:, self.off(gbuf[0]):self.off(gbuf[0]) + 2048].rearrange("p (c a w t) -> p c a w t", c=4, a=4, w=2)
        GK = gbuf[0].tensor[:, self.off(gbuf[2]):self.off(gbuf[2]) + 2048].rearrange("p (c a w t) -> p c a w t", c=4, a=4, w=2)
        m_g = []
        for src, out in ((BT, GB), (KT_, GK)):
            for c in range(4):
                b, ps, free = banks.take()
                m = each(ps.rearrange("p (a b) -> p a b", a=4), lambda h, p, src=src, c=c: src[h, p, 64 * c:64 * c + 64],
                         lambda h, p, c=c: QR[h, p, c, :, :].rearrange("p a b -> p (a b)"), (free,))
                m = P.v(lambda e, ps=ps, out=out, c=c: e.tensor_tensor(
                    out[:, c, :, :, :].rearrange("p a w t -> p a (w t)"), ps.rearrange("p (a b) -> p a b", a=4),
                    wm[:, 0:2, :].rearrange("p a b -> p (a b)").unsqueeze(1).broadcast_to([128, 4, 128]), ALU.mult), m)
                banks.free(b, m)
                m_g.append(m)
        mask = lambda i: wm[:, i, :].unsqueeze(1).broadcast_to([128, 8, 64])
        e8 = lambda a: a.rearrange("p (a b) -> p a b", a=8)
        Ld, LdT, Lo, A2, A2T, ZT = buf

        def tiles(a):
            v4 = four(a)
            return lambda h, c, p: v4[h, c, p, :]

        m_l = product(lambda h, c, p: QR[h, p, c, 0, :], lambda h, c, p: BT[h, p, 64 * c:64 * c + 64], [],
                      lambda c0, ps, m: [P.v(lambda e: e.tensor_tensor(e8(half(Ld, c0)), e8(ps), mask(2), ALU.mult), m),
                                         P.v(lambda e: e.tensor_tensor(e8(half(Lo, c0)), e8(ps), mask(3), ALU.mult), m)])
        m_t = []
        for c in range(4):
            m = P.v(lambda e, c=c: e.tensor_tensor(four(LdT)[:, c, :, :], GB[:, c, :, 0, :],
                                                   wm[:, 5, :].unsqueeze(1).broadcast_to([128, 4, 64]), ALU.mult), *m_g)
            m_t.append(P.v(lambda e, c=c: e.tensor_tensor(four(ZT)[:, c, :, :], wm[:, 4, :].unsqueeze(1).broadcast_to([128, 4, 64]),
                                                          four(LdT)[:, c, :, :], ALU.subtract), m))

        def copy(out, k="a"):
            return lambda c0, ps, m: [self.evac(k, half(out, c0), ps, m)]

        def plus(out, base):
            return lambda c0, ps, m: [P.v(lambda e: e.tensor_tensor(half(out, c0), ps, half(base, c0), ALU.add), m)]

        mA2 = product(tiles(LdT), tiles(Ld), m_l + m_t, copy(A2))
        mA2T = product(tiles(Ld), tiles(LdT), [], copy(A2T, "v"))
        both = mA2 + mA2T
        mZ = product(tiles(A2), tiles(ZT), both, plus(ZT, ZT))
        A4, A4T = Ld, LdT
        mA4 = product(tiles(A2T), tiles(A2), both, copy(A4))
        mA4T = product(tiles(A2), tiles(A2T), [], copy(A4T))
        mZ = product(tiles(A4), tiles(ZT), mZ + mA4, plus(ZT, ZT))
        A8 = A2T
        mA8 = product(tiles(A4T), tiles(A4), mA4T, copy(A8))
        mZ = product(tiles(A8), tiles(ZT), mZ + mA8, plus(ZT, ZT))
        XX, F, FT, F2, T1, INV = Ld, LdT, A2, A2T, Lo, buf[1]
        mX = product(tiles(ZT), lambda h, c, p: self.ident[h, h], mZ, copy(XX))
        mF = product(tiles(ZT), tiles(Lo), mZ, copy(F))
        mFT = product(tiles(Lo), tiles(ZT), mZ, copy(FT, "v"))
        mF2 = product(tiles(FT), tiles(F), mF + mFT, copy(F2))
        mT = P.v(lambda e: e.tensor_tensor(T1.rearrange("p (a b) -> p a b", a=16), wm[:, 4, :].unsqueeze(1).broadcast_to([128, 16, 64]),
                                           FT.rearrange("p (a b) -> p a b", a=16), ALU.subtract), *(mF2 + mFT))
        mT = product(tiles(F2), tiles(T1), mF2 + [mT], plus(T1, T1))
        m_inv = product(tiles(XX), tiles(T1), mT + mX, copy(INV))
        INV4, BR4, KR4, VR4 = four(INV), four(flat(BR)), four(flat(KR)), four(flat(VR))
        YT = t4(buf[0])
        P.fence()
        m_s = None
        m_ub = m_sa = None
        for c in range(4):
            def group(out, terms, marks):
                for p in range(4):
                    for h in H:
                        for i, (l, q) in enumerate(terms):
                            m = P.t(lambda e, p=p, h=h, l=l, q=q, i=i: e.matmul(out[h, p, :], l(h, p), q(h, p), start=i == 0,
                                                                                stop=i == len(terms) - 1, skip_group_check=True),
                                    *(marks if p == 0 and h is H[0] and i == 0 else ()),
                                    inc=p == 3 and h is H[1] and i == len(terms) - 1)
                return m

            def bank():
                b, ps, free = banks.take()
                return b, ps[:, 0:256].rearrange("p (a b) -> p a b", a=4), free

            b, ps, free = bank()
            terms = [(lambda h, p, c=c: GK[h, c, p, 0, :], lambda h, p, c=c: VR4[h, c, p, :])]
            if c:
                terms.append((lambda h, p, c=c: QR[h, p, c, 0, :], lambda h, p: S[h, p, :]))
            m = group(ps, terms, (free, m_s))
            m_ub = P.v(lambda e, ps=ps: e.tensor_copy(UB, ps), m, m_sa)
            banks.free(b, m_ub)
            b, ps, free = bank()
            m = group(ps, [(lambda h, p, c=c: INV4[h, c, p, :], lambda h, p: UB[h, p, :])], (free, m_ub))
            m_sa = P.v(lambda e, ps=ps: e.tensor_scalar(SA, ps, -1.0, None, ALU.mult), m, P.last("t"))
            banks.free(b, m_sa)
            b, ps, free = bank()
            terms = [(lambda h, p: SA[h, p, :], lambda h, p, c=c: GB[h, c, p, 1, :]),
                     (lambda h, p, c=c: VR4[h, c, p, :], lambda h, p, c=c: GK[h, c, p, 1, :])]
            if c:
                terms.append((lambda h, p: S[h, p, :], lambda h, p, c=c: QR[h, p, c, 1, :]))
            m_y = group(ps, terms, (free, m_sa))
            m = P.a(lambda e, ps=ps, c=c: e.activation(YT[:, :, 64 * c:64 * c + 64], ps, ACT.Copy), m_y)
            banks.free(b, m)
            if c < 3:
                b, ps, free = bank()
                m = group(ps, [(lambda h, p, c=c: BR4[h, c, p, :], lambda h, p: SA[h, p, :]),
                               (lambda h, p, c=c: KR4[h, c, p, :], lambda h, p, c=c: VR4[h, c, p, :])], (free,))
                if c:
                    m = P.v(lambda e, ps=ps: e.tensor_tensor(S, S, ps, ALU.add), m, m_y)
                else:
                    m = P.v(lambda e, ps=ps: e.tensor_copy(S, ps), m)
                banks.free(b, m)
                m_s = P.v(lambda e, c=c: e.tensor_tensor(S, S, PE_[:, :, c].unsqueeze(2).broadcast_to([128, 4, 64]), ALU.mult), m)
        P.fence()
        YC, SQ = t4(buf[2]), t4(buf[3])
        for hf in range(2):
            yt, yc, sq = (a[:, 2 * hf:2 * hf + 2, :].rearrange("p a b -> p (a b)") for a in (YT, YC, SQ))
            b, ps, free = banks.take()
            m = P.mm(ps, [(self.bones, yt)], free)
            m1 = P.v(lambda e, ps=ps, yt=yt, yc=yc: e.scalar_tensor_tensor(yc, ps, -1.0 / 64, yt, ALU.mult, ALU.add), m)
            banks.free(b, m1)
            m2 = P.a(lambda e, sq=sq, yc=yc: e.activation(sq, yc, ACT.Square), m1)
            b, ps, free = banks.take()
            m3 = P.mm(ps, [(self.bones, sq)], m2, free)
            m4 = P.a(lambda e, ps=ps, sq=sq: e.activation(sq, ps, ACT.Sqrt, scale=1.0 / 64, bias=self.eps_ln), m3)
            banks.free(b, m4)
            m5 = P.v(lambda e, sq=sq: e.reciprocal(sq, sq), m4)
            m6 = P.v(lambda e, sq=sq, yc=yc: e.tensor_tensor(yc, yc, sq, ALU.mult), m5)
        for p in range(4):
            m = self.affine("v", YC[:, p, :], YC[:, p, :], vec(5, p), vec(6, p), m6)
            m = P.v(lambda e, p=p: e.tensor_tensor(YC[:, p, :], YC[:, p, :], BON[:, p, :], ALU.add), m)
            b, ps, free = banks.take()
            m2 = P.mm(ps[:, 0:256], [(gup[:, p * 128:(p + 1) * 128], XG)], free)
            m = P.v(lambda e, p=p, ps=ps: e.tensor_tensor(MT[:, 4 + p, :], YC[:, p, :], ps[:, 0:256], ALU.mult), m, m2)
            banks.free(b, m)
        P.fence()

    def off(self, a):
        return a.offset

    def retention_mixer(self):
        P, A, I = self.P, self.A, self.I
        at0 = A.mark()
        banks = Banks(self.ps, [0, 1, 2, 3])
        grow = A.take(D)
        stat = A.take(32)
        mg = P.dma("a", grow, I["norms_2"][1, 3:4, :].broadcast_to([128, D]))
        DC = A.take(4, 2, 256)
        m_dc = P.dma("a", DC, I["k_decay"].rearrange("p (a b c) -> p a b c", a=4, b=2))
        QK = A.take(16, 256)
        HT = A.take(8, 256)
        V, G = A.take(2, 2048), A.take(2, 2048)
        ST = A.take(2, 2, 256)
        junk = A.take(2, D)
        mh = self.pre_norm(4, banks, G[:, :, 0:1024], HT, junk, stat[:, 0:4])
        P.fence()
        banks = Banks(self.ps, list(range(8)))
        W = I["odd_w_in_2"][0]
        m_p = []
        for blk in range(4):
            s, w, mw = self.cols(W, blk * 512, 512)
            for q in range(4):
                j = 4 * blk + q
                b, ps, free = banks.take()
                m = P.mm(ps[:, 0:256], [(w[:, k, q * 128:(q + 1) * 128], HT[:, k, :]) for k in range(8)], mw, free)
                if j < 8:
                    m1 = self.evac("a", QK[:, j, :], ps[:, 0:256], m)
                else:
                    m1 = P.a(lambda e, ps=ps, j=j: e.activation(QK[:, j, :], ps[:, 0:256], ACT.Copy, scale=1.0 / 16), m)
                banks.free(b, m1)
                m_p.append(m1)
            self.R.free(s, m)
        for blk in range(8):
            s, w, mw = self.cols(W, 2048 + blk * 512, 512)
            for t in range(2):
                b, ps, free = banks.take()
                m = P.mm(ps, [(HT[:, k, t * 128:(t + 1) * 128], w[:, k, :]) for k in range(8)], mw, free)
                if blk < 4:
                    m1 = self.evac("v", V[:, t, blk * 512:blk * 512 + 512], ps, m)
                else:
                    m1 = P.a(lambda e, ps=ps, t=t, blk=blk: e.activation(G[:, t, (blk - 4) * 512:(blk - 3) * 512], ps, ACT.Silu), m)
                banks.free(b, m1)
                m_p.append(m1)
            self.R.free(s, m)
        P.fence()
        banks = Banks(self.ps, [0, 1, 2, 3])
        yb = Banks(self.ps, [4, 5, 6, 7])
        r_st = [None, None]
        for h in range(4):
            u = h % 2
            for sT in range(2):
                b, ps, free = banks.take()
                m = P.mm(ps[:, 0:256], [(QK[:, 8 + 2 * h + k, sT * 128:(sT + 1) * 128], QK[:, 2 * h + k, :]) for k in range(2)], free)
                m_st = P.v(lambda e, ps=ps, h=h, sT=sT, u=u: e.tensor_tensor(ST[:, u, sT, :], ps[:, 0:256], DC[:, h, sT, :], ALU.mult),
                           m, m_dc, r_st[u])
                banks.free(b, m_st)
            for t in range(2):
                b, ps, free = yb.take()
                m = P.mm(ps, [(ST[:, u, sT, t * 128:(t + 1) * 128], V[:, sT, h * 512:(h + 1) * 512]) for sT in range(t + 1)], m_st, free)
                if t == 1:
                    r_st[u] = m
                st = stat[:, 8 + 2 * h + t:9 + 2 * h + t]
                m = P.a(lambda e, ps=ps, st=st, t=t: e.activation(junk[:, t, 0:512], ps, ACT.Square, accum_out=st), m, P.last("a"))
                m = self.rstd(st, st, 512, self.eps, m)
                g = G[:, t, h * 512:(h + 1) * 512]
                m = P.v(lambda e, ps=ps, st=st, g=g: e.scalar_tensor_tensor(g, ps, st, g, ALU.mult, ALU.mult), m)
                yb.free(b, m)
        P.fence()
        self.to_columns([G[:, 0, :], G[:, 1, :]], QK, 0, None, None, banks, [])
        P.fence()
        Y = self.ps[:, 4:8, :]
        for k0 in range(0, 16, 4):
            s, w, mw = self.rows(I["odd_w_out_2"][0], k0, 4)
            for k in range(4):
                for t in range(2):
                    for hf in range(2):
                        m = P.mm(Y[:, 2 * t + hf, :], [(QK[:, k0 + k, t * 128:(t + 1) * 128], w[:, k, hf * 512:(hf + 1) * 512])],
                                 mw, start=k0 + k == 0, stop=k0 + k == 15)
            self.R.free(s, m)
        self.post_norm_add(Y, 1, 3, 1.0, junk, stat[:, 4:8], [m], grow, mg)
        A.back(at0)

    def stages(self):
        return [self.first_columns, self.even_mixer, lambda: self.moe(0), self.pool_mixer,
                lambda: self.moe(1), self.final_norm, self.second_block_memory, lambda: self.ffn(0, 0), self.diff_rwkv_mixer,
                lambda: self.ffn(0, 1), lambda: self.ffn(1, 0), self.retention_mixer, lambda: self.ffn(1, 1)]

    def program(self):
        P = self.P
        self.load_constants()
        for stage in self.stages():
            stage()
        self.write_out()

    def write_out(self):
        P = self.P
        m = [P.last(k) for k in "tvag"]
        marks = [P.dma("s", self.out[0, t * 128:(t + 1) * 128, :], self.X[:, t, :], *m) for t in range(2)]
        P.queues["s"].append((marks, None, None))

    def finish(self, ctx):
        P = self.P
        block = ctx.enter_context(self.nc.Block())

        @block.sync
        def _(e):
            P.emit("s", e)

        @block.tensor
        def _(e):
            P.emit("t", e)

        @block.vector
        def _(e):
            P.emit("v", e)

        @block.scalar
        def _(e):
            P.emit("a", e)

        @block.gpsimd
        def _(e):
            P.emit("g", e)


def build_program(nc, I, out):
    with ExitStack() as ctx:
        k = Kernel(nc, ctx, I, out)
        k.program()
        k.finish(ctx)


_BIG = ["x", "ctx", "w_mod", "b_mod", "w_in_even", "w_out_even", "g_qnorm", "g_knorm", "g_hnorm", "w_in_odd", "w_pool_grp",
        "s_pool", "w_router", "w_exp_gate", "w_exp_up", "w_exp_down", "g_final", "norms_2", "ffn_wgu_2", "ffn_wd_2",
        "even_w_in_2", "even_w_out_2", "diff_lam_2", "diff_subln_2", "rwkv_w_up_2", "rwkv_a_up_2", "rwkv_g_up_2",
        "odd_w_in_2", "odd_w_out_2"]


def _pack_columns(inp):
    a = {k: np.asarray(inp[k]) for k in ("c", "c_ctx", "g_norm1", "g_norm2", "b_mod", "norms_2", "w_conv", "b_gate",
                                         "rwkv_mu_2", "rwkv_vec_2")}
    cc = np.stack([a["c"].reshape(8, 128).T, a["c_ctx"].reshape(8, 128).T], 2).reshape(128, 16)
    g1 = a["g_norm1"].reshape(16, 128).T
    g2 = a["g_norm2"].reshape(16, 128).T
    bm = a["b_mod"].reshape(96, 128).T
    nrm = a["norms_2"].reshape(2, 6, 8, 128)[:, [0, 2, 4]].reshape(48, 128).T
    conv = a["w_conv"].reshape(24, 128).T
    bgate = np.pad(a["b_gate"].reshape(16, 1), ((0, 112), (0, 0)))
    mu = a["rwkv_mu_2"].reshape(14, 128).T
    vec = a["rwkv_vec_2"].reshape(28, 128).T
    return np.ascontiguousarray(np.concatenate([cc, g1, g2, bm, nrm, conv, bgate, mu, vec], 1))


def kernel(**inputs):
    import concourse.bacc as bacc
    from concourse.bass_utils import run_bass_kernel_spmd

    nc = bacc.Bacc("TRN2", target_bir_lowering=False, num_devices=1)
    arrays = {n: np.ascontiguousarray(inputs[n]) for n in _BIG}
    arrays["vc"] = _pack_columns(inputs)
    for n, a in shape_constants().items():
        arrays["k_" + n] = a
    aps = {}
    for n, a in arrays.items():
        aps[n] = nc.dram_tensor("in_" + n, a.shape, mybir.dt.from_np(a.dtype), kind="ExternalInput").ap()
    out = nc.dram_tensor("out_x", (1, T, D), F32, kind="ExternalOutput").ap()
    build_program(nc, aps, out)
    r = run_bass_kernel_spmd(nc, [{"in_" + n: a for n, a in arrays.items()}], core_ids=[0])
    return r.results[0]["out_x"]
```

```python
from contextlib import ExitStack

import numpy as np
import concourse.bass as bass
from concourse import mybir

F32 = mybir.dt.float32
F32R = mybir.dt.float32r
U32 = mybir.dt.uint32
ALU = mybir.AluOpType
ACT = mybir.ActivationFunctionType
AX = mybir.AxisListType.X

D = 1024
T = 256
EPS = 1e-6
NSLOT = 6
SLOT = 4096
NEG = 1e30
A_COLS = 1536
ZB = 1792
D_FF = 2816
WINDOWS = (2, 4, 8, 16)
LAM0 = 0.8 - 0.6


def column_table():
    at, n = {}, 0
    for name, k in (("cc", 16), ("g1", 16), ("g2", 16), ("bm", 96), ("nrm", 48), ("conv", 24), ("bgate", 1),
                    ("mu", 14), ("vec", 28)):
        at[name] = n
        n += k
    return at, n


def shape_constants():
    f = np.float32
    cst = {}
    p = np.arange(128)
    base = np.zeros((128, 1024), f)
    base[:, 0:128] = np.eye(128, dtype=f)
    base[:, 128:384] = np.arange(256, dtype=f)[None, :]
    base[:, 384] = p
    base[:, 385] = p + 128
    base[:, 386] = EPS
    base[:, 387] = 64e-5
    base[:, 388] = 1.0
    base[:, 400:528] = (p[:, None] // 64 == p[None, :] // 64)
    base[:, 528:656] = np.eye(128, dtype=f)[:, ::-1]
    base[:, 656:784] = 1.0
    cst["base"] = base
    rows = (np.arange(256) // 64).astype(f)
    cols = (np.arange(256) % 64).astype(f)
    inv = (10000.0 ** (-np.arange(0, 32, 2, dtype=f) / f(32))).astype(f)
    ang = np.stack([rows[:, None] * inv, cols[:, None] * inv], 1).astype(f)
    c, s = np.cos(ang).astype(f), np.sin(ang).astype(f)
    cs = np.zeros((2, 256, 2, 2, 16), f)
    cs[0] = c[:, :, None, :]
    cs[1, :, :, 0] = -s
    cs[1, :, :, 1] = s
    cst["rope"] = cs.reshape(2, 2, 128, 64).transpose(2, 0, 1, 3).reshape(128, 256).copy()
    ml = np.zeros((128, 2, 128), f)
    ml[:, 0] = np.where(p[:, None] <= p[None, :], 0.0, NEG)
    ml[:, 1] = np.where(p[:, None] >= p[None, :], 0.0, NEG)
    cst["mmask"] = ml.reshape(128, 256)
    sel = np.zeros((128, 10, 128), f)
    for d in range(2):
        for h in range(4):
            sel[8 * d + h, 8, 32 * d + h] = 1.0
            sel[8 * d + 4 + h, 9, 32 * d + h] = 1.0
            sel[32 * d + h, 4 * d + h, :] = 1.0
    cst["sel"] = sel.reshape(128, 1280)
    band = np.zeros((4, 256, 256), f)
    t = np.arange(256)
    for g, w in enumerate(WINDOWS):
        lo, hi = w // 2, w - 1 - w // 2
        a, e = np.clip(t - lo, 0, 255), np.clip(t + hi, 0, 255)
        inside = (t[:, None] >= a[None, :]) & (t[:, None] <= e[None, :])
        band[g] = inside / (e - a + 1).astype(f)[None, :] - np.eye(256, dtype=f)
    cst["band"] = band.reshape(4, 2, 128, 256).transpose(2, 0, 1, 3).reshape(128, 2048).copy()
    slopes = 2.0 ** (-2.0 * np.arange(1, 5))
    allowed = (t[None, :] // 64) <= (t[:, None] // 64)
    bias = np.where(allowed[None], -slopes[:, None, None] * np.abs(t[:, None] - t[None, :])[None], -NEG).astype(f)
    cst["dbias"] = np.concatenate([bias[:, 0:128, 0:128], bias[:, 128:256, :]], 2).transpose(1, 0, 2).reshape(128, 1536).copy()
    logg = np.log(1.0 - 2.0 ** (-5.0 - np.arange(4)))
    dist = np.abs(t[:, None] - t[None, :])
    dec = np.where(allowed[None], np.exp(logg[:, None, None] * dist[None]), 0.0).astype(f)
    cst["decay"] = dec.transpose(0, 2, 1).reshape(4, 2, 128, 256).transpose(2, 0, 1, 3).reshape(128, 2048).copy()
    q = np.arange(128) % 64
    u = np.arange(64)
    wm = np.zeros((128, 5, 64), f)
    wm[:, 0] = q[:, None] < u[None, :]
    wm[:, 1] = q[:, None] <= u[None, :]
    wm[:, 2] = (q[:, None] > u[None, :]) & (q[:, None] // 16 == u[None, :] // 16)
    wm[:, 3] = (q[:, None] // 16) > (u[None, :] // 16)
    wm[:, 4] = q[:, None] == u[None, :]
    blk = np.zeros((128, 1, 64), f)
    blk[:, 0] = (q[:, None] // 16) == (u[None, :] // 16)
    cst["wmask"] = np.concatenate([wm, blk], 1).reshape(128, 384).copy()
    return cst


CONST_NAMES = ["base", "rope", "mmask", "sel", "band", "dbias", "decay", "wmask"]


class Program:

    def __init__(self, nc, ctx):
        self.nc = nc
        self.queues = {k: [] for k in "tvags"}
        self.sems = {k: ctx.enter_context(nc.semaphore("done_" + k)) for k in "tvag"}
        self.count = {k: 0 for k in "tvag"}
        self.small = {k: [ctx.enter_context(nc.semaphore(f"small_{k}{i}")) for i in range(12)] for k in "gsa"}
        self.small_used = {k: [0] * 12 for k in "gsa"}
        self.small_n = {k: 0 for k in "gsa"}
        self.chain = None

    def put(self, k, fn, after, inc=True):
        after = [m for m in after if m is not None]
        if inc:
            self.count[k] += 1
            self.queues[k].append((after, fn, (self.sems[k], 1)))
            mark = (self.sems[k], self.count[k])
            if self.chain is not None:
                self.chain[k] = mark
            return mark
        self.queues[k].append((after, fn, None))
        return None

    def t(self, fn, *after, inc=True):
        return self.put("t", fn, after, inc)

    def v(self, fn, *after):
        return self.put("v", fn, after)

    def a(self, fn, *after):
        return self.put("a", fn, after)

    def g(self, fn, *after):
        return self.put("g", fn, after)

    def mm(self, out, pairs, *after, start=True, stop=True):
        n = len(pairs)
        mark = None
        for i, (l, r) in enumerate(pairs):
            mark = self.t(lambda e, o=out, l=l, r=r, s=start and i == 0, q=stop and i == n - 1:
                          e.matmul(o, l, r, start=s, stop=q, skip_group_check=True),
                          *(after if i == 0 else ()), inc=i == n - 1)
        return mark

    def mm3(self, out, parts, *after, start=True, stop=True):
        pairs = []
        for lh, ll, rh, rl in parts:
            pairs += [(lh, rh), (lh, rl), (ll, rh)]
        return self.mm(out, pairs, *after, start=start, stop=stop)

    def tr(self, out, src, ident, *after, inc=True):
        return self.t(lambda e: e.transpose(out, src, ident), *after, inc=inc)

    def dma(self, k, out, src, *after, **kw):
        sems, used = self.small[k], self.small_used[k]
        i = self.small_n[k] % len(sems)
        self.small_n[k] += 1
        before = (sems[i], 16 * used[i]) if used[i] else None
        used[i] += 1
        after = [m for m in list(after) + [before] if m is not None]
        self.queues[k].append((after, lambda e: e.dma_start(out, src, **kw), (sems[i], 16)))
        return (sems[i], 16 * used[i])

    def last(self, k):
        if self.chain is not None:
            return self.chain.get(k)
        return (self.sems[k], self.count[k]) if self.count[k] else None

    def fence(self):
        if self.chain is not None:
            marks = list(self.chain.values())
            for k in "tvag":
                self.queues[k].append((marks, None, None))
            return
        marks = [self.last(k) for k in "tvag"] + [(self.small[k][i], 16 * n) for k in "gsa"
                                                   for i, n in enumerate(self.small_used[k]) if n]
        for k in "tvag":
            self.queues[k].append(([m for m in marks if m is not None], None, None))

    def emit(self, k, eng):
        seen = {}
        for after, fn, inc in self.queues[k]:
            need = {}
            for sem, n in (m for m in after if m is not None):
                if n > seen.get(sem.num, 0):
                    need[sem.num] = (sem, max(n, need.get(sem.num, (sem, 0))[1]))
            for num, (sem, n) in need.items():
                eng.wait_ge(sem, n)
                seen[num] = n
            if fn is not None:
                ins = fn(eng)
                if inc is not None:
                    ins.then_inc(*inc)


class Banks:

    def __init__(self, ps, ids):
        self.ps, self.ids, self.n = ps, ids, 0
        self.freed = {i: None for i in ids}

    def take(self):
        i = self.ids[self.n % len(self.ids)]
        self.n += 1
        return i, self.ps[:, i, :], self.freed[i]

    def free(self, i, mark):
        self.freed[i] = mark


class Ring:

    def __init__(self, P, tile, ctx):
        self.P, self.tile = P, tile
        self.sems = [ctx.enter_context(P.nc.semaphore(f"slot{i}")) for i in range(NSLOT)]
        self.fills = [0] * NSLOT
        self.freed = [[] for _ in range(NSLOT)]
        self.order = list(range(NSLOT))

    def load(self, *pieces):
        i = self.order.pop(0)
        self.order.append(i)
        for k, (view, src) in enumerate(pieces):
            self.P.queues["s"].append((self.freed[i] if k == 0 else [],
                                       lambda e, o=view(self.tile[:, i, :]), s=src: e.dma_start(o, s),
                                       (self.sems[i], 16)))
            self.fills[i] += 16
        return i, self.tile[:, i, :], (self.sems[i], self.fills[i])

    def free(self, i, mark):
        self.freed[i] = [mark]

    def lend_free(self, n, busy):
        slots = [i for i in self.order if i not in busy][:n]
        self.order = [i for i in self.order if i not in slots]
        return slots, [self.tile[:, i, :] for i in slots], [m for i in slots for m in self.freed[i]]

    def give_back(self, slots):
        marks = [m for m in (self.P.last(k) for k in "tvag") if m]
        for i in slots:
            self.freed[i] = marks
            self.order.append(i)

    def lend(self, n):
        self.order = [i for i in self.order if i < NSLOT - n]
        marks = [m for i in range(NSLOT - n, NSLOT) for m in self.freed[i]]
        return self.tile[:, NSLOT - n:NSLOT, :].rearrange("p a b -> p (a b)"), marks

    def restore(self):
        marks = [m for m in (self.P.last(k) for k in "tvag") if m]
        for i in range(NSLOT):
            if i not in self.order:
                self.freed[i] = marks
                self.order.append(i)


def interleave(P, *gens):
    gens = [(g, {}) for g in gens]
    while gens:
        for g in list(gens):
            P.chain = g[1]
            try:
                next(g[0])
            except StopIteration:
                gens.remove(g)
    P.chain = None


def after_steps(n, gen):
    for _ in range(n):
        yield
    yield from gen


class Arena:
    def __init__(self, tile, n, tile_r):
        self.tile, self.n, self.at = tile, n, 0
        self.tile_r = tile_r
        self.extra = []

    def take(self, *shape):
        n = int(np.prod(shape))
        for area in self.extra:
            if area[1] + n <= area[0].shape[1]:
                area[1] += n
                return self.shaped(area[0][:, area[1] - n:area[1]], shape)
        a = self.tile[:, self.at:self.at + n]
        self.at += n
        assert self.at <= self.n, (self.at, self.n)
        return self.shaped(a, shape)

    def take_r(self, *shape):
        at = self.at
        a = self.take(*shape)
        return a, self.shaped(self.tile_r[:, at:self.at], shape)

    def shaped(self, a, shape):
        if len(shape) == 2:
            a = a.rearrange("p (a b) -> p a b", a=shape[0])
        elif len(shape) == 3:
            a = a.rearrange("p (a b c) -> p a b c", a=shape[0], b=shape[1])
        elif len(shape) == 4:
            a = a.rearrange("p (a b c d) -> p a b c d", a=shape[0], b=shape[1], c=shape[2])
        return a

    def borrow(self, *extra):
        self.extra = [[a, 0] for a in extra]

    def mark(self):
        return self.at

    def back(self, at):
        self.at = at


class Kernel:
    def __init__(self, nc, ctx, I, out):
        self.nc, self.I, self.out = nc, I, out
        self.P = Program(nc, ctx)
        total = 53200 - NSLOT * SLOT
        at = -(-nc.sbuf_base // 32) * 32
        ring = ctx.enter_context(nc.sbuf_tensor("ring", [128, NSLOT * SLOT], F32))
        self.ring_r = nc.alloc_sbuf_tensor_at("ring_r", [128, NSLOT * SLOT], F32R, offset=at)
        at += 4 * NSLOT * SLOT
        big = ctx.enter_context(nc.sbuf_tensor("big", [128, total], F32))
        self.big_r = nc.alloc_sbuf_tensor_at("big_r", [128, total], F32R, offset=at)
        self.ps = ctx.enter_context(nc.psum_tensor("ps", [128, 8, 512], F32))
        self.R = Ring(self.P, ring[:, :].rearrange("p (a b) -> p a b", a=NSLOT), ctx)
        self.A = Arena(big, total, self.big_r)

    def evac(self, k, out, src, *after):
        if k == "v":
            return self.P.v(lambda e: e.tensor_copy(out, src), *after)
        return self.P.a(lambda e: e.activation(out, src, ACT.Copy), *after)

    def affine(self, k, out, src, scale, bias, *after):
        if k == "v":
            if bias is None:
                return self.P.v(lambda e: e.tensor_scalar(out, src, scale, None, ALU.mult), *after)
            return self.P.v(lambda e: e.tensor_scalar(out, src, scale, bias, ALU.mult, ALU.add), *after)
        if bias is None:
            return self.P.a(lambda e: e.activation(out, src, ACT.Copy, scale=scale), *after)
        return self.P.a(lambda e: e.activation(out, src, ACT.Identity, scale=scale, bias=bias), *after)

    def rstd(self, out, sums, n, eps, *after):
        m = self.P.a(lambda e: e.activation(out, sums, ACT.Sqrt, scale=1.0 / n, bias=eps), *after)
        return self.P.v(lambda e: e.reciprocal(out, out), m)

    def rms_rows(self, srcs, outs, junk, stat, after):
        P = self.P
        marks = []
        n = len(srcs)
        for i, (s, j) in enumerate(zip(srcs, junk)):
            marks.append(P.a(lambda e, s=s, j=j, i=i: e.activation(j, s, ACT.Square, accum_out=stat[:, i:i + 1]),
                             *after[i]))
        m = self.rstd(stat[:, n:2 * n], stat[:, 0:n], D, self.eps, *marks)
        return [P.v(lambda e, s=s, o=o, i=i: e.tensor_scalar(o, s, stat[:, n + i:n + i + 1], None, ALU.mult), m)
                for i, (s, o) in enumerate(zip(srcs, outs))]

    def to_columns(self, rows, dst, off, scale, bias, banks, after):
        P = self.P
        marks = []
        nk = dst.shape[1]
        for kc in range(0, nk, 2):
            b, ps, free = banks.take()
            for u in range(2):
                for tt in range(2):
                    m = P.tr(ps[:, (2 * u + tt) * 128:(2 * u + tt + 1) * 128],
                             rows[tt][:, (kc + u) * 128:(kc + u + 1) * 128], self.ident, free, *after,
                             inc=(u == 1 and tt == 1))
            ms = []
            if scale is None:
                ms.append(self.evac("va"[kc // 2 % 2], dst[:, kc:kc + 2, off:off + 256],
                                    ps.rearrange("p (a b) -> p a b", a=2), m))
            else:
                for u in range(2):
                    ms.append(self.affine("va"[kc // 2 % 2], dst[:, kc + u, off:off + 256],
                                          ps[:, u * 256:(u + 1) * 256], scale(kc + u),
                                          None if bias is None else bias(kc + u), m))
            banks.free(b, ms[-1])
            marks += ms
        return marks

    def to_column_parts(self, rows, hi_r, lo_r, scale, banks, after):
        P = self.P
        marks = []
        for kc in range(0, hi_r.shape[1], 2):
            b, ps, free = banks.take()
            for u in range(2):
                for tt in range(2):
                    m = P.tr(ps[:, (2 * u + tt) * 128:(2 * u + tt + 1) * 128],
                             rows[tt][:, (kc + u) * 128:(kc + u + 1) * 128], self.ident, free, *after,
                             inc=(u == 1 and tt == 1))
            both = [(kc + u, ps[:, u * 256:(u + 1) * 256], 1.0 if scale is None else scale(kc + u)) for u in range(2)]
            for k, p, sc in both:
                m1 = P.a(lambda e, k=k, p=p, sc=sc: e.activation(hi_r[:, k, :], p, ACT.Copy, scale=sc), m)
            for k, p, sc in both:
                m2 = P.v(lambda e, k=k, p=p, sc=sc: e.scalar_tensor_tensor(lo_r[:, k, :], p, sc, hi_r[:, k, :].bitcast(F32),
                                                                           ALU.mult, ALU.subtract), m1)
            banks.free(b, m2)
            marks.append(m2)
        return marks

    def split(self, src, hi_r, lo_r, *after):
        m = self.P.a(lambda e: e.activation(hi_r, src, ACT.Copy), *after)
        return self.P.v(lambda e: e.tensor_tensor(lo_r, src, hi_r.bitcast(F32), ALU.subtract), m)

    def start_parts(self, loads):
        self.R.lend(2)
        self.part_loads = loads
        self.part_at = 0
        self.part_free = [None, None]
        self.part_ready = []
        self.prepare_parts()

    def prepare_parts(self):
        if self.part_at == len(self.part_loads):
            return
        n, pieces = self.part_loads[self.part_at]
        u = self.part_at % 2
        self.part_at += 1
        i, s, m = self.R.load(*pieces)
        flat = lambda t, at: t[:, at:at + SLOT]
        hi_r = flat(self.ring_r, (4 + u) * SLOT)
        lo_r = flat(self.ring_r, i * SLOT)
        for q in range(2):
            sl = slice(q * n // 2, (q + 1) * n // 2)
            mark = self.split(s[:, sl], hi_r[:, sl], lo_r[:, sl], m, self.part_free[u])
        self.part_ready.append((i, u, hi_r[:, 0:n], lo_r[:, 0:n], mark))

    def parts(self, k):
        i, u, hi, lo, mark = self.part_ready.pop(0)
        self.prepare_parts()
        view = lambda a: a.rearrange("p (k n) -> p k n", k=k)
        return (i, u), view(hi), view(lo), mark

    def free_parts(self, s, mark):
        self.R.free(s[0], mark)
        self.part_free[s[1]] = mark

    def cols(self, W, c0, n):
        view = lambda s: s[:, 0:8 * n].rearrange("p (k n) -> p k n", k=8)
        i, s, m = self.R.load((view, W[0:1024, c0:c0 + n].rearrange("(k p) n -> p k n", p=128)))
        return i, view(s), m

    def rows(self, W, k0, nk):
        view = lambda s: s[:, 0:nk * 1024].rearrange("p (k n) -> p k n", k=nk)
        i, s, m = self.R.load((view, W[k0 * 128:(k0 + nk) * 128, 0:1024].rearrange("(k p) n -> p k n", p=128)))
        return i, view(s), m

    def load_constants(self):
        P, A, I = self.P, self.A, self.I
        self.X = A.take(2, D)
        base = A.take(1024)
        self.col_at, ncol = column_table()
        self.vc = A.take(ncol)
        m = [P.dma("s", self.vc, I["vc"]), P.dma("s", base, I["k_base"])]
        self.m_x = [P.dma("a", self.X[:, i, :], I["x"][0, i * 128:(i + 1) * 128, :]) for i in range(2)]
        self.ident = base[:, 0:128]
        self.iota = base[:, 128:384]
        self.iota_p = [base[:, 384:385], base[:, 385:386]]
        self.eps = base[:, 386:387]
        self.eps_ln = base[:, 387:388]
        self.onecol = base[:, 388:389]
        self.bones = base[:, 400:528]
        self.ones = base[:, 656:784]
        self.keep = A.mark()
        self.load_routers()
        self.gate = A.take(2, D)
        self.colm = [A.take(48, 2) for _ in range(2)]
        self.AC = [A.take(2, 8, 2) for _ in range(2)]
        self.PR = A.take(2, 512)
        self.sc = A.take(8, 32)
        for k in "tvag":
            P.queues[k].append((m, None, None))
        m = P.v(lambda e: e.memset(self.sc, 0.0))
        self.m_sc = P.a(lambda e: e.activation(self.sc[:, :, 0:2], self.col("cc", 16).rearrange("p (k t) -> p k t", t=2), ACT.Silu), m)
        self.mod_bank = Banks(self.ps, [7])
        self.mod_rows = [None, None]
        self.mod_n = 0
        self.mod_work = []

    def col(self, name, n, off=0):
        a = self.col_at[name] + off
        return self.vc[:, a:a + n]

    def adaln_block(self, i, blk):
        P, I = self.P, self.I
        s, w, mw = self.cols(I["w_mod"][i], blk * 512, 512)
        b, ps, free = self.mod_bank.take()
        for g in range(2):
            for j in range(4):
                k = 4 * g + j
                m = P.t(lambda e, j=j, k=k, g=g, w=w, ps=ps: e.matmul(ps[32 * j:32 * j + 32, :], self.sc[:, k, :], w[:, k, :], start=g == 0,
                                                                      stop=g == 1, skip_group_check=True),
                        *((mw, free, self.m_sc) if k == 0 else ()), inc=k == 7)
        self.R.free(s, m)
        u = self.mod_n % 2
        self.mod_n += 1
        row = self.PR[:, u, :]
        m = P.v(lambda e, ps=ps, row=row: e.tensor_copy(row, ps), m, self.mod_rows[u])
        for q in range(4):
            mt = P.tr(ps[:, 128 * q:128 * q + 128], row[:, 128 * q:128 * q + 128], self.ident, m, inc=q == 3)
        self.mod_rows[u] = mt
        out = self.colm[i][:, 4 * blk:4 * blk + 4, :]
        view = ps.rearrange("p (q j t) -> p q t j", q=4, j=4)[:, :, 0:2, :]
        m = P.v(lambda e, out=out, view=view: e.tensor_reduce(out, view, AX, ALU.add), mt)
        self.mod_bank.free(b, m)
        bias = self.col("bm", 4, 48 * i + 4 * blk).unsqueeze(2).broadcast_to([128, 4, 2])
        return P.v(lambda e, out=out, bias=bias: e.tensor_tensor(out, out, bias, ALU.add), m)

    def norm_columns(self, i, w, marks):
        P = self.P
        c = self.colm[i]
        g = self.col("g1" if w == 0 else "g2", 8, 8 * i).unsqueeze(2).broadcast_to([128, 8, 2])
        m = P.v(lambda e: e.scalar_tensor_tensor(self.AC[i][:, w, :, :], c[:, 24 * w + 8:24 * w + 16, :], 1.0, g, ALU.add, ALU.mult),
                *marks)
        return [m]

    def gate_rows(self, i, which, banks, marks):
        P = self.P
        for hf in range(2):
            b, ps, free = banks.take()
            for q in range(4):
                t = 24 * which + 16 + 4 * hf + q
                m = P.mm(ps[:, 128 * q:128 * q + 128], [(self.colm[i][:, t, 0:1].broadcast_to([128, 128]), self.ident)], free, *marks)
            m = self.evac("av"[hf], self.gate[:, which, 512 * hf:512 * hf + 512], ps, m)
            banks.free(b, m)

    def set_layer(self, i):
        self.layer = i
        self.B = lambda w, kc, t: self.colm[i][:, 24 * w + kc, t:t + 1]
        self.Ac = lambda w, kc, t: self.AC[i][:, w, kc, t:t + 1]

    def first_columns(self):
        for blk in range(4):
            m = self.adaln_block(0, blk)
        self.m_mod = self.norm_columns(0, 0, [m])
        self.set_layer(0)
        self.mod_work = [(0, b) for b in range(4, 12)] + [(1, b) for b in range(12)]

    def fill(self, n=1):
        for _ in range(n):
            if self.mod_work:
                self.adaln_block(*self.mod_work.pop(0))

    def even_mixer(self):
        P, A, I = self.P, self.A, self.I
        banks = Banks(self.ps, [0, 1, 2, 3, 4, 5])
        at0 = A.mark()
        stat = A.take(96)
        rope = A.take(2, 2, 64)
        mmask = A.take(2, 128)
        sel = A.take(10, 128)
        grow = A.take(2, 64)
        ghn = A.take(512)
        QK = A.take(8, 512)
        V1 = A.take(4, 4, 129)
        OB = A.take(2, 512)
        QA = A.take(2, 512)
        KA = A.take(4, 2, 2, 64)
        VA = A.take(4, 128)
        G16 = A.take(512)
        at1 = A.mark()
        HT = A.take(8, 512)
        at2 = A.mark()
        XN = A.take(2, D)
        CTX = A.take(2, D)
        junk = QK[:, 0:4, :].rearrange("p (a b) c -> p a (b c)", a=2)
        m_ctx = [P.dma("a", CTX[:, i, :], I["ctx"][0, i * 128:(i + 1) * 128, :]) for i in range(2)]
        m_c = [P.dma("a", rope, I["k_rope"].rearrange("p (a b c) -> p a b c", a=2, b=2)),
               P.dma("a", mmask, I["k_mmask"].rearrange("p (a b) -> p a b", a=2)),
               P.dma("a", sel, I["k_sel"].rearrange("p (a b) -> p a b", a=10)),
               P.dma("a", grow[:, 0, :], I["g_qnorm"][0:1, :].broadcast_to([128, 64])),
               P.dma("a", grow[:, 1, :], I["g_knorm"][0:1, :].broadcast_to([128, 64])),
               P.dma("a", ghn, I["g_hnorm"][0:1, :].broadcast_to([128, 512]))]
        rows = lambda t: [t[:, 0, :], t[:, 1, :]]
        m = self.rms_rows(rows(self.X), rows(XN), rows(junk), stat[:, 0:4], [(x,) for x in self.m_x])
        mc = self.rms_rows(rows(CTX), rows(CTX), rows(junk), stat[:, 4:8], [(x, m[1]) for x in m_ctx])
        P.queues["s"].append((m_ctx, None, None))
        self.first_columns()
        m_h = self.to_columns(rows(XN), HT, 256, lambda k: self.Ac(0, k, 0), lambda k: self.B(0, k, 0), banks,
                              m + self.m_mod)
        m_h += self.to_columns(rows(CTX), HT, 0, lambda k: self.Ac(0, k, 1), lambda k: self.B(0, k, 1), banks, mc)
        W = I["w_in_even"][0]
        for k in "tvag":
            P.queues[k].append((m_c, None, None))
        P.fence()

        def row_form(c0, n, tiles, use):
            s, w, mw = self.cols(W, c0, n)
            for t in tiles:
                b, ps, free = banks.take()
                m = P.mm(ps[:, 0:n], [(HT[:, k, t * 128:(t + 1) * 128], w[:, k, :]) for k in range(8)], mw, free)
                banks.free(b, use(t, ps, m))
                if t == tiles[-1]:
                    self.R.free(s, m)
                yield

        s, w, mw = self.cols(W, 2816, 16)
        b, ps, free = banks.take()
        m = P.mm(ps[0:16, :], [(w[:, k, :], HT[:, k, :]) for k in range(8)], mw, free)
        self.R.free(s, m)
        m_g16 = P.v(lambda e, ps=ps: e.tensor_scalar(G16[0:16, :], ps[0:16, :], self.col("bgate", 1)[0:16, :], None, ALU.add), m)
        banks.free(b, m_g16)

        A.back(at2)
        RAW = A.take(8, 512)
        m_qk = [None] * 8
        for c0, base, lo in ((1280, 4, 0), (768, 0, 256)):
            s, w, mw = self.cols(W, c0, 512)
            for q in range(4):
                j = base + q
                b, ps, free = banks.take()
                n = 512 - lo
                m = P.mm(ps[:, 0:n], [(w[:, k, q * 128:(q + 1) * 128], HT[:, k, lo:512]) for k in range(8)], mw, free)
                m_raw = self.evac("a", RAW[:, j, lo:512], ps[:, 0:n], m)
                banks.free(b, m_raw)
                w0, w1, w2 = (self.col("conv", 1, 8 * i + j) for i in range(3))
                sv = RAW[:, j, lo:512].rearrange("p (a b) -> p a b", b=256)
                dv = QK[:, j, lo:512].rearrange("p (a b) -> p a b", b=256)
                m1 = P.v(lambda e, s=sv, d=dv, w=w1: e.tensor_scalar(d, s, w, None, ALU.mult), m_raw)
                m1 = P.v(lambda e, s=sv, d=dv, w=w0: e.scalar_tensor_tensor(d[:, :, 1:256], s[:, :, 0:255], w, d[:, :, 1:256],
                                                                            ALU.mult, ALU.add), m1)
                m1 = P.v(lambda e, s=sv, d=dv, w=w2: e.scalar_tensor_tensor(d[:, :, 0:255], s[:, :, 1:256], w, d[:, :, 0:255],
                                                                            ALU.mult, ALU.add), m1)
                m_qk[j] = P.a(lambda e, d=dv: e.activation(d, d, ACT.Silu), m1)
                if j >= 4:
                    m_qk[j] = P.g(lambda e, j=j: e.tensor_scalar(QK[:, j, :], QK[:, j, :], 128.0 ** -0.5, None, ALU.mult), m_qk[j])
            self.R.free(s, m)
        m_one = P.g(lambda e: e.memset(V1[:, :, :, 128:129], 1.0))
        m_v1 = {}

        def use_v(t, ps, m):
            m_v1[t] = self.evac("a", V1[:, t, :, 0:128], ps.rearrange("p (h d) -> p h d", h=4), m)
            return m_v1[t]

        def use_o(t, ps, m):
            return P.a(lambda e: e.activation(OB[:, t - 2, :], ps, ACT.Sigmoid), m)

        m_kv = {}

        def use_kv(t, ps, m):
            P.v(lambda e: e.tensor_copy(KA[:, t, :, 0, :], ps[:, 0:128].rearrange("p (h d) -> p h d", h=2)), m)
            m_kv[t] = P.v(lambda e: e.tensor_copy(VA[:, t, :], ps[:, 128:256]), m)
            return m_kv[t]

        def use_q(t, ps, m):
            m_kv[t + 2] = self.evac("a", QA[:, t - 2, :], ps, m)
            return m_kv[t + 2]

        lent, _ = self.R.lend(3)
        P.fence()
        A.back(at2)
        MT = A.take(8, 256)
        A.borrow(lent)
        abanks = Banks(self.ps, [4, 5])

        def attention():
            yield from row_form(512, 256, range(4), use_kv)
            yield from row_form(0, 512, (2, 3), use_q)
            yield from row_form(2304, 512, (2, 3), use_o)
            yield from self.attention(QA, KA, VA, stat, rope, grow, MT, abanks, list(m_kv.values()))

        def modulation():
            while self.mod_work:
                self.fill()
                for _ in range(3):
                    yield
            self.gate_rows(0, 0, self.mod_bank, [P.last("v")])
            yield
            self.gate_rows(0, 1, self.mod_bank, [P.last("v")])
            yield
            self.norm_columns(0, 1, [P.last("v")])
            for w in range(2):
                self.m_mod = self.norm_columns(1, w, [P.last("v")])

        banks = Banks(self.ps, [4, 5])
        interleave(P, self.mlstm_gates(G16, sel, QK), row_form(1792, 512, range(4), use_v))
        parts = self.gate_parts
        parts["marks"] += list(m_v1.values()) + [m_one]
        interleave(P, attention(), self.mlstm(0, parts, QK, V1, mmask, sel), self.mlstm(1, parts, QK, V1, mmask, sel), modulation())
        P.fence()
        banks = Banks(self.ps, [0, 1, 2, 3, 4, 5])
        self.mlstm_out(parts, OB, stat, ghn, MT, banks)
        P.fence()
        A.borrow()
        self.R.restore()
        tmp = A.take(2, 512)
        W = I["w_out_even"][0]
        for half in range(2):
            s, w, mw = self.cols(W, half * 512, 512)
            for t in range(2):
                b, ps, free = banks.take()
                sl = slice(half * 512, half * 512 + 512)
                m = P.mm(ps, [(MT[:, k, t * 128:(t + 1) * 128], w[:, k, :]) for k in range(8)], mw, free)
                m1 = P.v(lambda e, ps=ps, t=t, sl=sl: e.tensor_tensor(tmp[:, t, :], ps, self.gate[:, 0, sl], ALU.mult),
                         m, P.last("g"))
                banks.free(b, m1)
                P.g(lambda e, t=t, sl=sl: e.tensor_tensor(self.X[:, t, sl], self.X[:, t, sl], tmp[:, t, :], ALU.add), m1)
            self.R.free(s, m)
        P.fence()
        A.back(at0)

    def mlstm_gates(self, G16, sel, QK):
        P, A = self.P, self.A
        banks = Banks(self.ps, [0, 1, 2, 3])
        IG, LF, BB = (A.take(512) for _ in range(3))
        MM = G16
        P.g(lambda e: e.memset(IG, 0.0))
        mz = P.g(lambda e: e.memset(LF, 0.0))
        flip = lambda a: a.rearrange("p (c t) -> p c t", c=2)[:, :, ::-1]
        for which, dst in ((8, IG), (9, LF)):
            b, ps, free = banks.take()
            m = P.mm(ps[0:64, :], [(sel[0:16, which, 0:64], G16[0:16, :])], free)
            P.v(lambda e, ps=ps, d=dst: e.tensor_copy(d[0:4, :], ps[0:4, :]), m, mz)
            mf = P.v(lambda e, ps=ps, d=dst: e.tensor_copy(d[32:36, :].rearrange("p (c t) -> p c t", c=2), flip(ps[32:36, :])), m, mz)
            banks.free(b, mf)
        yield
        R = slice(0, 36)
        m = P.v(lambda e: e.scalar_tensor_tensor(BB[R, :], LF[R, :], -1.0, LF[R, :], ALU.mult, ALU.max), mf)
        m = P.a(lambda e: e.activation(BB[R, :], BB[R, :], ACT.Exp, scale=-1.0), m)
        m = P.a(lambda e: e.activation(BB[R, :], BB[R, :], ACT.Ln, bias=self.onecol[R, :]), m)
        m = P.v(lambda e: e.scalar_tensor_tensor(LF[R, :], LF[R, :], 0.0, BB[R, :], ALU.min, ALU.subtract), m)
        yield
        m = P.v(lambda e: e.tensor_tensor_scan(BB[R, :], self.onecol[R, :].broadcast_to([36, 512]), LF[R, :], 0.0, ALU.mult, ALU.add), m)
        m = P.v(lambda e: e.tensor_tensor(IG[R, :], IG[R, :], BB[R, :], ALU.subtract), m)
        m = P.v(lambda e: e.tensor_tensor_scan(MM[R, :], IG[R, :], IG[R, :], -NEG, ALU.max, ALU.max), m)
        m = P.v(lambda e: e.tensor_tensor(LF[R, :], MM[R, :], BB[R, :], ALU.add), m)
        for src, dst in ((IG, BB), (MM, IG), (LF, MM)):
            P.v(lambda e, s=src, o=dst: e.tensor_copy(o[0:4, :], s[0:4, :]), m)
            m = P.v(lambda e, s=src, o=dst: e.tensor_copy(o[32:36, :].rearrange("p (c t) -> p c t", c=2), flip(s[32:36, :])), m)
        m_mb = P.v(lambda e: e.tensor_copy(LF[0:1, 0:1], LF[0:1, 0:1]), m)
        GC = A.take(4, 36)
        EM = A.take(4, 36)
        marks = [m_mb]
        for src, dst in ((BB, GC), (MM, EM)):
            yield
            b, ps, free = banks.take()
            for c in range(4):
                m = P.tr(ps[:, c * 36:c * 36 + 36], src[R, c * 128:(c + 1) * 128], self.ident[0:36, 0:36], free, m_mb, inc=c == 3)
            if dst is GC:
                m = P.v(lambda e, ps=ps: e.tensor_copy(GC, ps[:, 0:144].rearrange("p (a b) -> p a b", a=4)), m)
            else:
                m = P.a(lambda e, ps=ps: e.activation(EM, ps[:, 0:144].rearrange("p (a b) -> p a b", a=4), ACT.Exp, scale=-1.0), m)
            marks.append(m)
            banks.free(b, m)
        KR = A.take(4, 4, 128)
        for c in range(4):
            b, ps, free = banks.take()
            for h in range(4):
                m = P.tr(ps[:, h * 128:(h + 1) * 128], QK[:, 4 + h, c * 128:(c + 1) * 128], self.ident, free, inc=h == 3)
            m = self.evac("av"[c % 2], KR[:, :, c, :], ps.rearrange("p (h d) -> p h d", h=4), m)
            marks.append(m)
            banks.free(b, m)
        HO = A.take(2, 2, 512)
        own = [dict(CS=A.take(2, 129), ME=A.take(2, 4), W2=A.take(8), DN=A.take(8), WS=A.take(2, 8), DT=A.take(2, 128), ST=A.take(2, 128),
                    QS=A.take(2, 128), KW=A.take(2, 128), bc=self.ps[:, 2 * d, :], work=Banks(self.ps, [2 * d + 1])) for d in range(2)]
        self.gate_parts = dict(GC=GC, EM=EM, KR=KR, HO=HO, MX=IG, marks=marks, own=own, LF=LF)

    def mlstm(self, d, parts, QK, V1, mmask, sel):
        P = self.P
        GC, EM, KR, HO, MX, ready = (parts[k] for k in ("GC", "EM", "KR", "HO", "MX", "marks"))
        o = parts["own"][d]
        CS, ME, W2, DN, WS, DT, ST, QS, KW, bc, work = (o[k] for k in ("CS", "ME", "W2", "DN", "WS", "DT", "ST", "QS", "KW", "bc", "work"))
        order = [[0, 1, 2, 3], [1, 0, 3, 2]][d]
        qt = lambda h, c: QK[:, h, c * 128:(c + 1) * 128]
        kt = lambda h, c: QK[:, 4 + h, c * 128:(c + 1) * 128]
        R = slice(0, 36)
        w_free = [None, None]
        t_st = [None, None]
        t_kw = [None, None]
        t_cs = [None, None]
        bc_free = []
        a_w2 = None
        for h in range(4):
            r = 32 * d + h
            m = P.mm(bc, [(sel[R, 4 * d + h, :], MX[R, :])], *bc_free, *ready)
            me = ME[:, h % 2, :]
            m_me = P.v(lambda e, me=me: e.tensor_copy(me, bc.rearrange("p (c t) -> p c t", c=4)[:, :, 0 if d else 127]), m, *bc_free)
            yield
            mw = P.v(lambda e, r=r, me=me: e.tensor_tensor(W2[:, 0:4], GC[:, :, r], me, ALU.subtract), m_me, a_w2)
            for c in (1, 2):
                p0, p1 = order[c - 1], order[c]
                mw = P.v(lambda e, c=c, p0=p0, p1=p1, me=me: e.tensor_tensor(
                    W2[:, 3 + c:4 + c], me[:, p0:p0 + 1], me[:, p1:p1 + 1], ALU.subtract), m_me, a_w2)
            w = WS[:, h % 2, :]
            m_w = a_w2 = P.a(lambda e, w=w: e.activation(w[:, 0:6], W2[:, 0:6], ACT.Exp), mw, w_free[h % 2])
            m_dt, m_qs = {}, {}
            for c in (2, 3):
                oc, u, pe = order[c], c % 2, order[c - 1]
                dt, qs, bcc = DT[:, u, :], QS[:, u, :], bc[:, oc * 128:(oc + 1) * 128]
                m1 = P.v(lambda e, oc=oc, r=r, dt=dt, bcc=bcc: e.scalar_tensor_tensor(
                    dt, bcc, GC[:, oc, r:r + 1], mmask[:, d, :], ALU.subtract, ALU.max), m_me)
                m4 = P.a(lambda e, qs=qs, bcc=bcc, me=me, pe=pe: e.activation(qs, bcc, ACT.Exp, scale=-1.0, bias=me[:, pe:pe + 1]),
                         m_me, t_st[u], m1)
                m_dt[u] = P.a(lambda e, dt=dt: e.activation(dt, dt, ACT.Exp, scale=-1.0), m1)
                m_qs[u] = P.v(lambda e, h=h, oc=oc, qs=qs: e.tensor_tensor(qs, qs, qt(h, oc), ALU.mult), m4)
                bc_free = [m1, m4]
                yield
            m_state = None
            for c in range(4):
                oc = order[c]
                cs = CS[:, c % 2, :]
                pc = CS[:, (c + 1) % 2, :]
                if c >= 2:
                    u = c % 2
                    dt, st, qs = DT[:, u, :], ST[:, u, :], QS[:, u, :]
                    b, ps, free = work.take()
                    m2 = P.mm(ps[:, 0:128], [(kt(h, oc), qt(h, oc))], free)
                    m3 = P.v(lambda e, ps=ps, dt=dt, st=st: e.tensor_tensor(st, dt, ps[:, 0:128], ALU.mult), m_dt[u], m2, t_st[u])
                    yield
                    m6 = P.mm(ps[:, 256:385], [(st, V1[:, oc, h, :]), (qs, pc)], m3, m_qs[u], m_state)
                    t_st[u] = m6
                    t_cs[(c + 1) % 2] = m6
                    dn = DN[:, 4 * u:4 * u + 1]
                    m7 = P.v(lambda e, ps=ps, dn=dn, oc=oc, r=r: e.tensor_scalar(dn, ps[:, 384:385], -1.0, EM[:, oc, r:r + 1], ALU.mult, ALU.max),
                             m6)
                    m7 = P.v(lambda e, ps=ps, dn=dn: e.tensor_tensor(dn, dn, ps[:, 384:385], ALU.max), m7)
                    m7 = P.v(lambda e, dn=dn: e.reciprocal(dn, dn), m7)
                    m8 = P.v(lambda e, ps=ps, dn=dn, h=h, oc=oc: e.tensor_scalar(
                        HO[:, d, oc - 2, h * 128:(h + 1) * 128], ps[:, 256:384], dn, None, ALU.mult), m7)
                    work.free(b, m8)
                    yield
                if c < 3:
                    kw = KW[:, c % 2, :]
                    m1 = P.v(lambda e, h=h, oc=oc, w=w, kw=kw: e.tensor_scalar(kw, KR[:, h, oc, :], w[:, oc:oc + 1], None, ALU.mult),
                             m_w, t_kw[c % 2])
                    b, ps, free = work.take()
                    m2 = P.mm(ps[:, 0:129], [(kw, V1[:, oc, h, :])], m1, free)
                    t_kw[c % 2] = m2
                    if c == 0:
                        m_state = P.v(lambda e, ps=ps, cs=cs: e.tensor_copy(cs, ps[:, 0:129]), m2, t_cs[0])
                    else:
                        m_state = P.v(lambda e, ps=ps, cs=cs, pc=pc, c=c, w=w: e.scalar_tensor_tensor(
                            cs, pc, w[:, 3 + c:4 + c], ps[:, 0:129], ALU.mult, ALU.add), m2, m_state, t_cs[c % 2])
                    w_free[h % 2] = m_state
                    work.free(b, m_state)
                    yield

    def mlstm_out(self, parts, OB, stat, ghn, MT, banks):
        P = self.P
        HO, KR, sq = parts["HO"], parts["KR"], parts["LF"]
        HM = KR.rearrange("p a b c -> p (a b c)")[:, 0:1024].rearrange("p (a b) -> p a b", a=2)
        as4 = lambda a: a.rearrange("p (h d) -> p h d", h=4)
        m1 = None
        for t in range(2):
            m = P.v(lambda e, t=t: e.tensor_tensor(HM[:, t, :], HO[:, 0, t, :], HO[:, 1, t, :], ALU.add))
            s4 = stat[:, 16 + 8 * t:20 + 8 * t]
            m1 = P.a(lambda e, t=t: e.activation(sq, HM[:, t, :], ACT.Square), m, P.last("v"))
            m2 = P.v(lambda e, s4=s4: e.tensor_reduce(s4, as4(sq), AX, ALU.add), m1)
            m3 = self.rstd(s4, s4, 128, self.eps, m2)
            m4 = P.v(lambda e, t=t, s4=s4: e.tensor_tensor(as4(HM[:, t, :]), as4(HM[:, t, :]), s4.unsqueeze(2).broadcast_to([128, 4, 128]),
                                                           ALU.mult), m3)
            m5 = P.v(lambda e, t=t: e.tensor_tensor(HM[:, t, :], HM[:, t, :], ghn, ALU.mult), m4)
            m_hm = P.v(lambda e, t=t: e.tensor_tensor(HM[:, t, :], HM[:, t, :], OB[:, t, :], ALU.mult), m5)
        self.to_columns([HM[:, 0, :], HM[:, 1, :]], MT[:, 4:8, :], 0, None, None, banks, [m_hm])

    def attention(self, QA, KA, VA, stat, rope, grow, MT, banks, ready):
        P, A = self.P, self.A
        KT = A.take(2, 512)
        QT = A.take(8, 256)
        SP_ = MT[:, 4:8, :].rearrange("p (a b) c -> p a (b c)", a=2)
        PT = A.take(4, 256)
        sq, t1, t2 = SP_[:, 0, :], SP_[:, 1, :], PT[:, 0:2, :].rearrange("p a b -> p (a b)")
        mx = A.take(16)
        sm = A.take(16)
        m_z = P.g(lambda e: e.memset(QT, 0.0))
        kview = lambda t: KA[:, t, :, 0, :]
        qview = lambda t: QA[:, t, :].rearrange("p (h d) -> p h d", h=8)
        m_fin = []
        m_prev = None
        for which, (view, heads, tiles, lat) in enumerate(((qview, 8, (0, 1), (0, 1)), (kview, 2, (0, 1, 2, 3), (2, 3)))):
            for t in tiles:
                x = view(t)
                n = heads * 64
                as3 = lambda a, heads=heads, n=n: a[:, 0:n].rearrange("p (h d) -> p h d", h=heads)
                st = stat[:, 32:32 + heads]
                m = P.a(lambda e, x=x, as3=as3: e.activation(as3(sq), x, ACT.Square), m_prev, *ready)
                m = P.v(lambda e, as3=as3, st=st: e.tensor_reduce(st, as3(sq), AX, ALU.add), m, m_prev)
                m = self.rstd(st, st, 64, self.eps, m)
                yield
                m = P.v(lambda e, x=x, st=st, heads=heads: e.tensor_tensor(x, x, st.unsqueeze(2).broadcast_to([128, heads, 64]), ALU.mult), m)
                m = P.v(lambda e, x=x, heads=heads, which=which: e.tensor_tensor(
                    x, x, grow[:, which:which + 1, :].broadcast_to([128, heads, 64]), ALU.mult), m)
                if t in lat:
                    lt = t - lat[0]
                    cosv, sinv = rope[:, 0, lt, :], rope[:, 1, lt, :]
                    ma = P.g(lambda e, x=x, as3=as3, c=cosv, heads=heads: e.tensor_tensor(
                        as3(t1), x, c.unsqueeze(1).broadcast_to([128, heads, 64]), ALU.mult), m)
                    for half in range(2):
                        mb = P.v(lambda e, x=x, as3=as3, s=sinv, heads=heads, half=half: e.tensor_tensor(
                            as3(t2).rearrange("p h (a b c) -> p h a b c", a=2, b=2)[:, :, :, half, :],
                            x.rearrange("p h (a b c) -> p h a b c", a=2, b=2)[:, :, :, 1 - half, :],
                            s.rearrange("p (a b c) -> p a b c", a=2, b=2)[:, :, half, :].unsqueeze(1).broadcast_to([128, heads, 2, 16]),
                            ALU.mult), m)
                    m = P.v(lambda e, x=x, as3=as3: e.tensor_tensor(x, as3(t1), as3(t2), ALU.add), ma, mb)
                if which == 1:
                    m = P.v(lambda e, t=t: e.tensor_copy(KA[:, t, :, 1, :], KA[:, t, :, 0, :]), m)
                m_prev = m
                m_fin.append(m)
                yield
        mq, mk = [], []
        for p in range(4):
            b, ps, free = banks.take()
            for t in range(2):
                m = P.tr(ps[:, t * 128:(t + 1) * 128], QA[:, t, p * 128:(p + 1) * 128], self.ident, free, m_fin[1], inc=t == 1)
            mq.append(self.evac("a", QT[0:64, 2 * p, :], ps[0:64, 0:256], m, m_z))
            mq.append(self.evac("a", QT[64:128, 2 * p + 1, :], ps[64:128, 0:256], m, m_z))
            banks.free(b, mq[-1])
            yield
        for kv in range(2):
            b, ps, free = banks.take()
            for t in range(4):
                m = P.tr(ps[:, t * 128:(t + 1) * 128], KA[:, t, kv, :, :].rearrange("p a d -> p (a d)"), self.ident, free,
                         *m_fin, inc=t == 3)
            mk.append(self.evac("v", KT[:, kv, :], ps, m))
            banks.free(b, mk[-1])
            yield
        r_sp, r_pt = [None, None], None
        ob = self.ps[:, 6, :]
        m_ob = None
        for h in range(8):
            kv = h // 4
            for t in range(2):
                i = 8 * t + h
                sp = SP_[:, t, :]
                b, ps, free = banks.take()
                m = P.mm(ps, [(QT[:, h, t * 128:(t + 1) * 128], KT[:, kv, :])], free, *(mq + mk))
                m1 = P.v(lambda e, ps=ps, i=i: e.tensor_reduce(mx[:, i:i + 1], ps, AX, ALU.max), m)
                m1 = P.v(lambda e, i=i: e.tensor_scalar(mx[:, i:i + 1], mx[:, i:i + 1], -0.125, None, ALU.mult), m1)
                m2 = P.a(lambda e, ps=ps, i=i, sp=sp: e.activation(sp, ps, ACT.Exp, scale=0.125, bias=mx[:, i:i + 1],
                                                                   accum_out=sm[:, i:i + 1]), m1, r_sp[t])
                yield
                m3 = P.v(lambda e, i=i: e.reciprocal(sm[:, i:i + 1], sm[:, i:i + 1]), m2)
                m3 = P.v(lambda e, i=i, sp=sp: e.tensor_scalar(sp, sp, sm[:, i:i + 1], None, ALU.mult), m3)
                for c in range(4):
                    m4 = P.tr(ps[:, c * 128:(c + 1) * 128], sp[:, c * 128:(c + 1) * 128], self.ident, m3, inc=c == 3)
                r_sp[t] = m4
                m5 = self.evac("va"[t], PT[:, :, t * 128:(t + 1) * 128], ps.rearrange("p (c t) -> p c t", c=4), m4, r_pt)
                banks.free(b, m5)
                if t == 0:
                    m_p0 = m5
                yield
            hp = slice(64 * (h % 2), 64 * (h % 2) + 64)
            r_pt = P.mm(ob[hp, 0:256], [(VA[:, c, kv * 64:(kv + 1) * 64], PT[:, c, :]) for c in range(4)], m5, m_p0, m_ob)
            m_ob = self.evac("v", MT[hp, h // 2, :], ob[hp, 0:256], r_pt)
            yield

    def moe(self, i):
        P, A, I = self.P, self.A, self.I
        at0 = A.mark()
        banks = Banks(self.ps, [0, 1, 2, 3, 4, 5])
        rows = lambda t: [t[:, 0, :], t[:, 1, :]]
        XS = A.take(8, 512)
        GR = A.take(16, 256)
        XN = A.take(2, D)
        at_h = A.mark()
        HT = A.take(8, 256)
        _, PN = A.take_r(2, 512)
        _, XH = A.take_r(2, D)
        _, XL = A.take_r(2, D)
        AF = A.take(2, 16)
        stat = A.take(24)
        CUR = A.take(2, 256)
        VL = A.take(32)
        IX = A.take(32)
        IF = A.take(32)
        REP = A.take(128)
        MI = A.take(16, 32)
        IC = A.take(16)
        VCOL = A.take(16)
        WR, m_wr = self.router[i]
        m = self.rms_rows(rows(self.X), rows(XN), [XS[:, 0:2, :].rearrange("p a b -> p (a b)"), XS[:, 2:4, :].rearrange("p a b -> p (a b)")],
                          stat[:, 0:4], [(), ()])
        m_xn = list(m)
        mh = self.to_columns(rows(XN), HT, 0, lambda k: self.Ac(1, k, 0), lambda k: self.B(1, k, 0), banks, m + self.m_mod)
        for t in range(2):
            m_xn.append(self.split(XN[:, t, :], XH[:, t, :], XL[:, t, :], *m_xn[0:2]))
        b, lg, free = banks.take()
        ms = []
        for t in range(2):
            ms.append(P.mm(lg[:, 16 * t:16 * t + 16], [(HT[:, k, t * 128:(t + 1) * 128], WR[:, k, :]) for k in range(8)], free, m_wr, *mh))
        m = P.v(lambda e: e.tensor_reduce(stat[:, 8:10], lg[:, 0:32].rearrange("p (t e) -> p t e", t=2), AX, ALU.max), *ms)
        m = P.v(lambda e: e.tensor_scalar(stat[:, 10:12], stat[:, 8:10], -1.0, None, ALU.mult), m)
        for t in range(2):
            me = P.a(lambda e, t=t: e.activation(AF[:, t, :], lg[:, 16 * t:16 * t + 16], ACT.Exp, bias=stat[:, 10 + t:11 + t],
                                                 accum_out=stat[:, 12 + t:13 + t]), m)
        banks.free(b, me)
        m = P.v(lambda e: e.reciprocal(stat[:, 14:16], stat[:, 12:14]), me)
        m = P.v(lambda e: e.tensor_tensor(AF, AF, stat[:, 14:16].unsqueeze(2).broadcast_to([128, 2, 16]), ALU.mult), m)
        b, ps, free = banks.take()
        for t in range(2):
            m2 = P.tr(ps[0:16, t * 128:(t + 1) * 128], AF[:, t, :], self.ident, free, m, inc=t == 1)
        E = slice(0, 16)
        m = P.v(lambda e, ps=ps: e.tensor_copy(CUR[E, 0, :], ps[E, 0:256]), m2)
        banks.free(b, m)
        for r in range(4):
            cur, nxt = CUR[E, r % 2, :], CUR[E, (r + 1) % 2, :]
            v8 = VL[E, 8 * r:8 * r + 8]
            i8 = IX[E, 8 * r:8 * r + 8].bitcast(U32)
            mv = P.v(lambda e, v8=v8, cur=cur: e.max(v8, cur), m)
            P.v(lambda e, v8=v8, cur=cur, i8=i8: e.max_index(i8, v8, cur), mv)
            m = P.v(lambda e, v8=v8, cur=cur, nxt=nxt: e.match_replace(nxt, v8, cur, -1.0), mv)
        m = P.v(lambda e: e.tensor_copy(IF[E, :], IX[E, :].bitcast(U32)), P.last("v"))
        for src, dst in ((IF, IC), (VL, VCOL)):
            m1 = P.v(lambda e, src=src: e.tensor_copy(REP[E, :].rearrange("p (a b) -> p a b", a=4),
                                                      src[E, :].unsqueeze(1).broadcast_to([16, 4, 32])), m, P.last("t"))
            b, ps2, free = banks.take()
            m2 = P.tr(ps2[:, 0:16], REP[E, :], self.ident[E, 0:16], free, m1)
            m_ic = P.v(lambda e, dst=dst, ps2=ps2: e.tensor_copy(dst, ps2[:, 0:16]), m2)
            banks.free(b, m_ic)
        m1 = P.v(lambda e: e.tensor_tensor(MI[E, :, :], IF[E, :].unsqueeze(1).broadcast_to([16, 16, 32]),
                                           self.ident[E, 0:16].unsqueeze(2).broadcast_to([16, 16, 32]), ALU.mult), m)
        b, ps3, free = banks.take()
        m2 = P.mm(ps3, [(self.ones[E, :], MI[E, :, :].rearrange("p a b -> p (a b)"))], m1, free)
        for t in range(2):
            m_p = P.v(lambda e, t=t: e.tensor_scalar(PN[:, t, :], ps3, self.iota_p[t], None, ALU.is_equal), m2)
        banks.free(b, m_p)
        for k in range(8):
            b, ps, free = banks.take()
            c = slice(k * 128, (k + 1) * 128)
            m = P.mm(ps, [(x[:, t, c], PN[:, t, :]) for t in range(2) for x in (XH, XL)], m_p, free, *m_xn)
            m_xs = self.affine("av"[k % 2], XS[:, k, :], ps, self.Ac(1, k, 0), self.B(1, k, 0), m)
            banks.free(b, m_xs)
        m_ready = [P.last("a"), P.last("v"), *banks.freed.values()]
        for e_ in range(16):
            m_gr = P.v(lambda e, n=e_: e.tensor_scalar(GR[:, n, :], self.iota, IC[:, n:n + 1], VCOL[:, n:n + 1],
                                                       ALU.is_equal, ALU.mult), m_ic)
        if i == 0:
            self.load_pool_constants()
        A.back(at_h)
        SG = A.take(256)
        AA = A.take(256)
        AT = A.take(2, 4, 32)
        OS = A.take(D)
        GU = [self.ps[:, 0, 0:256], self.ps[:, 1, 0:256]]
        TR = self.ps[:, 0, 256:512]
        O = [self.ps[:, 2, :], self.ps[:, 3, :]]
        Y = self.ps[:, 4:8, :]
        P.queues["t"].append((m_ready, None, None))
        free_gu = free_tr = None
        free_o = ()
        m_comb = None
        pend = None

        def combine(n, *mo):
            for t in range(2):
                for hf in range(2):
                    m = P.mm(Y[:, 2 * t + hf, :], [(GR[:, n, t * 128:(t + 1) * 128], OS[:, hf * 512:(hf + 1) * 512])], m_gr, *mo,
                             start=n == 0, stop=n == 15)
            return m

        for n in range(16):
            for which, name in enumerate(("w_exp_gate", "w_exp_up")):
                for hk in range(2):
                    s, w, mw = self.rows(I[name][i, n], 4 * hk, 4)
                    for k in range(4):
                        for j in range(4):
                            first = k == 0 and j == 0
                            m = P.t(lambda e, j=j, k=k, hk=hk, w=w, which=which, n=n: e.matmul(
                                GU[which][32 * j:32 * j + 32, :], XS[:, 4 * hk + k, 32 * n:32 * n + 32],
                                w[:, k, 256 * j:256 * j + 256], start=hk == 0 and k == 0, stop=hk == 1 and k == 3, skip_group_check=True),
                                *((mw, free_gu) if first else ()), inc=k == 3 and j == 3)
                    self.R.free(s, m)
                if which == 0:
                    mg = P.a(lambda e: e.activation(SG, GU[0], ACT.Silu), m, P.last("v"))
                    if pend is not None:
                        m_comb = combine(*pend)
            ma = P.v(lambda e: e.tensor_tensor(AA, SG, GU[1], ALU.mult), mg, m, P.last("t"))
            free_gu = ma
            for hh in range(2):
                mt = P.tr(TR[:, 128 * hh:128 * hh + 128], AA[:, 128 * hh:128 * hh + 128], self.ident, ma, free_tr, inc=hh == 1)
            m_at = self.evac("v", AT.rearrange("p a b c -> p (a b c)"), TR, mt)
            free_tr = m_at
            for hk in range(2):
                s, w, mw = self.rows(I["w_exp_down"][i, n], 4 * hk, 4)
                for hf in range(2):
                    for j in range(4):
                        kk = 4 * hk + j
                        m = P.t(lambda e, j=j, hf=hf, hk=hk, w=w, kk=kk: e.matmul(
                            O[hf][32 * j:32 * j + 32, :], AT[:, kk % 2, kk // 2, :], w[:, j, 512 * hf:512 * hf + 512],
                            start=hk == 0, stop=hk == 1, skip_group_check=True),
                            *((mw, m_at, *free_o) if j == 0 else ()), inc=hf == 1 and j == 3)
                self.R.free(s, m)
            m1 = P.a(lambda e: e.activation(OS[:, 0:512], O[0], ACT.Copy), m, m_comb)
            m2 = P.v(lambda e: e.tensor_copy(OS[:, 512:1024], O[1]), m, m_comb)
            free_o = (m1, m2)
            pend = (n, m1, m2)
        m = combine(*pend)
        P.fence()
        A.back(at0)
        tmp = A.take(2, 2, 512)
        for t in range(2):
            for hf in range(2):
                sl = slice(512 * hf, 512 * hf + 512)
                m1 = P.v(lambda e, t=t, hf=hf, sl=sl: e.tensor_tensor(tmp[:, t, hf, :], Y[:, 2 * t + hf, :], self.gate[:, 1, sl], ALU.mult), m)
                P.g(lambda e, t=t, hf=hf, sl=sl: e.tensor_tensor(self.X[:, t, sl], self.X[:, t, sl], tmp[:, t, hf, :], ALU.add), m1)
        P.fence()
        A.back(at0)

    def load_routers(self):
        self.router = []
        for i in range(2):
            WR = self.A.take(8, 16)
            self.router.append((WR, self.P.dma("a", WR, self.I["w_router"][i].rearrange("(k p) e -> p k e", p=128))))

    def load_pool_constants(self):
        P, A, I = self.P, self.A, self.I
        at = A.mark()
        P.queues["a"].append(([P.last("t"), P.last("v"), P.last("g")], None, None))
        A.back(A.n - 5120)
        BD = A.take(4, 2, 256)
        WG = A.take(4, 2, 256)
        SPG = A.take(D)
        A.back(at)
        self.pool_constants = (BD, WG, SPG, P.dma("a", BD, I["k_band"].rearrange("p (a b c) -> p a b c", a=4, b=2)),
                               P.dma("a", WG, I["w_pool_grp"][0].rearrange("g (k p) n -> p g k n", p=128)),
                               P.dma("a", SPG, I["s_pool"][0:1, :].broadcast_to([128, D])))

    def pool_mixer(self):
        P, A, I = self.P, self.A, self.I
        self.set_layer(1)
        at0 = A.mark()
        banks = Banks(self.ps, list(range(8)))
        self.gate_rows(1, 0, banks, [])
        self.gate_rows(1, 1, banks, [])
        m_gate = [P.last("a"), P.last("v")]
        rows = lambda t: [t[:, 0, :], t[:, 1, :]]
        XN = A.take(2, D)
        HT = A.take(8, 256)
        U = A.take(2, D)
        PT = A.take(8, 256)
        stat = A.take(8)
        BD, WG, SPG, m_bd, m_wg, m_sp = self.pool_constants
        m_sg = P.v(lambda e: e.tensor_tensor(SPG, SPG, self.gate[:, 0, :], ALU.mult), m_sp, *m_gate)
        m = self.rms_rows(rows(self.X), rows(XN), rows(U), stat[:, 0:4], [(), ()])
        mh = self.to_columns(rows(XN), HT, 0, lambda k: self.Ac(0, k, 0), lambda k: self.B(0, k, 0), banks, m + self.m_mod)
        for half in range(2):
            s, w, mw = self.cols(I["w_in_odd"][0], half * 512, 512)
            for t in range(2):
                b, ps, free = banks.take()
                m = P.mm(ps, [(HT[:, k, t * 128:(t + 1) * 128], w[:, k, :]) for k in range(8)], mw, free, *mh)
                m_u = self.evac("av"[t], U[:, t, half * 512:half * 512 + 512], ps, m)
                banks.free(b, m_u)
            self.R.free(s, m)
        marks = [P.last("v"), P.last("a")]
        mp = []
        for c in range(0, 8, 2):
            b, ps, free = banks.take()
            for u in range(2):
                m = P.mm(ps[:, 256 * u:256 * u + 256], [(U[:, t, (c + u) * 128:(c + u + 1) * 128], BD[:, c // 2, t, :]) for t in range(2)],
                         free, m_bd, *marks)
            mp.append(self.evac("av"[c // 2 % 2], PT[:, c:c + 2, :], ps.rearrange("p (a b) -> p a b", a=2), m))
            banks.free(b, mp[-1])
        for t in range(2):
            for g2 in range(2):
                b, ps, free = banks.take()
                for u in range(2):
                    g = 2 * g2 + u
                    m = P.mm(ps[:, 256 * u:256 * u + 256], [(PT[:, 2 * g + k, t * 128:(t + 1) * 128], WG[:, g, k, :]) for k in range(2)],
                             free, m_wg, *mp)
                sl = slice(512 * g2, 512 * g2 + 512)
                tmp = XN[:, t, sl]
                m1 = P.v(lambda e, ps=ps, sl=sl, tmp=tmp: e.tensor_tensor(tmp, ps, SPG[:, sl], ALU.mult), m, m_sg)
                banks.free(b, m1)
                P.g(lambda e, t=t, sl=sl, tmp=tmp: e.tensor_tensor(self.X[:, t, sl], self.X[:, t, sl], tmp, ALU.add), m1)
        P.fence()
        A.back(at0)

    def final_norm(self):
        P, A, I = self.P, self.A, self.I
        at0 = A.mark()
        g = A.take(D)
        junk = A.take(2, D)
        stat = A.take(4)
        mg = P.dma("a", g, I["g_final"].rearrange("(a n) -> a n", a=1).broadcast_to([128, D]))
        rows = lambda t: [t[:, 0, :], t[:, 1, :]]
        m = self.rms_rows(rows(self.X), rows(junk), rows(junk), stat, [(), ()])
        for t in range(2):
            P.v(lambda e, t=t: e.tensor_tensor(self.X[:, t, :], junk[:, t, :], g, ALU.mult), mg, m[t])
        P.fence()
        A.back(at0)

    def second_block_memory(self):
        self.A.back(self.keep)
        I = self.I
        loads = []

        def cols(W, c0, n):
            loads.append((8 * n, [(lambda s, n=n: s[:, 0:8 * n].rearrange("p (k n) -> p k n", k=8),
                                   W[0:1024, c0:c0 + n].rearrange("(k p) n -> p k n", p=128))]))

        def rows(W, k0, nk):
            loads.append((1024 * nk, [(lambda s, nk=nk: s[:, 0:nk * 1024].rearrange("p (k n) -> p k n", k=nk),
                                       W[k0 * 128:(k0 + nk) * 128, 0:1024].rearrange("(k p) n -> p k n", p=128))]))

        def ffn(i, j):
            W = I["ffn_wgu_2"][i, j]
            view = lambda c: (lambda s: s.rearrange("p (k n) -> p k n", k=8)[:, :, c:c + 256])
            src = lambda c: W[:, c:c + 256].rearrange("(k p) n -> p k n", p=128)
            for blk in range(11):
                loads.append((SLOT, [(view(0), src(256 * blk)), (view(256), src(D_FF + 256 * blk))]))
            for k0 in range(0, 22, 4):
                rows(I["ffn_wd_2"][i, j], k0, min(4, 22 - k0))

        def mixer0():
            for c0 in (0, 512, 1024, 1536, 2048, 2560):
                cols(I["even_w_in_2"][0], c0, 512)
            cols(I["even_w_in_2"][0], 3072, 256)
            for half in range(2):
                cols(I["even_w_out_2"][0], half * 512, 512)

        def mixer1():
            for blk in range(12):
                cols(I["odd_w_in_2"][0], blk * 512, 512)
            for k0 in range(0, 16, 4):
                rows(I["odd_w_out_2"][0], k0, 4)

        for f in (lambda: ffn(0, 0), mixer0, lambda: ffn(0, 1), lambda: ffn(1, 0), mixer1, lambda: ffn(1, 1)):
            f()
        self.start_parts(loads)
        self.m_tile = [None, None]

    def pre_norm(self, at, banks, XN, HT, junk, stat):
        rows = lambda t: [t[:, 0, :], t[:, 1, :]]
        m = []
        for t in range(2):
            m += self.rms_rows([self.X[:, t, :]], [XN[:, t, :]], [junk[:, t, :]], stat[:, 2 * t:2 * t + 2], [(self.m_tile[t],)])
        return self.to_column_parts(rows(XN), *HT, lambda k: self.col("nrm", 1, 8 * at + k), banks, m)

    def post_norm_add(self, Y, layer, k, factor, junk, stat, m_y, grow, m_g):
        P = self.P
        for t in range(2):
            y = Y[:, 2 * t:2 * t + 2, :].rearrange("p a b -> p (a b)")
            st = stat[:, 2 + t:3 + t]
            m = P.a(lambda e, t=t, y=y: e.activation(junk[:, t, :], y, ACT.Square, accum_out=stat[:, t:t + 1]), m_y[t])
            m = self.rstd(st, stat[:, t:t + 1], D, self.eps, m)
            if factor != 1.0:
                m = P.v(lambda e, st=st: e.tensor_scalar(st, st, factor, None, ALU.mult), m)
            m = P.v(lambda e, t=t, y=y, st=st: e.scalar_tensor_tensor(junk[:, t, :], y, st, grow, ALU.mult, ALU.mult), m, m_g)
            self.m_tile[t] = P.v(lambda e, t=t: e.tensor_tensor(self.X[:, t, :], self.X[:, t, :], junk[:, t, :], ALU.add), m)

    def ffn(self, i, j):
        P, A, I = self.P, self.A, self.I
        at0 = A.mark()
        banks = Banks(self.ps, [0, 1, 2, 3])
        XN, junk = A.take(2, D), A.take(2, D)
        _, HH = A.take_r(8, 256)
        _, HL = A.take_r(8, 256)
        _, AH = A.take_r(22, 256)
        _, AL = A.take_r(22, 256)
        SG = A.take(4, 256)
        grow = A.take(D)
        stat = A.take(8)
        mg = P.dma("g", grow, I["norms_2"][i, 1 + 4 * j:2 + 4 * j, :].broadcast_to([128, D]), P.last("v"))
        mh = self.pre_norm(3 * i + 2 * j, banks, XN, (HH, HL), junk, stat[:, 0:4])
        m_sg = [None] * 4
        m_ha = []
        for blk in range(11):
            s, wh, wl, mw = self.parts(8)
            for q in range(2):
                f = 2 * blk + q
                b, ps, free = banks.take()
                for u in range(2):
                    c = slice(256 * u + 128 * q, 256 * u + 128 * q + 128)
                    m = P.mm3(ps[:, 256 * u:256 * u + 256], [(wh[:, k, c], wl[:, k, c], HH[:, k, :], HL[:, k, :]) for k in range(8)],
                              mw, free, *mh)
                sg = SG[:, f % 4, :]
                m1 = P.a(lambda e, ps=ps, sg=sg: e.activation(sg, ps[:, 0:256], ACT.Silu), m, m_sg[f % 4])
                m2 = P.v(lambda e, ps=ps, sg=sg: e.tensor_tensor(sg, sg, ps[:, 256:512], ALU.mult), m1)
                banks.free(b, m2)
                m2 = P.a(lambda e, sg=sg, f=f: e.activation(AH[:, f, :], sg, ACT.Copy), m2)
                m2 = P.g(lambda e, sg=sg, f=f: e.tensor_tensor(AL[:, f, :], sg, AH[:, f, :].bitcast(F32), ALU.subtract), m2)
                m_sg[f % 4] = m2
                m_ha.append(m2)
            self.free_parts(s, m)
        Y = self.ps[:, 4:8, :]
        for k0 in range(0, 22, 4):
            nk = min(4, 22 - k0)
            s, wh, wl, mw = self.parts(nk)
            order = [(k, t) for k in range(nk) for t in range(2)] if k0 + nk < 22 else [(k, t) for t in range(2) for k in range(nk)]
            m_y = [None, None]
            for k, t in order:
                for hf in range(2):
                    r, c = slice(t * 128, (t + 1) * 128), slice(hf * 512, (hf + 1) * 512)
                    m = m_y[t] = P.mm3(Y[:, 2 * t + hf, :], [(AH[:, k0 + k, r], AL[:, k0 + k, r], wh[:, k, c], wl[:, k, c])],
                                       mw, m_ha[k0 + k], start=k0 + k == 0, stop=k0 + k == 21)
            self.free_parts(s, m)
        self.post_norm_add(Y, i, 1, 0.5, junk, stat[:, 4:8], m_y, grow, mg)
        A.back(at0)

    def diff_attention(self, HT, mh, MT, banks):
        P, A, I = self.P, self.A, self.I
        HH, HL = HT
        QT, KT = A.take(4, 256), A.take(4, 256)
        VA = A.take(2, 512)
        OA = A.take(2, 512)
        bias = A.take(4, 384)
        lam = A.take(256)
        sub = A.take(128)
        S = A.take(2, 512)
        Pm = A.take(2, 256)
        PT = A.take(2, 256)
        stat = A.take(2, 16)
        st8 = A.take(24)
        m_b = P.dma("a", bias, I["k_dbias"].rearrange("p (a b) -> p a b", a=4))
        m_l = P.dma("a", lam, I["diff_lam_2"].rearrange("a b c -> a (b c)").broadcast_to([128, 256]))
        m_s = P.dma("a", sub, I["diff_subln_2"].broadcast_to([128, 128]))
        l4 = lam.rearrange("p (a b c) -> p a b c", a=2, b=2)
        m = P.v(lambda e: e.tensor_tensor(l4[:, :, 0, :], l4[:, :, 0, :], l4[:, :, 1, :], ALU.mult), m_l)
        m = P.v(lambda e: e.tensor_reduce(st8[:, 0:2], l4[:, :, 0, :], AX, ALU.add), m)
        m = P.a(lambda e: e.activation(st8[:, 0:2], st8[:, 0:2], ACT.Exp), m)
        m = P.v(lambda e: e.tensor_tensor(st8[:, 2:3], st8[:, 0:1], st8[:, 1:2], ALU.subtract), m)
        m_lam = P.v(lambda e: e.tensor_scalar(st8[:, 2:3], st8[:, 2:3], LAM0, None, ALU.add), m)
        m_p = []
        for dst, sc in ((QT, 0.125), (KT, 1.0)):
            s, wh, wl, mw = self.parts(8)
            for q in range(4):
                b, ps, free = banks.take()
                c = slice(q * 128, (q + 1) * 128)
                m = P.mm3(ps[:, 0:256], [(wh[:, k, c], wl[:, k, c], HH[:, k, :], HL[:, k, :]) for k in range(8)], mw, free, *mh)
                m_p.append(P.a(lambda e, ps=ps, dst=dst, q=q, sc=sc: e.activation(dst[:, q, :], ps[:, 0:256], ACT.Copy, scale=sc), m))
                banks.free(b, m_p[-1])
            self.free_parts(s, m)
        s, wh, wl, mw = self.parts(8)
        for t in range(2):
            b, ps, free = banks.take()
            r = slice(t * 128, (t + 1) * 128)
            m = P.mm3(ps, [(HH[:, k, r], HL[:, k, r], wh[:, k, :], wl[:, k, :]) for k in range(8)], mw, free)
            m_p.append(self.evac("a", VA[:, t, :], ps, m))
            banks.free(b, m_p[-1])
        self.free_parts(s, m)
        yield
        rs, rp, rt = [None] * 2, [None] * 2, [None] * 2
        m_o = None
        for t in range(2):
            n = 128 * (t + 1)
            ob = self.ps[:, 7, :]
            for h in range(4):
                u = h % 2
                sv = S[:, u, 0:2 * n].rearrange("p (a b) -> p a b", a=2)
                off = 128 * t
                for mp in range(2):
                    hp = slice(64 * mp, 64 * mp + 64)
                    b, ps, free = banks.take()
                    m = P.mm(ps[:, 0:n], [(QT[hp, h, t * 128:(t + 1) * 128], KT[hp, h, 0:n])], free, *m_p)
                    m1 = P.v(lambda e, sv=sv, ps=ps, h=h, off=off, n=n, mp=mp: e.tensor_tensor(
                        sv[:, mp, :], ps[:, 0:n], bias[:, h, off:off + n], ALU.add), m, m_b, rp[u])
                    banks.free(b, m1)
                yield
                st = stat[:, u, :]
                m1 = P.v(lambda e, sv=sv, st=st: e.tensor_reduce(st[:, 0:2], sv, AX, ALU.max), m1)
                m1 = P.v(lambda e, st=st: e.tensor_scalar(st[:, 0:2], st[:, 0:2], -1.0, None, ALU.mult), m1)
                for mp in range(2):
                    m2 = P.a(lambda e, sv=sv, st=st, mp=mp: e.activation(sv[:, mp, :], sv[:, mp, :], ACT.Exp, bias=st[:, mp:mp + 1],
                                                                        accum_out=st[:, 2 + mp:3 + mp]), m1)
                m3 = P.v(lambda e, st=st: e.reciprocal(st[:, 4:6], st[:, 2:4]), m2)
                m3 = P.v(lambda e, st=st: e.tensor_tensor(st[:, 5:6], st[:, 5:6], st8[:, 2:3], ALU.mult), m3, m_lam)
                m3 = P.v(lambda e, sv=sv, st=st: e.tensor_scalar(sv[:, 1, :], sv[:, 1, :], st[:, 5:6], None, ALU.mult), m3)
                pm = Pm[:, u, 0:n]
                m3 = P.v(lambda e, sv=sv, st=st, pm=pm: e.scalar_tensor_tensor(pm, sv[:, 0, :], st[:, 4:5], sv[:, 1, :], ALU.mult,
                                                                              ALU.subtract), m3, rs[u])
                rp[u] = m3
                yield
                b, ps, free = banks.take()
                for c in range(t + 1):
                    m4 = P.tr(ps[:, c * 128:(c + 1) * 128], pm[:, c * 128:(c + 1) * 128], self.ident, m3, free, inc=c == t)
                rs[u] = m4
                m5 = self.evac("a", PT[:, u, 0:n], ps[:, 0:n], m4, rt[u])
                banks.free(b, m5)
                yield
                m6 = P.mm(ob[:, h * 128:(h + 1) * 128], [(PT[:, u, c * 128:(c + 1) * 128], VA[:, c, h * 128:(h + 1) * 128])
                                                        for c in range(t + 1)], m5, m_o)
                rt[u] = m6
            sq = S[:, 0, :]
            m7 = P.a(lambda e, ob=ob, sq=sq: e.activation(sq, ob, ACT.Square), m6, rp[0], P.last("v"))
            s4 = st8[:, 8 + 4 * t:12 + 4 * t]
            m7 = P.v(lambda e, s4=s4, sq=sq: e.tensor_reduce(s4, sq.rearrange("p (h d) -> p h d", h=4), AX, ALU.add), m7)
            m7 = self.rstd(s4, s4, 128, self.eps, m7)
            m7 = P.v(lambda e, s4=s4: e.tensor_scalar(s4, s4, 1.0 - LAM0, None, ALU.mult), m7)
            as4 = lambda a: a.rearrange("p (h d) -> p h d", h=4)
            m_o = P.v(lambda e, ob=ob, s4=s4, t=t: e.tensor_tensor(as4(OA[:, t, :]), as4(ob), s4.unsqueeze(2).broadcast_to([128, 4, 128]),
                                                                  ALU.mult), m7)
            rp[0] = m_o
            m8 = P.v(lambda e, t=t: e.tensor_tensor(as4(OA[:, t, :]), as4(OA[:, t, :]), sub.unsqueeze(1).broadcast_to([128, 4, 128]),
                                                    ALU.mult), m_o, m_s)
        self.to_columns([OA[:, 0, :], OA[:, 1, :]], MT[:, 0:4, :], 0, None, None, banks, [m8])

    def diff_rwkv_mixer(self):
        P, A, I = self.P, self.A, self.I
        P.fence()
        at0 = A.mark()
        banks = Banks(self.ps, [0, 1, 2, 3, 4, 5, 6])
        MT = A.take(8, 256)
        grow = A.take(D)
        stat = A.take(16)
        QRf, HH = A.take_r(2048)
        mg = P.dma("a", grow, I["norms_2"][0, 3:4, :].broadcast_to([128, D]))
        as8 = lambda a: a.rearrange("p (a b) -> p a b", a=8)
        low_at = A.take_r(2048)
        HT = (as8(HH), as8(low_at[1]))
        at1 = A.mark()
        XN, junk = A.take(2, D), A.take(2, D)
        mh = self.pre_norm(1, banks, XN, HT, junk, stat[:, 0:4])
        P.fence()
        A.back(at1)
        slots, areas, free = self.R.lend_free(2, [r[0] for r in self.part_ready])
        for k in "tvag":
            P.queues[k].append((free, None, None))
        P.queues["a"].append(([P.last(k) for k in "tvg"], None, None))
        A.borrow(*areas)
        attention = self.diff_attention(HT, mh, MT, Banks(self.ps, [4, 5, 6]))
        next(attention)
        A.borrow()
        interleave(P, after_steps(20, attention), self.rwkv(HT, QRf, low_at[0], MT, Banks(self.ps, [0, 1, 2, 3])))
        P.fence()
        self.R.give_back(slots)
        A.back(at1)
        _, MH = A.take_r(8, 256)
        _, ML = A.take_r(8, 256)
        m_mt = self.split(MT, MH, ML)
        junk = A.take(2, D)
        Y = self.ps[:, 4:8, :]
        for half in range(2):
            s, wh, wl, mw = self.parts(8)
            for t in range(2):
                r = slice(t * 128, (t + 1) * 128)
                m = P.mm3(Y[:, 2 * t + half, :], [(MH[:, k, r], ML[:, k, r], wh[:, k, :], wl[:, k, :]) for k in range(8)], mw, m_mt)
            self.free_parts(s, m)
        self.post_norm_add(Y, 0, 3, 1.0, junk, stat[:, 4:8], [m, m], grow, mg)
        P.fence()
        A.back(at0)

    def rwkv(self, HT, QRf, rows_at, MT, banks):
        P, A, I = self.P, self.A, self.I
        HH, HL = HT
        buf = [A.take(D) for _ in range(6)]
        gbuf = [A.take(D) for _ in range(4)]
        BT, KT_, VR, BON = (A.take(4, 256) for _ in range(4))
        BR, KR = (rows_at[:, 1024 * i:1024 * i + 1024].rearrange("p (a b) -> p a b", a=4) for i in range(2))
        XWA, XG = A.take(256), A.take(256)
        Z = A.take(2, 257)
        ups, gup = A.take(512), A.take(512)
        wm = A.take(6, 64)
        d0 = A.take(256)
        UB, SA, S = A.take(4, 64), A.take(4, 64), A.take(4, 64)
        m_c = [P.dma("a", ups[0:64, :], I["rwkv_w_up_2"][0]), P.dma("a", ups[64:128, :], I["rwkv_a_up_2"][0]),
               P.dma("a", gup, I["rwkv_g_up_2"][0]), P.dma("a", wm, I["k_wmask"].rearrange("p (a b) -> p a b", a=6))]
        for k in "tvag":
            P.queues[k].append((m_c, None, None))
        P.g(lambda e: e.memset(Z[:, :, 0:1], 0.0))
        P.g(lambda e: e.memset(d0, 1.0))
        m_z0 = P.g(lambda e: e.memset(d0.rearrange("p (a b) -> p a b", b=64)[:, :, 0:1], 0.0), P.last("g"))
        t4 = lambda a: a.rearrange("p (a b) -> p a b", a=4)
        r, k, v = t4(buf[0]), t4(buf[1]), t4(buf[2])
        dst = [r[:, i, :] for i in range(4)] + [k[:, i, :] for i in range(4)] + [v[:, i, :] for i in range(4)] + [XWA, XG]
        rz = [None, None]
        for n0, n in ((0, 4), (4, 4), (8, 4), (12, 2)):
            s, wh, wl, mw = self.parts(8)
            for q in range(n):
                j = n0 + q
                z = Z[:, j % 2, :]
                b, ps, free = banks.take()
                c = slice(q * 128, (q + 1) * 128)
                m = P.mm3(ps[:, 0:256], [(wh[:, kc, c], wl[:, kc, c], HH[:, kc, :], HL[:, kc, :]) for kc in range(8)], mw, free)
                m1 = P.a(lambda e, z=z, ps=ps: e.activation(z[:, 1:257], ps[:, 0:256], ACT.Copy), m, rz[j % 2], m_z0)
                banks.free(b, m1)
                m2 = P.v(lambda e, z=z, o=dst[j]: e.tensor_tensor(o, z[:, 0:256], z[:, 1:257], ALU.subtract), m1)
                m_zs = P.v(lambda e, z=z, o=dst[j], j=j: e.scalar_tensor_tensor(o, o, self.col("mu", 1, j), z[:, 1:257], ALU.mult, ALU.add), m2)
                rz[j % 2] = m_zs
                yield
            self.free_parts(s, m)
        vec = lambda i, p: self.col("vec", 1, 4 * i + p)
        SG, AA, KK = t4(buf[3]), t4(buf[4]), t4(buf[5])
        P0, P1, PI, TM = (t4(g) for g in gbuf)
        m_th = P.a(lambda e: e.activation(XWA[0:64, :], XWA[0:64, :], ACT.Tanh), m_zs)
        m_xg = P.a(lambda e: e.activation(XG, XG, ACT.Sigmoid), m_zs)
        ms, mk = [], []
        for p in range(4):
            for lo, dd, vi, out in ((0, m_th, 0, SG), (64, m_zs, 1, AA)):
                b, ps, free = banks.take()
                m = P.mm(ps[:, 0:256], [(ups[lo:lo + 64, p * 128:(p + 1) * 128], XWA[lo:lo + 64, :])], dd, free)
                m = P.a(lambda e, ps=ps, out=out, p=p, vi=vi: e.activation(out[:, p, :], ps[:, 0:256], ACT.Sigmoid, bias=vec(vi, p)), m)
                banks.free(b, m)
                ms.append(m)
            mk.append(P.v(lambda e, p=p: e.tensor_tensor_scan(P0[:, p, :], d0, SG[:, p, :], 0.0, ALU.mult, ALU.add), ms[-2], m_z0))
            yield
        m1 = P.v(lambda e: e.tensor_tensor(P1, P0, SG, ALU.subtract), mk[-1])
        C = float(np.exp(-0.5))
        m_pi = P.a(lambda e: e.activation(PI, P0, ACT.Exp, scale=C), mk[-1])
        m_p1 = P.a(lambda e: e.activation(P1, P1, ACT.Exp, scale=-C), m1)
        m_p0 = P.a(lambda e: e.activation(P0, P0, ACT.Exp, scale=-C), m_pi)
        yield
        for p in range(4):
            m = P.v(lambda e, p=p: e.tensor_scalar(KK[:, p, :], k[:, p, :], vec(2, p), None, ALU.mult), m_zs)
        m = P.a(lambda e: e.activation(TM, KK, ACT.Square), m)
        for hf in range(2):
            b, ps, free = banks.take()
            m2 = P.mm(ps, [(self.bones, TM[:, 2 * hf:2 * hf + 2, :])], m, free)
            sl = TM[:, 2 * hf:2 * hf + 2, :].rearrange("p a b -> p (a b)")
            m3 = P.a(lambda e, ps=ps, sl=sl: e.activation(sl, ps, ACT.Sqrt), m2)
            banks.free(b, m3)
        yield
        m3 = P.v(lambda e: e.tensor_scalar(TM, TM, 1e-12, None, ALU.max), m3)
        m3 = P.v(lambda e: e.reciprocal(TM, TM), m3)
        m_kk = P.v(lambda e: e.tensor_tensor(KK, KK, TM, ALU.mult), m3)
        yield
        for p in range(4):
            m = P.v(lambda e, p=p: e.tensor_scalar(TM[:, p, :], AA[:, p, :], -1.0, vec(3, p), ALU.add, ALU.mult), m_kk, ms[-1])
        m_k = P.v(lambda e: e.scalar_tensor_tensor(k, TM, 1.0, k, ALU.add, ALU.mult), m)
        yield
        QR = QRf.rearrange("p (a c w t) -> p a c w t", a=4, c=4, w=2)
        c4 = lambda a, p: a[:, p, :].rearrange("p (c t) -> p c t", c=4)
        fence_h = P.last("t")
        for p in range(4):
            P.v(lambda e, p=p: e.tensor_tensor(QR[:, p, :, 0, :], c4(KK, p), c4(P1, p), ALU.mult), m_p1, fence_h)
            m_qr = P.v(lambda e, p=p: e.tensor_tensor(QR[:, p, :, 1, :], c4(r, p), c4(P0, p), ALU.mult), m_p0)
        yield
        PE_ = A.take(4, 4)
        m_pe = P.v(lambda e: e.tensor_copy(PE_, P0.rearrange("p a (c t) -> p a c t", c=4)[:, :, :, 63]), m_p0)
        m = P.v(lambda e: e.tensor_tensor(BT, KK, AA, ALU.mult), m_kk)
        m_bt = P.v(lambda e: e.tensor_tensor(BT, BT, PI, ALU.mult), m, m_pi)
        m_kt = P.v(lambda e: e.tensor_tensor(KT_, k, PI, ALU.mult), m_k)
        yield
        for p in range(4):
            m = P.v(lambda e, p=p: e.scalar_tensor_tensor(TM[:, p, :], r[:, p, :], vec(4, p), k[:, p, :], ALU.mult, ALU.mult), m_k)
        for hf in range(2):
            b, ps, free = banks.take()
            m2 = P.mm(ps, [(self.bones, TM[:, 2 * hf:2 * hf + 2, :])], m, free)
            m3 = P.v(lambda e, ps=ps, hf=hf: e.tensor_tensor(BON[:, 2 * hf:2 * hf + 2, :].rearrange("p a b -> p (a b)"), ps,
                                                             v[:, 2 * hf:2 * hf + 2, :].rearrange("p a b -> p (a b)"), ALU.mult), m2)
            banks.free(b, m3)
        m_bon = m2
        yield
        H = [slice(0, 64), slice(64, 128)]

        def each(out, lhs, rhs, marks, width=64):
            for p in range(4):
                for h in H:
                    m = P.t(lambda e, p=p, h=h: e.matmul(out[h, p, :], lhs(h, p), rhs(h, p), start=True, stop=True, skip_group_check=True),
                            *(marks if p == 0 and h is H[0] else ()), inc=p == 3 and h is H[1])
            return m

        def product(lhs, rhs, marks, use):
            last = {}
            for c0 in (0, 2):
                need = tuple(m for d in marks for m in (d[c0] if isinstance(d, dict) else [d]))
                b, ps, free = banks.take()
                pv = ps.rearrange("p (c a b) -> p c a b", c=2, a=4)
                for c in range(2):
                    m = each(pv[:, c, :, :], lambda h, p, c=c0 + c: lhs(h, c, p), lambda h, p, c=c0 + c: rhs(h, c, p),
                             need + (free,))
                last[c0] = use(c0, ps, m)
                banks.free(b, last[c0][-1])
            return last

        four = lambda a: a.rearrange("p (c a b) -> p c a b", c=4, a=4)
        half = lambda a, c0: a[:, 256 * c0:256 * c0 + 512]
        m_rows = []
        flat = lambda a: a.rearrange("p a b -> p (a b)")
        for src, out, mk_ in ((BT, flat(BR), m_bt), (KT_, flat(KR), m_kt), (v, flat(VR), m_zs)):
            yield
            m_rows.append(product(lambda h, c, p, src=src: src[h, p, 64 * c:64 * c + 64], lambda h, c, p: self.ident[h, h], [mk_],
                              lambda c0, ps, m, out=out: [self.evac("a", half(out, c0), ps, m)]))
        P.queues["v"].append(([P.last(k) for k in "ag"] + [m_bon], None, None))
        GB = gbuf[0].tensor[:, self.off(gbuf[0]):self.off(gbuf[0]) + 2048].rearrange("p (c a w t) -> p c a w t", c=4, a=4, w=2)
        GK = gbuf[0].tensor[:, self.off(gbuf[2]):self.off(gbuf[2]) + 2048].rearrange("p (c a w t) -> p c a w t", c=4, a=4, w=2)
        m_g = []
        for src, out, mk_ in ((BT, GB, m_bt), (KT_, GK, m_kt)):
            for c in range(4):
                b, ps, free = banks.take()
                m = each(ps.rearrange("p (a b) -> p a b", a=4), lambda h, p, src=src, c=c: src[h, p, 64 * c:64 * c + 64],
                         lambda h, p, c=c: QR[h, p, c, :, :].rearrange("p a b -> p (a b)"), (free, m_qr, mk_))
                m = P.v(lambda e, ps=ps, out=out, c=c: e.tensor_tensor(
                    out[:, c, :, :, :].rearrange("p a w t -> p a (w t)"), ps.rearrange("p (a b) -> p a b", a=4),
                    wm[:, 0:2, :].rearrange("p a b -> p (a b)").unsqueeze(1).broadcast_to([128, 4, 128]), ALU.mult), m)
                banks.free(b, m)
                m_g.append(m)
                yield
        mask = lambda i: wm[:, i, :].unsqueeze(1).broadcast_to([128, 8, 64])
        e8 = lambda a: a.rearrange("p (a b) -> p a b", a=8)
        Ld, LdT, Lo, A2, A2T, ZT = buf

        def tiles(a):
            v4 = four(a)
            return lambda h, c, p: v4[h, c, p, :]

        m_l = product(lambda h, c, p: QR[h, p, c, 0, :], lambda h, c, p: BT[h, p, 64 * c:64 * c + 64], [m_qr, m_bt],
                      lambda c0, ps, m: [P.v(lambda e: e.tensor_tensor(e8(half(Ld, c0)), e8(ps), mask(2), ALU.mult), m),
                                         P.v(lambda e: e.tensor_tensor(e8(half(Lo, c0)), e8(ps), mask(3), ALU.mult), m)])
        yield
        m_t = {0: [], 2: []}
        for c in range(4):
            m = P.v(lambda e, c=c: e.tensor_tensor(four(LdT)[:, c, :, :], GB[:, c, :, 0, :],
                                                   wm[:, 5, :].unsqueeze(1).broadcast_to([128, 4, 64]), ALU.mult), *m_g)
            m_t[c // 2 * 2].append(P.v(lambda e, c=c: e.tensor_tensor(four(ZT)[:, c, :, :], wm[:, 4, :].unsqueeze(1).broadcast_to([128, 4, 64]),
                                                          four(LdT)[:, c, :, :], ALU.subtract), m))

        def copy(out, k="av"):
            return lambda c0, ps, m: [self.evac(k[c0 // 2 % len(k)], half(out, c0), ps, m)]

        def plus(out, base):
            return lambda c0, ps, m: [P.v(lambda e: e.tensor_tensor(half(out, c0), ps, half(base, c0), ALU.add), m)]

        yield
        mA2 = product(tiles(LdT), tiles(Ld), [m_l, m_t], copy(A2))
        yield
        mA2T = product(tiles(Ld), tiles(LdT), [m_l, m_t], copy(A2T))
        yield
        A4, A4T = Ld, LdT
        mZ = product(tiles(A2), tiles(ZT), [mA2, m_t], plus(ZT, ZT))
        yield
        mA4 = product(tiles(A2T), tiles(A2), [mA2, mA2T], copy(A4))
        yield
        mA4T = product(tiles(A2), tiles(A2T), [], copy(A4T))
        yield
        mZ = product(tiles(A4), tiles(ZT), [mZ, mA4], plus(ZT, ZT))
        yield
        A8 = A2T
        mA8 = product(tiles(A4T), tiles(A4), [mA4T], copy(A8))
        yield
        mZ = product(tiles(A8), tiles(ZT), [mZ, mA8], plus(ZT, ZT))
        yield
        XX, F, FT, F2, T1, INV = Ld, LdT, A2, A2T, Lo, buf[1]
        mX = product(tiles(ZT), lambda h, c, p: self.ident[h, h], [mZ], copy(XX))
        yield
        mF = product(tiles(ZT), tiles(Lo), [mZ], copy(F))
        yield
        mFT = product(tiles(Lo), tiles(ZT), [mZ], copy(FT, "v"))
        yield
        mF2 = product(tiles(FT), tiles(F), [mF, mFT], copy(F2))
        yield
        mT = {c0: [P.v(lambda e, c0=c0: e.tensor_tensor(e8(half(T1, c0)), wm[:, 4, :].unsqueeze(1).broadcast_to([128, 8, 64]),
                                                        e8(half(FT, c0)), ALU.subtract), *mFT[2])] for c0 in (0, 2)}
        mT = product(tiles(F2), tiles(T1), [mF2, mT], plus(T1, T1))
        yield
        m_inv = product(tiles(XX), tiles(T1), [mT, mX], copy(INV))
        yield
        INV4, BR4, KR4, VR4 = four(INV), four(flat(BR)), four(flat(KR)), four(flat(VR))
        YT = t4(buf[0])
        ready = [m for d in m_rows + [m_inv] for ms_ in d.values() for m in ms_] + m_g
        P.queues["t"].append((ready, None, None))
        m_s = None
        m_ub = m_sa = None
        for c in range(4):
            def group(out, terms, marks):
                for p in range(4):
                    for h in H:
                        for i, (l, q) in enumerate(terms):
                            m = P.t(lambda e, p=p, h=h, l=l, q=q, i=i: e.matmul(out[h, p, :], l(h, p), q(h, p), start=i == 0,
                                                                                stop=i == len(terms) - 1, skip_group_check=True),
                                    *(marks if p == 0 and h is H[0] and i == 0 else ()),
                                    inc=p == 3 and h is H[1] and i == len(terms) - 1)
                return m

            def bank():
                b, ps, free = banks.take()
                return b, ps[:, 0:256].rearrange("p (a b) -> p a b", a=4), free

            yield
            b, ps, free = bank()
            terms = [(lambda h, p, c=c: GK[h, c, p, 0, :], lambda h, p, c=c: VR4[h, c, p, :])]
            if c:
                terms.append((lambda h, p, c=c: QR[h, p, c, 0, :], lambda h, p: S[h, p, :]))
            m = group(ps, terms, (free, m_s))
            m_ub = P.v(lambda e, ps=ps: e.tensor_copy(UB, ps), m, m_sa)
            banks.free(b, m_ub)
            yield
            b, ps, free = bank()
            m = group(ps, [(lambda h, p, c=c: INV4[h, c, p, :], lambda h, p: UB[h, p, :])], (free, m_ub))
            m_sa = P.v(lambda e, ps=ps: e.tensor_scalar(SA, ps, -1.0, None, ALU.mult), m, P.last("t"))
            banks.free(b, m_sa)
            yield
            b, ps, free = bank()
            terms = [(lambda h, p: SA[h, p, :], lambda h, p, c=c: GB[h, c, p, 1, :]),
                     (lambda h, p, c=c: VR4[h, c, p, :], lambda h, p, c=c: GK[h, c, p, 1, :])]
            if c:
                terms.append((lambda h, p: S[h, p, :], lambda h, p, c=c: QR[h, p, c, 1, :]))
            m_y = group(ps, terms, (free, m_sa))
            m = P.a(lambda e, ps=ps, c=c: e.activation(YT[:, :, 64 * c:64 * c + 64], ps, ACT.Copy), m_y)
            banks.free(b, m)
            if c < 3:
                yield
                b, ps, free = bank()
                m = group(ps, [(lambda h, p, c=c: BR4[h, c, p, :], lambda h, p: SA[h, p, :]),
                               (lambda h, p, c=c: KR4[h, c, p, :], lambda h, p, c=c: VR4[h, c, p, :])], (free,))
                if c:
                    m = P.v(lambda e, ps=ps: e.tensor_tensor(S, S, ps, ALU.add), m, m_y)
                else:
                    m = P.v(lambda e, ps=ps: e.tensor_copy(S, ps), m)
                banks.free(b, m)
                m_s = P.v(lambda e, c=c: e.tensor_tensor(S, S, PE_[:, :, c].unsqueeze(2).broadcast_to([128, 4, 64]), ALU.mult), m)
        P.fence()
        yield
        YC, SQ = t4(buf[2]), t4(buf[3])
        for hf in range(2):
            yt, yc, sq = (a[:, 2 * hf:2 * hf + 2, :].rearrange("p a b -> p (a b)") for a in (YT, YC, SQ))
            b, ps, free = banks.take()
            m = P.mm(ps, [(self.bones, yt)], free)
            m1 = P.v(lambda e, ps=ps, yt=yt, yc=yc: e.scalar_tensor_tensor(yc, ps, -1.0 / 64, yt, ALU.mult, ALU.add), m)
            banks.free(b, m1)
            m2 = P.a(lambda e, sq=sq, yc=yc: e.activation(sq, yc, ACT.Square), m1)
            b, ps, free = banks.take()
            m3 = P.mm(ps, [(self.bones, sq)], m2, free)
            m4 = P.a(lambda e, ps=ps, sq=sq: e.activation(sq, ps, ACT.Sqrt, scale=1.0 / 64, bias=self.eps_ln), m3)
            banks.free(b, m4)
            m5 = P.v(lambda e, sq=sq: e.reciprocal(sq, sq), m4)
            m6 = P.v(lambda e, sq=sq, yc=yc: e.tensor_tensor(yc, yc, sq, ALU.mult), m5)
        for p in range(4):
            m = self.affine("v", YC[:, p, :], YC[:, p, :], vec(5, p), vec(6, p), m6)
            m = P.v(lambda e, p=p: e.tensor_tensor(YC[:, p, :], YC[:, p, :], BON[:, p, :], ALU.add), m)
            b, ps, free = banks.take()
            m2 = P.mm(ps[:, 0:256], [(gup[:, p * 128:(p + 1) * 128], XG)], free)
            m = P.v(lambda e, p=p, ps=ps: e.tensor_tensor(MT[:, 4 + p, :], YC[:, p, :], ps[:, 0:256], ALU.mult), m, m2)
            banks.free(b, m)
        P.fence()

    def off(self, a):
        return a.offset

    def retention_mixer(self):
        P, A, I = self.P, self.A, self.I
        P.fence()
        at0 = A.mark()
        banks = Banks(self.ps, [0, 1, 2, 3])
        grow = A.take(D)
        stat = A.take(32)
        mg = P.dma("a", grow, I["norms_2"][1, 3:4, :].broadcast_to([128, D]))
        DC = A.take(4, 2, 256)
        m_dc = P.dma("a", DC, I["k_decay"].rearrange("p (a b c) -> p a b c", a=4, b=2))
        QK, QH = A.take_r(16, 256)
        _, HH = A.take_r(8, 256)
        _, HL = A.take_r(8, 256)
        at_v = A.mark()
        V, G = A.take(2, 2048), A.take(2, 2048)
        QL = self.big_r[:, at_v:at_v + 4096].rearrange("p (a b) -> p a b", a=16)
        ST = A.take(2, 2, 256)
        junk = A.take(2, D)
        mh = self.pre_norm(4, banks, G[:, :, 0:1024], (HH, HL), junk, stat[:, 0:4])
        P.fence()
        banks = Banks(self.ps, list(range(8)))
        m_p = []
        for blk in range(4):
            s, wh, wl, mw = self.parts(8)
            for q in range(4):
                j = 4 * blk + q
                b, ps, free = banks.take()
                c = slice(q * 128, (q + 1) * 128)
                m = P.mm3(ps[:, 0:256], [(wh[:, k, c], wl[:, k, c], HH[:, k, :], HL[:, k, :]) for k in range(8)], mw, free, *mh)
                if j < 8:
                    m1 = self.evac("a", QK[:, j, :], ps[:, 0:256], m)
                else:
                    m1 = P.a(lambda e, ps=ps, j=j: e.activation(QK[:, j, :], ps[:, 0:256], ACT.Copy, scale=1.0 / 16), m)
                banks.free(b, m1)
                m_p.append(m1)
            self.free_parts(s, m)
        for blk in range(8):
            s, wh, wl, mw = self.parts(8)
            for t in range(2):
                b, ps, free = banks.take()
                r = slice(t * 128, (t + 1) * 128)
                m = P.mm3(ps, [(HH[:, k, r], HL[:, k, r], wh[:, k, :], wl[:, k, :]) for k in range(8)], mw, free)
                if blk < 4:
                    m1 = self.evac("v", V[:, t, blk * 512:blk * 512 + 512], ps, m)
                else:
                    m1 = P.a(lambda e, ps=ps, t=t, blk=blk: e.activation(G[:, t, (blk - 4) * 512:(blk - 3) * 512], ps, ACT.Silu), m)
                banks.free(b, m1)
                m_p.append(m1)
            self.free_parts(s, m)
        P.fence()
        banks = Banks(self.ps, [0, 1, 2, 3])
        yb = Banks(self.ps, [4, 5, 6, 7])
        r_st = [None, None]
        for h in range(4):
            u = h % 2
            for sT in range(2):
                b, ps, free = banks.take()
                m = P.mm(ps[:, 0:256], [(QK[:, 8 + 2 * h + k, sT * 128:(sT + 1) * 128], QK[:, 2 * h + k, :]) for k in range(2)], free)
                m_st = P.v(lambda e, ps=ps, h=h, sT=sT, u=u: e.tensor_tensor(ST[:, u, sT, :], ps[:, 0:256], DC[:, h, sT, :], ALU.mult),
                           m, m_dc, r_st[u])
                banks.free(b, m_st)
            for t in range(2):
                b, ps, free = yb.take()
                m = P.mm(ps, [(ST[:, u, sT, t * 128:(t + 1) * 128], V[:, sT, h * 512:(h + 1) * 512]) for sT in range(t + 1)], m_st, free)
                if t == 1:
                    r_st[u] = m
                st = stat[:, 8 + 2 * h + t:9 + 2 * h + t]
                m = P.a(lambda e, ps=ps, st=st, t=t: e.activation(junk[:, t, 0:512], ps, ACT.Square, accum_out=st), m, P.last("a"))
                m = self.rstd(st, st, 512, self.eps, m)
                g = G[:, t, h * 512:(h + 1) * 512]
                m = P.v(lambda e, ps=ps, st=st, g=g: e.scalar_tensor_tensor(g, ps, st, g, ALU.mult, ALU.mult), m)
                yb.free(b, m)
        P.fence()
        self.to_column_parts([G[:, 0, :], G[:, 1, :]], QH, QL, None, banks, [])
        P.fence()
        Y = self.ps[:, 4:8, :]
        for k0 in range(0, 16, 4):
            s, wh, wl, mw = self.parts(4)
            order = [(k, t) for k in range(4) for t in range(2)] if k0 < 12 else [(k, t) for t in range(2) for k in range(4)]
            m_y = [None, None]
            for k, t in order:
                for hf in range(2):
                    r, c = slice(t * 128, (t + 1) * 128), slice(hf * 512, (hf + 1) * 512)
                    m = m_y[t] = P.mm3(Y[:, 2 * t + hf, :], [(QH[:, k0 + k, r], QL[:, k0 + k, r], wh[:, k, c], wl[:, k, c])],
                                       mw, start=k0 + k == 0, stop=k0 + k == 15)
            self.free_parts(s, m)
        self.post_norm_add(Y, 1, 3, 1.0, junk, stat[:, 4:8], m_y, grow, mg)
        P.fence()
        A.back(at0)

    def stages(self):
        return [self.even_mixer, lambda: self.moe(0), self.pool_mixer,
                lambda: self.moe(1), self.final_norm, self.second_block_memory, lambda: self.ffn(0, 0), self.diff_rwkv_mixer,
                lambda: self.ffn(0, 1), lambda: self.ffn(1, 0), self.retention_mixer, lambda: self.ffn(1, 1)]

    def program(self):
        P = self.P
        self.load_constants()
        for stage in self.stages():
            stage()
        self.write_out()

    def write_out(self):
        P = self.P
        m = [P.last(k) for k in "tvag"]
        marks = [P.dma("s", self.out[0, t * 128:(t + 1) * 128, :], self.X[:, t, :], *m) for t in range(2)]
        P.queues["s"].append((marks, None, None))

    def finish(self, ctx):
        P = self.P
        block = ctx.enter_context(self.nc.Block())

        @block.sync
        def _(e):
            P.emit("s", e)

        @block.tensor
        def _(e):
            P.emit("t", e)

        @block.vector
        def _(e):
            P.emit("v", e)

        @block.scalar
        def _(e):
            P.emit("a", e)

        @block.gpsimd
        def _(e):
            P.emit("g", e)


def build_program(nc, I, out):
    with ExitStack() as ctx:
        k = Kernel(nc, ctx, I, out)
        k.program()
        k.finish(ctx)


_BIG = ["x", "ctx", "w_mod", "b_mod", "w_in_even", "w_out_even", "g_qnorm", "g_knorm", "g_hnorm", "w_in_odd", "w_pool_grp",
        "s_pool", "w_router", "w_exp_gate", "w_exp_up", "w_exp_down", "g_final", "norms_2", "ffn_wgu_2", "ffn_wd_2",
        "even_w_in_2", "even_w_out_2", "diff_lam_2", "diff_subln_2", "rwkv_w_up_2", "rwkv_a_up_2", "rwkv_g_up_2",
        "odd_w_in_2", "odd_w_out_2"]


def _pack_columns(inp):
    a = {k: np.asarray(inp[k]) for k in ("c", "c_ctx", "g_norm1", "g_norm2", "b_mod", "norms_2", "w_conv", "b_gate",
                                         "rwkv_mu_2", "rwkv_vec_2")}
    cc = np.stack([a["c"].reshape(8, 128).T, a["c_ctx"].reshape(8, 128).T], 2).reshape(128, 16)
    g1 = a["g_norm1"].reshape(16, 128).T
    g2 = a["g_norm2"].reshape(16, 128).T
    bm = a["b_mod"].reshape(96, 128).T
    nrm = a["norms_2"].reshape(2, 6, 8, 128)[:, [0, 2, 4]].reshape(48, 128).T
    conv = a["w_conv"].reshape(24, 128).T
    bgate = np.pad(a["b_gate"].reshape(16, 1), ((0, 112), (0, 0)))
    mu = a["rwkv_mu_2"].reshape(14, 128).T
    vec = a["rwkv_vec_2"].reshape(28, 128).T
    return np.ascontiguousarray(np.concatenate([cc, g1, g2, bm, nrm, conv, bgate, mu, vec], 1))


def kernel(**inputs):
    import concourse.bacc as bacc
    from concourse.bass_utils import run_bass_kernel_spmd

    nc = bacc.Bacc("TRN2", target_bir_lowering=False, num_devices=1)
    arrays = {n: np.ascontiguousarray(inputs[n]) for n in _BIG}
    arrays["vc"] = _pack_columns(inputs)
    for n, a in shape_constants().items():
        arrays["k_" + n] = a
    aps = {}
    for n, a in arrays.items():
        aps[n] = nc.dram_tensor("in_" + n, a.shape, mybir.dt.from_np(a.dtype), kind="ExternalInput").ap()
    out = nc.dram_tensor("out_x", (1, T, D), F32, kind="ExternalOutput").ap()
    build_program(nc, aps, out)
    r = run_bass_kernel_spmd(nc, [{"in_" + n: a for n, a in arrays.items()}], core_ids=[0])
    return r.results[0]["out_x"]
```
